# Optimizing a Trainium2 kernel written in Bass

```python
import math
import jax, jax.numpy as jnp
from jax import lax
import numpy as np

D_MODEL = 2048
BATCH = 1
SEQ = 512
DEPTH = 1

GRID_W = 64
CTX_LEN = 256
N_HEADS = 16
QK_NOPE = 128
QK_ROPE = 64
V_DIM = 128
Q_LORA = 512
KV_LORA = 512
ROPE_THETA = 10000.0
N_FOURIER_GROUPS = 4
FOURIER_GROUP_DIM = 256
FOURIER_DIM = N_FOURIER_GROUPS * FOURIER_GROUP_DIM
KV_END = KV_LORA + QK_ROPE
IN_SPLITS = (KV_LORA, KV_END, KV_END + Q_LORA, KV_END + Q_LORA + FOURIER_DIM,
             KV_END + Q_LORA + FOURIER_DIM + D_MODEL)
IN_DIM = KV_END + Q_LORA + FOURIER_DIM + 2 * D_MODEL
PEER_HEADS = 8
N_KEYS = 128
N_EXPERTS = N_KEYS * N_KEYS
PEER_KEY_DIM = 256
PEER_HALF = PEER_KEY_DIM // 2
PEER_TOPK = 16
Q_BLOCK = 128
TOKEN_BLOCK = 128
DEEPNORM_ALPHA = (2.0 * DEPTH) ** 0.25
DEEPNORM_BETA = (8.0 * DEPTH) ** -0.25
EPS = 1e-6

kernel_name = 'hybrid_mla_fnet_peer_dit_block'

def _layer_norm(x, g=None, b=None):
    xf = x.astype(jnp.float32)
    mu = jnp.mean(xf, axis=-1, keepdims=True)
    var = jnp.mean(jnp.square(xf - mu), axis=-1, keepdims=True)
    y = (xf - mu) * lax.rsqrt(var + EPS)
    if g is not None:
        y = y * g + b
    return y.astype(x.dtype)

def _rms_norm(x, g):
    xf = x.astype(jnp.float32)
    y = xf * lax.rsqrt(jnp.mean(jnp.square(xf), axis=-1, keepdims=True) + EPS)
    return (y * g).astype(x.dtype)

def _modulate(x, shift, scale):
    return _layer_norm(x) * (1 + scale) + shift

def _axial_rope(row, col):
    half = QK_ROPE // 2
    inv = ROPE_THETA ** (-jnp.arange(0, half, 2, dtype=jnp.float32) / half)
    ang = jnp.concatenate([row[:, None] * inv, col[:, None] * inv], axis=-1)
    return jnp.cos(ang), jnp.sin(ang)

def _apply_rope(x, cos, sin):
    xp = x.reshape(x.shape[:-1] + (QK_ROPE // 2, 2))
    x1, x2 = xp[..., 0], xp[..., 1]
    cos = cos.astype(x.dtype)
    sin = sin.astype(x.dtype)
    out = jnp.stack([x1 * cos - x2 * sin, x1 * sin + x2 * cos], axis=-1)
    return out.reshape(x.shape)

def _mla_kv(ckv, kr, kv_norm_g, w_ukv, rope):
    B, T = ckv.shape[:2]
    kv = (_rms_norm(ckv, kv_norm_g) @ w_ukv).reshape(B, T, N_HEADS, QK_NOPE + V_DIM)
    k_nope, v = kv[..., :QK_NOPE], kv[..., QK_NOPE:]
    if rope is not None:
        kr = _apply_rope(kr, rope[0], rope[1])
    k_rope = jnp.broadcast_to(kr[:, :, None, :], (B, T, N_HEADS, QK_ROPE))
    return jnp.concatenate([k_nope, k_rope], axis=-1), v

def _mla_q(cq, q_norm_g, w_uq, rope):
    B, S = cq.shape[:2]
    q = (_rms_norm(cq, q_norm_g) @ w_uq).reshape(B, S, N_HEADS, QK_NOPE + QK_ROPE)
    q_nope, q_rope = q[..., :QK_NOPE], q[..., QK_NOPE:]
    if rope is not None:
        q_rope = _apply_rope(q_rope, rope[0][:, None, :], rope[1][:, None, :])
    return jnp.concatenate([q_nope, q_rope], axis=-1)

def _attend_blocks(q, k, v):
    B, S, H, Dqk = q.shape
    Dv = v.shape[-1]
    nb = S // Q_BLOCK
    scale = Dqk ** -0.5
    qb = q.reshape(B, nb, Q_BLOCK, H, Dqk).transpose(1, 0, 2, 3, 4)

    def one(q_blk):
        s = jnp.einsum('bqhd,bkhd->bhqk', q_blk, k, preferred_element_type=jnp.float32) * scale
        p = jax.nn.softmax(s, axis=-1)
        return jnp.einsum('bhqk,bkhd->bqhd', p.astype(v.dtype), v)

    o = lax.map(one, qb)
    return o.transpose(1, 0, 2, 3, 4).reshape(B, S, H, Dv)

def _fourier_mix(f):
    B, S, _ = f.shape
    g = f.reshape(B, S, N_FOURIER_GROUPS, FOURIER_GROUP_DIM).astype(jnp.float32)
    y = jnp.real(jnp.fft.fft2(g, axes=(1, 3), norm='ortho'))
    return y.reshape(B, S, FOURIER_DIM).astype(f.dtype)

def _mixer_out(q, k, v, f, ga, gb, w_o_mla, w_fourier, w_out):
    B, S = q.shape[:2]
    y_a = _attend_blocks(q, k, v).reshape(B, S, N_HEADS * V_DIM) @ w_o_mla
    y_b = _fourier_mix(f) @ w_fourier
    merged = jax.nn.sigmoid(ga) * y_a + jax.nn.sigmoid(gb) * y_b
    return merged @ w_out

def _peer(h, wq, keys, u, v):
    B, S, D = h.shape
    T = B * S
    hf = h.reshape(T, D)
    q = (hf @ wq).reshape(T, PEER_HEADS, 2, PEER_HALF)
    s = jnp.einsum('thpd,hpkd->thpk', q, keys, preferred_element_type=jnp.float32)
    s1, i1 = lax.top_k(s[:, :, 0], PEER_TOPK)
    s2, i2 = lax.top_k(s[:, :, 1], PEER_TOPK)
    cand_s = (s1[..., :, None] + s2[..., None, :]).reshape(T, PEER_HEADS, PEER_TOPK * PEER_TOPK)
    cand_i = (i1[..., :, None] * N_KEYS + i2[..., None, :]).reshape(T, PEER_HEADS, PEER_TOPK * PEER_TOPK)
    top_s, pos = lax.top_k(cand_s, PEER_TOPK)
    idx = jnp.take_along_axis(cand_i, pos, axis=-1)
    w = jax.nn.softmax(top_s, axis=-1)
    nb = T // TOKEN_BLOCK

    def one(args):
        hb, ib, wb = args
        a = jnp.einsum('td,thkd->thk', hb, u[ib], preferred_element_type=jnp.float32)
        coef = (wb * jax.nn.gelu(a, approximate=False)).astype(v.dtype)
        return jnp.einsum('thk,thkd->td', coef, v[ib])

    out = lax.map(one, (hf.reshape(nb, TOKEN_BLOCK, D),
                        idx.reshape(nb, TOKEN_BLOCK, PEER_HEADS, PEER_TOPK),
                        w.reshape(nb, TOKEN_BLOCK, PEER_HEADS, PEER_TOPK)))
    return out.reshape(B, S, D)

def setup_inputs(seed: int = 0) -> dict:
    key = jax.random.key(seed)
    ks = jax.random.split(key, 24)
    L, D = DEPTH, D_MODEL

    def nrm(k, shape, s):
        return jax.random.normal(k, shape, jnp.float32) * s

    return {
        'x': nrm(ks[0], (BATCH, SEQ, D), 1.0),
        'c': nrm(ks[1], (BATCH, D), 1.0),
        'ctx': nrm(ks[2], (BATCH, CTX_LEN, D), 1.0),
        'c_ctx': nrm(ks[3], (D,), 1.0),
        'w_mod': nrm(ks[4], (L, D, 6 * D), 0.5 * D ** -0.5),
        'b_mod': nrm(ks[5], (L, 6 * D), 0.01),
        'w_in': nrm(ks[6], (L, D, IN_DIM), D ** -0.5),
        'b_in': nrm(ks[7], (L, IN_DIM), 0.01),
        'q_norm_g': 1.0 + nrm(ks[8], (L, Q_LORA), 0.01),
        'w_uq': nrm(ks[9], (L, Q_LORA, N_HEADS * (QK_NOPE + QK_ROPE)), Q_LORA ** -0.5),
        'kv_norm_g': 1.0 + nrm(ks[10], (L, KV_LORA), 0.01),
        'w_ukv': nrm(ks[11], (L, KV_LORA, N_HEADS * (QK_NOPE + V_DIM)), KV_LORA ** -0.5),
        'w_o_mla': nrm(ks[12], (L, N_HEADS * V_DIM, D), (N_HEADS * V_DIM) ** -0.5),
        'w_fourier': nrm(ks[13], (L, FOURIER_DIM, D), FOURIER_DIM ** -0.5),
        'w_out': nrm(ks[14], (L, D, D), DEEPNORM_BETA * D ** -0.5),
        'ln1_g': 1.0 + nrm(ks[15], (L, D), 0.01),
        'ln1_b': nrm(ks[16], (L, D), 0.01),
        'peer_wq': nrm(ks[17], (L, D, PEER_HEADS * PEER_KEY_DIM), D ** -0.5),
        'peer_keys': nrm(ks[18], (L, PEER_HEADS, 2, N_KEYS, PEER_HALF), PEER_HALF ** -0.5),
        'peer_u': nrm(ks[19], (L, N_EXPERTS, D), D ** -0.5),
        'peer_v': nrm(ks[20], (L, N_EXPERTS, D), DEEPNORM_BETA * PEER_HEADS ** -0.5),
        'ln2_g': 1.0 + nrm(ks[21], (L, D), 0.01),
        'ln2_b': nrm(ks[22], (L, D), 0.01),
    }

def reference(x, c, ctx, c_ctx, w_mod, b_mod, w_in, b_in, q_norm_g, w_uq, kv_norm_g, w_ukv,
              w_o_mla, w_fourier, w_out, ln1_g, ln1_b, peer_wq, peer_keys, peer_u, peer_v,
              ln2_g, ln2_b):
    D = D_MODEL
    ROWS = x.shape[1] // GRID_W
    row = jnp.repeat(jnp.arange(ROWS, dtype=jnp.float32), GRID_W)
    col = jnp.tile(jnp.arange(GRID_W, dtype=jnp.float32), ROWS)
    rope = _axial_rope(row, col)

    for l in range(DEPTH):
        last = l == DEPTH - 1
        mod_x = (jax.nn.silu(c) @ w_mod[l] + b_mod[l])[:, None, :]
        sh1, sc1, g1, sh2, sc2, g2 = jnp.split(mod_x, 6, axis=-1)
        n_cm = 2 if last else 6
        mod_c = jax.nn.silu(c_ctx) @ w_mod[l][:, :n_cm * D] + b_mod[l][:n_cm * D]
        mc = jnp.split(mod_c, n_cm)

        hx = _modulate(x, sh1, sc1)
        hc = _modulate(ctx, mc[0], mc[1])
        px = hx @ w_in[l] + b_in[l]
        ckv_x, kr_x, cq_x, f_x, ga_x, gb_x = jnp.split(px, IN_SPLITS, axis=-1)
        n_cc = KV_END if last else IN_DIM
        pc = hc @ w_in[l][:, :n_cc] + b_in[l][:n_cc]
        parts_c = jnp.split(pc, IN_SPLITS[:1] if last else IN_SPLITS, axis=-1)

        k_c, v_c = _mla_kv(parts_c[0], parts_c[1], kv_norm_g[l], w_ukv[l], None)
        k_x, v_x = _mla_kv(ckv_x, kr_x, kv_norm_g[l], w_ukv[l], rope)
        q_x = _mla_q(cq_x, q_norm_g[l], w_uq[l], rope)
        y_x = _mixer_out(q_x, jnp.concatenate([k_c, k_x], axis=1), jnp.concatenate([v_c, v_x], axis=1),
                         f_x, ga_x, gb_x, w_o_mla[l], w_fourier[l], w_out[l])
        if not last:
            q_c = _mla_q(parts_c[2], q_norm_g[l], w_uq[l], None)
            y_c = _mixer_out(q_c, k_c, v_c, parts_c[3], parts_c[4], parts_c[5],
                             w_o_mla[l], w_fourier[l], w_out[l])
            ctx = _layer_norm(DEEPNORM_ALPHA * ctx + mc[2] * y_c, ln1_g[l], ln1_b[l])
        x = _layer_norm(DEEPNORM_ALPHA * x + g1 * y_x, ln1_g[l], ln1_b[l])

        y_x = _peer(_modulate(x, sh2, sc2), peer_wq[l], peer_keys[l], peer_u[l], peer_v[l])
        x = _layer_norm(DEEPNORM_ALPHA * x + g2 * y_x, ln2_g[l], ln2_b[l])
        if not last:
            y_c = _peer(_modulate(ctx, mc[3], mc[4]), peer_wq[l], peer_keys[l], peer_u[l], peer_v[l])
            ctx = _layer_norm(DEEPNORM_ALPHA * ctx + mc[5] * y_c, ln2_g[l], ln2_b[l])
    return x


_drawn_inputs = setup_inputs


def setup_inputs(seed=0):
    import zlib

    import numpy as np

    out = dict(_drawn_inputs(seed))
    spreads = {}
    factors = {'ctx': 8.0,
     'c_ctx': 6.689,
     'b_mod': 8.0,
     'b_in': 8.0,
     'q_norm_g': 8.0,
     'w_uq': 8.0,
     'kv_norm_g': 8.0,
     'ln1_g': 29.01,
     'ln1_b': 30.325,
     'ln2_g': 30.124,
     'ln2_b': 31.216,
     'peer_wq': 8.0,
     'peer_keys': 8.0,
     'peer_u': 8.0,
     'peer_v': 8.0}
    for name, (base, spread) in spreads.items():
        noise = np.random.default_rng([zlib.crc32(name.encode()), seed]).standard_normal(out[name].shape)
        drawn = base * np.exp(spread * noise) if base else spread * noise
        out[name] = __import__('jax').numpy.asarray(drawn.astype(out[name].dtype))
    for name, factor in factors.items():
        out[name] = (out[name] * factor).astype(out[name].dtype)
    return out
```

```python
import concourse.bass as bass
from concourse import mybir
import numpy as np
from contextlib import ExitStack

fp32 = mybir.dt.float32
f32r = mybir.dt.float32r
u32 = mybir.dt.uint32
ALU = mybir.AluOpType
ACT = mybir.ActivationFunctionType
AX = mybir.AxisListType

P = 128
D, T, TC = 2048, 512, 256
DC, TB, CB = D // P, T // P, TC // P
NKEY = T + TC
KB = NKEY // P
HEADS, NOPE, ROPE, VD = 16, 128, 64, 128
LORA = 512
LC = LORA // P
QK = NOPE + ROPE
FD, FG, GD = 1024, 4, 256
PH, NK, TOPK = 8, 128, 16
EPS = 1e-6
ALPHA = 2.0 ** 0.25
GRID_W = 64
C_KR = LORA
C_CQ = LORA + ROPE
C_F = C_CQ + LORA
C_GA = C_F + FD
M_SH1, M_SC1, M_G1, M_SH2, M_SC2, M_G2 = (DC * k for k in range(6))
V_C, V_CC, V_QG, V_KVG, V_BKV, V_BKR, V_BR = 0, 16, 32, 36, 40, 44, 45
V_ROWS = V_BR + 44
LN_ORDER = (0, 1, 4, 2, 5, 3, 6, 7)


def constants():
    ident = np.eye(P, dtype=np.float32)
    swap = np.zeros((P, P), np.float32)
    for a in range(0, P, 2):
        swap[a + 1, a] = -1.0
        swap[a, a + 1] = 1.0
    half = ROPE // 2
    inv = 10000.0 ** (-np.arange(0, half, 2, dtype=np.float32) / np.float32(half))
    pos = np.arange(T)
    row = (pos // GRID_W).astype(np.float32)
    col = (pos % GRID_W).astype(np.float32)
    ang = np.concatenate([row[:, None] * inv, col[:, None] * inv], -1).astype(np.float32)
    ang = np.repeat(ang.T, 2, axis=0)
    rot = np.stack([np.tile(np.cos(ang), (2, 1)), np.tile(np.sin(ang), (2, 1))], 1).astype(np.float32)
    k = np.arange(T)
    w = 2 * np.pi * ((k[:, None] * k[None]) % T) / T
    dft_t = np.stack([np.cos(w), np.sin(w)]) / np.sqrt(T)
    k = np.arange(GD)
    w = 2 * np.pi * ((k[:, None] * k[None]) % GD) / GD
    dft_c = np.stack([np.cos(w), -np.sin(w)]) / np.sqrt(GD)
    iota = np.tile(np.arange(P, dtype=np.float32), (P, 1))
    return {"k_ident": ident, "k_swap": swap, "k_rot": rot, "k_dft_t": dft_t.astype(np.float32),
            "k_dft_c": dft_c.astype(np.float32), "k_iota": iota}


class Tally:

    def __init__(self, eng, sem):
        self.eng, self.sem, self.at, self.n = eng, sem, 0, 0

    def inc(self, ins):
        ins.then_inc(self.sem, 1)
        self.at, self.n = self.at + 1, self.n + 1

    def link(self, ins):
        self.inc(ins)
        self.eng.wait_ge(self.sem, self.at)


def mm3(pe, out, lh, ll, rh, rl, first, last):
    pe.matmul(out, lh, rh, start=first, stop=False)
    pe.matmul(out, lh, rl, start=False, stop=False)
    return pe.matmul(out, ll, rh, start=False, stop=last)


def layer_kernel(nc, a, out, dbg=None):
    ctx = ExitStack()
    BASE = 16640

    def sb(name, kb, shape, dt=fp32):
        return nc.alloc_sbuf_tensor_at(name, shape, dt, offset=BASE + int(kb * 1024))

    def sem(name):
        return ctx.enter_context(nc.semaphore(name))

    with ctx:
        px_d = nc.dram_tensor("px_scratch", [FD // P + 2 * DC, P, T], fp32, kind="Internal").ap()
        x1_d = nc.dram_tensor("x1_scratch", [T, D], fp32, kind="Internal").ap()
        route_d = nc.dram_tensor("route_scratch", [NK, NK, T], fp32, kind="Internal").ap()

        ident = sb("ident", 0, [P, P])
        vecT = sb("vecT", 0.5, [P, V_ROWS])
        bmodT = sb("bmodT", 1, [P, 96])
        modT = sb("modT", 1.5, [P, 96, 2])
        ones = sb("ones", 2.25, [P, P])
        swap = sb("swap", 2.75, [P, P], f32r)
        silu = sb("silu", 3.25, [P, DC, 2])
        stats = sb("stats", 3.375, [P, 8, 4, 6])
        mv = sb("mv", 4.125, [P, 8, 2])
        vare = sb("vare", 4.1875, [P, 8])
        rstd = sb("rstd", 4.21875, [P, 8])
        mhalf = sb("mhalf", 4.25, [P, 8])
        rmx = sb("rmx", 4.28125, [P, 8])
        nmx = sb("nmx", 4.3125, [P, 8])
        rsum = sb("rsum", 4.34375, [P, 8])
        rinv = sb("rinv", 4.375, [P, 8])
        silu_t = sb("silu_t", 4.5, [P, 2 * DC])
        xtok = sb("xtok", 8, [P, TB, D])
        ctok = sb("ctok", 40, [P, CB, D])
        wm = [sb(f"wm{s}", 56 + 16 * s, [P, DC, 256]) for s in range(2)]
        hxh, hxl = sb("hxh", 96, [P, DC, T], f32r), sb("hxl", 128, [P, DC, T], f32r)
        hch, hcl = sb("hch", 160, [P, DC, TC], f32r), sb("hcl", 176, [P, DC, TC], f32r)
        affx = [sb(f"affx{s}", 192 + 2 * s, [P, T]) for s in range(2)]
        vrows = sb("vrows", 196, [P, P])
        mrows = sb("mrows", 196.5, [P, P])
        swap_f = sb("swap_f", 197, [P, P])
        modrow = sb("modrow", 96, [2, 32 * P])
        mbuf = [sb(f"mbuf{s}", (64, 72, 88, 96, 88)[s], [P, DC, P]) for s in range(5)]
        mred = [sb(f"mred{s}", 206 + s / 2, [P, P]) for s in range(2)]
        wraw = [sb(f"wraw{s}", 8 + 8 * s, [P, DC, P]) for s in range(2)]
        wh = [sb(f"wh{s}", 24 + 8 * s, [P, DC, P], f32r) for s in range(2)]
        wl = [sb(f"wl{s}", 40 + 8 * s, [P, DC, P], f32r) for s in range(2)]
        ckv = sb("ckv", 56, [P, LC, NKEY])
        kr = sb("kr", 68, [P, NKEY])
        cq = sb("cq", 71, [P, LC, T])
        stg = [sb(f"stg{s}", 85 + 2 * s, [P, T]) for s in range(2)]
        sq = [sb(f"sq{s}", 79 + 3 * s, [P, NKEY]) for s in range(2)]
        rot = sb("rot", 89, [P, 2, T])
        diag = sb("diag", 93, [P, NKEY])
        krh, krl = sb("krh", 192, [P, NKEY], f32r), sb("krl", 195, [P, NKEY], f32r)
        tmp = sb("tmp", 198, [P, NKEY])
        ckvh, ckvl = sb("ckvh", 160, [P, LC, NKEY], f32r), sb("ckvl", 172, [P, LC, NKEY], f32r)
        cqh = sb("cqh", 184, [P, LC, T], f32r)
        cql = sb("cql", 56, [P, LC, T], f32r)
        oT = sb("oT", 96, [P, HEADS, T])
        praw_q = sb("praw_q", 8, [P, LC, 2 * QK])
        praw_kv = sb("praw_kv", 14, [P, LC, 512])
        pqh, pql = sb("pqh", 22, [P, LC, 2 * QK], f32r), sb("pql", 28, [P, LC, 2 * QK], f32r)
        pkh, pkl = sb("pkh", 34, [P, LC, 512], f32r), sb("pkl", 42, [P, LC, 512], f32r)
        qh, ql = sb("qh", 50, [P, 2, T], f32r), sb("ql", 64, [P, 2, T], f32r)
        qrh, qrl = sb("qrh", 54, [P, T], f32r), sb("qrl", 68, [P, T], f32r)
        rt = [sb(f"rt{s}", 70 + 2 * s, [P, T]) for s in range(2)]
        kTh, kTl = sb("kTh", 74, [P, 2, NKEY], f32r), sb("kTl", 80, [P, 2, NKEY], f32r)
        vh, vl = sb("vh", 128, [P, KB, 2, P], f32r), sb("vl", 199, [P, KB, 2, P], f32r)
        prob = [sb("prob0", 86, [P, NKEY]), sb("prob1", 93, [P, NKEY])]
        pTh, pTl = sb("pTh", 134, [P, KB, T], f32r), sb("pTl", 146, [P, KB, T], f32r)
        dtraw = sb("dtraw", 8, [P, 2, TB, T])
        dth, dtl = sb("dth", 24, [P, 2, TB, T], f32r), sb("dtl", 40, [P, 2, TB, T], f32r)
        dcraw = sb("dcraw", 56, [P, 2, 2, GD])
        dch, dcl = sb("dch", 60, [P, 2, 2, GD], f32r), sb("dcl", 64, [P, 2, 2, GD], f32r)
        fT = sb("fT", 68, [P, 2, T])
        fh, fl = sb("fh", 72, [P, TB, GD], f32r), sb("fl", 76, [P, TB, GD], f32r)
        gh, gl = sb("gh", 80, [P, 2, 2, T], f32r), sb("gl", 88, [P, 2, 2, T], f32r)
        yh, yl = sb("yh", 160, [P, FD // P, T], f32r), sb("yl", 176, [P, FD // P, T], f32r)
        oh = sb("oh", 128, [P, HEADS, T], f32r)
        ol = sb("ol", 56, [P, HEADS, T], f32r)
        gate = [sb(f"gate{s}", 192 + 4 * s, [P, 2, T]) for s in range(2)]
        mt = [sb(f"mt{s}", 200 + 2 * s, [P, T]) for s in range(2)]
        merged = sb("merged", 96, [P, DC, T])
        mh, ml = sb("mh", 128, [P, DC, T], f32r), sb("ml", 160, [P, DC, T], f32r)
        xres = sb("xres", 56, [P, TB, D])
        ybuf = [sb(f"ybuf{s}", 192 + 2 * s, [P, T]) for s in range(2)]
        ln_g, ln_b = sb("ln_g", 88, [P, D]), sb("ln_b", 96, [P, D])
        xn2 = sb("xn2", 160, [P, TB, D])
        h2h, h2l = sb("h2h", 104, [P, DC, T], f32r), sb("h2l", 8, [P, DC, T], f32r)
        aff2 = [sb(f"aff2_{s}", 40 + 2 * s, [P, T]) for s in range(2)]
        w2raw = [sb(f"w2raw{s}", 40 + 8 * s, [P, DC, P]) for s in range(2)]
        w2h = [sb(f"w2h{s}", 56 + 8 * s, [P, DC, P], f32r) for s in range(2)]
        w2l = [sb(f"w2l{s}", 72 + 8 * s, [P, DC, P], f32r) for s in range(2)]
        keys = sb("keys", 88, [P, 2 * PH, P])
        keyh, keyl = sb("keyh", 136, [P, 2 * PH, P], f32r), sb("keyl", 144, [P, 2 * PH, P], f32r)
        pq = [[sb(f"pq{p}{s}", 152 + 4 * s + 2 * p, [P, T], f32r) for s in range(2)] for p in range(2)]
        score = sb("score", 168, [P, TB, 2 * PH, NK])
        sc1 = sb("tk_sc1", 40, [P, 2 * PH, NK])
        sc2 = sb("tk_sc2", 48, [P, 2 * PH, NK])
        top = sb("tk_top", 56, [P, 2 * PH, TOPK])
        topi = sb("tk_topi", 57, [P, 2 * PH, TOPK], u32)
        topf = sb("tk_topf", 58, [P, 2 * PH, TOPK])
        cand = sb("tk_cand", 59, [P, PH, 256])
        cand2 = sb("tk_cand2", 67, [P, PH, 256])
        best = sb("tk_best", 75, [P, PH, TOPK])
        besti = sb("tk_besti", 75.5, [P, PH, TOPK], u32)
        bpos = sb("tk_bpos", 76, [P, 2, PH, TOPK], u32)
        bposf = sb("tk_bposf", 77, [P, 2, PH, TOPK])
        pick = sb("tk_pick", 78, [P, PH * TOPK, TOPK])
        chosen = sb("tk_chosen", 86, [P, 3, PH * TOPK])
        smalls = sb("tk_smalls", 87.5, [P, 3, PH])
        wait_pad = sb("wait_pad", 87.875, [P, 1])
        iota = sb("iota", 88, [P, P])
        chT = sb("chT", 89, [P, 3, T])
        chwh, chwl = sb("chwh", 95, [P, T], f32r), sb("chwl", 97, [P, T], f32r)
        oneI = [sb(f"oneI{s}", 40 + 2 * s, [P, 4, P], f32r) for s in range(2)]
        oneJh = [sb(f"oneJh{s}", 44 + 2 * s, [P, 4, P], f32r) for s in range(2)]
        oneJl = [sb(f"oneJl{s}", 48 + 2 * s, [P, 4, P], f32r) for s in range(2)]
        RT = 64
        route = [sb(f"route{s}", 136 + 32 * s, [P, NK, RT]) for s in range(2)]
        uraw = [sb(f"uraw{s}", 40 + 8 * s, [P, D]) for s in range(2)]
        vraw = [sb(f"vraw{s}", 56 + 8 * s, [P, D]) for s in range(2)]
        uTh, uTl = sb("uTh", 72, [P, DC, P], f32r), sb("uTl", 80, [P, DC, P], f32r)
        wt = [sb(f"wt{s}", 88 + 2 * s, [P, T]) for s in range(2)]
        act_g = sb("act_g", 5.5, [P, T])
        coh = [sb(f"coh{s}", 92 + 2 * s, [P, T], f32r) for s in range(4)]
        col = [sb(f"col{s}", (100, 102, 136, 138)[s], [P, T], f32r) for s in range(4)]
        v2h, v2l = sb("v2h", 140, [P, 2, D], f32r), sb("v2l", 156, [P, 2, D], f32r)
        acc = sb("acc", 172, [P, TB, D])
        xfin = sb("xfin", 8, [P, TB, D])
        g2row, ln2_g, ln2_b = sb("g2row", 40, [P, D]), sb("ln2_g_b", 48, [P, D]), sb("ln2_b_b", 56, [P, D])
        diag2 = sb("diag2", 64, [P, 4, P])
        affc = [sb(f"affc{s}", 5.5 + s, [P, TC]) for s in range(2)]

        pp = [ctx.enter_context(nc.psum_tensor(f"pp{k}", [P, 1024], fp32)) for k in range(4)]
        raw_q = praw_q[:, :, :].rearrange("p c (h n) -> p c h n", h=2)
        q_parts = [(raw_q[:, :, :, 0:NOPE], 0, 2 * NOPE), (raw_q[:, :, :, NOPE:QK], 2 * NOPE, 2 * QK)]

        pb = [pp[k // 2][:, 512 * (k % 2):512 * (k % 2) + 512] for k in range(8)]

        vec_in, x_in, cst_in = sem("vec_in"), sem("x_in"), sem("cst_in")
        wm_in = [sem(f"wm_in{s}") for s in range(2)]
        ones_set, half_set = sem("ones_set"), sem("half_set")
        vec_turned, vec_copied = sem("vec_turned"), sem("vec_copied")
        silu_exp, silu_set = sem("silu_exp"), sem("silu_set")
        wm_used, mod_set = sem("wm_used"), sem("mod_set")
        var_set, rstd_set, xn_set = sem("var_set"), sem("rstd_set"), sem("xn_set")
        h_turned, h_affine, h_split = sem("h_turned"), sem("h_affine"), sem("h_split")
        swap_set = sem("swap_set")
        w_in_ = [sem(f"w_in{s}") for s in range(2)]
        w_hi, w_lo, w_used, w_out_ = sem("w_hi"), sem("w_lo"), sem("w_used"), sem("w_out_done")
        dve_chain, act_chain = sem("dve_chain"), sem("act_chain")
        sq_set, sq_used = sem("sq_set"), sem("sq_used")
        ssq_done = sem("ssq_done")
        dg_set, lora_scaled, lora_split = sem("dg_set"), sem("lora_scaled"), sem("lora_split")
        h_hi, one_plus, stg_set = sem("h_hi"), sem("one_plus"), sem("stg_set")
        st_done = [sem(f"st_done{s}") for s in range(2)]
        bc_done, lora_hi, kr_hi = sem("bc_done"), sem("lora_hi"), sem("kr_hi")
        row_turned = sem("row_turned")
        mu_in = [sem(f"mu_in{s}") for s in range(5)]
        mu_prod, mu_red, mu_sum, mu_set = sem("mu_prod"), sem("mu_red"), sem("mu_sum"), sem("mu_set")
        pw_in, pw_hi, pw_lo = sem("pw_in"), sem("pw_hi"), sem("pw_lo")
        pj_done, pj_hi, pj_lo, rope_set = sem("pj_done"), sem("pj_hi"), sem("pj_lo"), sem("rope_set")
        s_done, rope_mid, mx_set, nmx_set, exp_done, inv_set, prob_set = (
            sem(n) for n in ("s_done", "rope_mid", "mx_set", "nmx_set", "exp_done", "inv_set", "prob_set"))
        p_turned, pT_hi, pT_lo, pv_done, o_set = (
            sem(n) for n in ("p_turned", "pT_hi", "pT_lo", "pv_done", "o_set"))
        dft_in, dft_hi, dft_split, f_in = sem("dft_in"), sem("dft_hi"), sem("dft_split"), sem("f_in")
        f_turned, f_hi, f_lo = sem("f_turned"), sem("f_hi"), sem("f_lo")
        g_done, g_hi, g_lo, y_done, y_hi, y_lo = (sem(n) for n in ("g_done", "g_hi", "g_lo", "y_done", "y_hi", "y_lo"))
        o_hi, o_lo = sem("o_hi"), sem("o_lo")
        gate_in = [sem(f"gate_in{s}") for s in range(2)]
        merged_set, m_hi, m_lo = sem("merged_set"), sem("m_hi"), sem("m_lo")
        res_in, y_turned, y_added, ln_in = sem("res_in"), sem("y_turned"), sem("y_added"), sem("ln_in")
        x1_set, x1_stored, xn2_set = sem("x1_set"), sem("x1_stored"), sem("xn2_set")
        h2_turned, h2_affine, h2_hi, h2_split = (sem(n) for n in ("h2_turned", "h2_affine", "h2_hi", "h2_split"))
        keys_in, keys_turned, key_hi, key_lo = (sem(n) for n in ("keys_in", "keys_turned", "key_hi", "key_lo"))
        pq_hi, sc_done, sc_set = sem("pq_hi"), sem("sc_done"), sem("sc_set")
        tk_chain, iota_in, tk_diff, tk_exp, tk_chosen, ch_turned, ch_set, chw_hi, chw_set = (
            sem(n) for n in ("tk_chain", "iota_in", "tk_diff", "tk_exp", "tk_chosen", "ch_turned", "ch_set", "chw_hi", "chw_set"))
        one_set, r_done, r_set = sem("one_set"), sem("r_done"), sem("r_set")
        r_stored = [sem(f"r_stored{s}") for s in range(2)]
        u_in = [sem(f"u_in{s}") for s in range(2)]
        v_in = [sem(f"v_in{s}") for s in range(2)]
        wt_in = [sem(f"wt_in{s}") for s in range(2)]
        u_turned, u_hi, u_lo, a_done, gelu_set = (sem(n) for n in ("u_turned", "u_hi", "u_lo", "a_done", "gelu_set"))
        co_set, co_hi, co_lo, v_hi, v_lo, e_done, e_added = (
            sem(n) for n in ("co_set", "co_hi", "co_lo", "v_hi", "v_lo", "e_done", "e_added"))
        fin_in, fin_set, fin_stored, g2_diag, g2_done, g2_copied = (
            sem(n) for n in ("fin_in", "fin_set", "fin_stored", "g2_diag", "g2_done", "g2_copied"))
        kr_ready, kr_swapped, kr_roped, kr_split = (sem(n) for n in
                                                    ("kr_ready", "kr_swapped", "kr_roped", "kr_split"))

        block = ctx.enter_context(nc.Block())

        wmod_v = a["w_mod"][0].rearrange("(c p) n -> p c n", p=P)
        win_v = a["w_in"][0].rearrange("(c p) n -> p c n", p=P)
        NPX = 49
        FIRST_ST = 9
        MG1 = 16
        MU = 2 * MG1
        SS = QK ** -0.5

        @block.sync
        def _(sp):
            def row(n0, n1, src):
                sp.dma_start(vrows[n0:n1, :], src).then_inc(vec_in, 16)

            row(V_C, V_CC, a["c"][0].rearrange("(r n) -> r n", n=P))
            row(V_CC, V_QG, a["c_ctx"].rearrange("(r n) -> r n", n=P))
            row(V_QG, V_KVG, a["q_norm_g"][0].rearrange("(r n) -> r n", n=P))
            row(V_KVG, V_BKV, a["kv_norm_g"][0].rearrange("(r n) -> r n", n=P))
            row(V_BKV, V_BKR, a["b_in"][0, 0:C_KR].rearrange("(r n) -> r n", n=P))
            row(V_BR, V_ROWS, a["b_in"][0, C_CQ:].rearrange("(r n) -> r n", n=P))
            for h in range(2):
                sp.dma_start(vrows[V_BKR:V_BKR + 1, ROPE * h:ROPE * h + ROPE],
                             a["b_in"][0:1, C_KR:C_CQ]).then_inc(vec_in, 16)
            sp.dma_start(mrows[0:96, :], a["b_mod"][0].rearrange("(r n) -> r n", n=P)).then_inc(vec_in, 16)
            sp.dma_start(ident[:, :], a["k_ident"]).then_inc(vec_in, 16)
            sp.dma_start(swap_f[:, :], a["k_swap"]).then_inc(vec_in, 16)

            def mod_group(g, s):
                if not isinstance(g, int) or g >= 2:
                    sp.wait_ge(wm_used, g - 1)
                sp.dma_start(wm[s][:, :, :], wmod_v[:, :, bass.ts(g, 256)]).then_inc(wm_in[s], 16)

            mod_group(0, 0)
            mod_group(1, 1)
            with sp.Fori(1, MG1 // 2) as i:
                mod_group(2 * i, 0)
                mod_group(2 * i + 1, 1)

            sp.wait_ge(h_turned, DC)

            def px_block(b, s):
                if not isinstance(b, int) or b >= 2:
                    sp.wait_ge(w_lo, b - 1)
                if isinstance(b, int) and b == 4:
                    for h in range(2):
                        sp.dma_start(wraw[s][:, :, ROPE * h:ROPE * h + ROPE],
                                     win_v[:, :, C_KR:C_CQ]).then_inc(w_in_[s], 16)
                    return
                at = b * P if isinstance(b, int) and b < 4 else (b - 5) * P + C_CQ
                sp.dma_start(wraw[s][:, :, :], win_v[:, :, bass.ds(at, P)]).then_inc(w_in_[s], 16)

            def mod_unit(j, s, wait=None):
                if wait is not None:
                    sp.wait_ge(mu_red, wait)
                sp.dma_start(mbuf[s][:, :, :], wmod_v[:, :, bass.ds((j + MU) * P, P)]).then_inc(mu_in[s], 16)

            for b in range(17):
                px_block(b, b % 2)
            sp.wait_ge(lora_split, 2 * LC)
            mod_unit(0, 0)
            mod_unit(1, 1)
            px_block(17, 1)
            px_block(18, 0)
            with sp.Fori(1, 16) as i:
                px_block(2 * i + 17, 1)
                mod_unit(2 * i, 0, 2 * i - 1)
                px_block(2 * i + 18, 0)
                mod_unit(2 * i + 1, 1, 2 * i)

            uq_v = a["w_uq"][0].rearrange("(c p) n -> p c n", p=P)
            ukv_v = a["w_ukv"][0].rearrange("(c p) n -> p c n", p=P)
            sp.wait_ge(w_lo, NPX)

            def pair_loads(p):
                sp.dma_start(praw_q[:, :, :], uq_v[:, :, bass.ds(p * (2 * QK), 2 * QK)]).then_inc(pw_in, 16)
                sp.dma_start(praw_kv[:, :, :], ukv_v[:, :, bass.ds(p * 512, 512)]).then_inc(pw_in, 16)

            pair_loads(0)
            with sp.Fori(1, HEADS // 2) as p:
                sp.wait_ge(pw_lo, 2 * p)
                pair_loads(p)

            sp.wait_ge(pj_done, 10 * (HEADS // 2))
            sp.dma_start(dtraw[:, :, :, :], a["k_dft_t"].rearrange("w (b p) s -> p w b s", p=P)).then_inc(dft_in, 16)
            sp.wait_ge(pv_done, HEADS)
            for ss in st_done:
                sp.wait_ge(ss, 16 * ((NPX - FIRST_ST) // 2))
            sp.dma_start(dcraw[:, :, :, :], a["k_dft_c"].rearrange("w (b p) c -> p w b c", p=P)).then_inc(dft_in, 16)
            sp.dma_start(fT[:, :, :], px_d[0:2].rearrange("k p t -> p k t")).then_inc(f_in, 16)
            with sp.Fori(1, FG) as g:
                sp.wait_ge(f_turned, g * 2)
                sp.dma_start(fT[:, :, :], px_d[bass.ds(2 * g, 2)].rearrange("k p t -> p k t")).then_inc(f_in, 16)

            wo_v = a["w_o_mla"][0].rearrange("(c p) n -> p c n", p=P)
            wf_v = a["w_fourier"][0].rearrange("(c p) n -> p c n", p=P)
            wout_v = a["w_out"][0].rearrange("(c p) n -> p c n", p=P)
            sp.wait_ge(y_lo, FD // P)

            def merge_loads(m, s):
                sp.wait_ge(w_lo, 2 * m + NPX - 1)
                sp.dma_start(wraw[1][:, :, :], wo_v[:, :, bass.ts(m, P)]).then_inc(w_in_[1], 16)
                sp.wait_ge(w_lo, 2 * m + NPX)
                sp.dma_start(wraw[0][:, 0:FD // P, :], wf_v[:, :, bass.ts(m, P)]).then_inc(w_in_[0], 16)
                if not isinstance(m, int) or m >= 2:
                    sp.wait_ge(merged_set, m - 1)
                sp.dma_start(gate[s][:, 0, :], px_d[bass.ds(m + 8, 1)].rearrange("a p t -> (a p) t")).then_inc(gate_in[s], 16)
                sp.dma_start(gate[s][:, 1, :], px_d[bass.ds(m + 24, 1)].rearrange("a p t -> (a p) t")).then_inc(gate_in[s], 16)
                mod_unit(m + 32, 2, m + 32)

            merge_loads(0, 0)
            merge_loads(1, 1)
            with sp.Fori(1, DC // 2) as i:
                merge_loads(2 * i, 0)
                merge_loads(2 * i + 1, 1)
            NM = NPX + 2 * DC
            sp.wait_ge(w_lo, NM - 1)
            sp.dma_start(wraw[1][:, :, :], wout_v[:, :, 0:P]).then_inc(w_in_[1], 16)
            sp.wait_ge(w_lo, NM)
            sp.dma_start(wraw[0][:, :, :], wout_v[:, :, P:2 * P]).then_inc(w_in_[0], 16)
            sp.wait_ge(w_used, NM)
            sp.dma_start(xres[:, :, :], a["x"][0].rearrange("(b p) d -> p b d", p=P)).then_inc(res_in, 16)
            sp.wait_ge(m_lo, DC)
            sp.wait_ge(mu_red, 48)
            sp.dma_start(ln_g[:, :], a["ln1_g"][0:1, :].to_broadcast([P, D])).then_inc(ln_in, 16)
            sp.dma_start(ln_b[:, :], a["ln1_b"][0:1, :].to_broadcast([P, D])).then_inc(ln_in, 16)
            with sp.Fori(1, DC // 2) as i:
                sp.wait_ge(w_lo, 2 * i + NM - 1)
                sp.dma_start(wraw[1][:, :, :], wout_v[:, :, bass.ds(i * (2 * P), P)]).then_inc(w_in_[1], 16)
                sp.wait_ge(w_lo, 2 * i + NM)
                sp.dma_start(wraw[0][:, :, :], wout_v[:, :, bass.ds(i * (2 * P) + P, P)]).then_inc(w_in_[0], 16)
            for b in range(TB):
                sp.wait_ge(x1_set, b + 1)
                sp.dma_start(x1_d[P * b:P * b + P, :], xres[:, b, :]).then_inc(x1_stored, 16)
            wq_v = a["peer_wq"][0].rearrange("(c p) n -> p c n", p=P)
            NO = NM + DC
            sp.wait_ge(x1_set, TB)
            sp.dma_start(keys[:, :, :], a["peer_keys"][0].rearrange("h p k d -> k (h p) d")).then_inc(keys_in, 16)
            sp.wait_ge(h2_split, DC)
            sp.wait_ge(keys_turned, 4)
            with sp.Fori(0, DC // 2) as i:
                for s in (1, 0):
                    sp.wait_ge(w_lo, 2 * i + NO - s)
                    sp.dma_start(w2raw[s][:, :, :], wq_v[:, :, bass.ds(i * (2 * P) + (1 - s) * P, P)]).then_inc(w_in_[s], 16)
                    mod_unit(2 * i + 49 - s, 4 - s, 2 * i + 48 - s)

            sp.wait_ge(mu_red, 64)
            sp.dma_start(iota[:, :], a["k_iota"]).then_inc(iota_in, 16)
            sp.wait_ge(ch_set, TB)
            for ss in r_stored:
                sp.sem_inc(ss, 16)
            with sp.Fori(0, T // RT // 2) as i:
                for s in range(2):
                    sp.wait_ge(r_set, 32 * i + 16 * s + 16)
                    sp.dma_start(route_d[:, :, bass.ds(i * (2 * RT) + s * RT, RT)], route[s][:, :, :]).then_inc(r_stored[s], 16)
            for ss in r_stored:
                sp.wait_ge(ss, 16 * (T // RT // 2) + 16)

            u_v = a["peer_u"][0].rearrange("(i j) d -> i j d", j=NK)
            v_v = a["peer_v"][0].rearrange("(i j) d -> i j d", j=NK)
            sp.wait_ge(r_done, P)

            flat = lambda t, k: t[bass.ds(k, 1)].rearrange("a j d -> (a j) d")

            def u_load(i, s):
                if not isinstance(i, int) or i >= 2:
                    sp.wait_ge(u_turned, i - 1)
                sp.dma_start(uraw[s][:, :], flat(u_v, i)).then_inc(u_in[s], 16)

            def coef_loads(i, s):
                if not isinstance(i, int) or i >= 2:
                    sp.wait_ge(co_set, i - 1)
                sp.dma_start(wt[s][:, :], route_d[:, bass.ds(i, 1), :].rearrange("j a t -> j (a t)")).then_inc(wt_in[s], 16)
                if not isinstance(i, int) or i >= 2:
                    sp.wait_ge(v_lo, i - 1)
                sp.dma_start(vraw[s][:, :], flat(v_v, i)).then_inc(v_in[s], 16)

            u_load(0, 0)
            u_load(1, 1)
            coef_loads(0, 0)
            u_load(2, 0)
            coef_loads(1, 1)
            with sp.Fori(1, NK // 2 - 1) as i:
                u_load(2 * i + 1, 1)
                coef_loads(2 * i, 0)
                u_load(2 * i + 2, 0)
                coef_loads(2 * i + 1, 1)
            u_load(NK - 1, 1)
            coef_loads(NK - 2, 0)
            coef_loads(NK - 1, 1)
            sp.wait_ge(a_done, NK)
            sp.wait_ge(x1_stored, 16 * TB)
            sp.dma_start(xfin[:, :, :], x1_d.rearrange("(b p) d -> p b d", p=P)).then_inc(fin_in, 16)
            sp.wait_ge(v_lo, NK)
            sp.dma_start(ln2_g[:, :], a["ln2_g"][0:1, :].to_broadcast([P, D])).then_inc(fin_in, 16)
            sp.dma_start(ln2_b[:, :], a["ln2_b"][0:1, :].to_broadcast([P, D])).then_inc(fin_in, 16)
            for b in range(TB):
                sp.wait_ge(fin_set, b + 1)
                sp.dma_start(out[0, P * b:P * b + P, :], acc[:, b, :]).then_inc(fin_stored, 16)
            sp.wait_ge(fin_stored, 16 * TB)
            for ss in st_done:
                sp.wait_ge(ss, 16 * ((NPX - FIRST_ST) // 2))

        def w_loaded(b):
            if isinstance(b, int):
                return 16 * (b // 2 + 1) + (16 if b % 2 == 0 and b >= 4 else 0)
            raise AssertionError

        @block.gpsimd
        def _(pool):
            pool.memset(ones[:, :], 1.0).then_inc(ones_set, 1)
            pool.memset(mhalf[:, :], -0.5).then_inc(half_set, 1)
            pool.wait_ge(half_set, 1)
            pool.wait_ge(var_set, 1)
            pool.tensor_tensor(rstd[:, 0:6], vare[:, 0:6], mhalf[:, 0:6], ALU.pow).then_inc(rstd_set, 1)
            pool.wait_ge(var_set, 2)
            pool.tensor_tensor(rstd[:, 0:6], vare[:, 0:6], mhalf[:, 0:6], ALU.pow).then_inc(rstd_set, 1)
            pool.wait_ge(var_set, 3)
            pool.tensor_tensor(rstd[:, 0:4], vare[:, 0:4], mhalf[:, 0:4], ALU.pow).then_inc(rstd_set, 1)

            def store(n, s):
                pool.wait_ge(stg_set, n + 1)
                pool.dma_start(px_d[bass.ds(n, 1)].rearrange("a p t -> (a p) t"), stg[s][:, :]).then_inc(st_done[s], 16)

            def unit(s, at):
                pool.wait_ge(mu_in[s], at)
                pool.tensor_tensor(mbuf[s][:, :, :], mbuf[s][:, :, :], silu[:, :, 0:1].to_broadcast([P, DC, P]),
                                   ALU.mult).then_inc(mu_prod, 1)

            with pool.Fori(0, 4) as i:
                store(2 * i, 0)
                store(2 * i + 1, 1)
            with pool.Fori(0, 16) as i:
                for s in range(2):
                    unit(s, 16 * i + 16)
                    store(2 * i + 8 + s, s)
            with pool.Fori(0, DC) as m:
                unit(2, 16 * m + 16)
            def inv_std(k, n):
                pool.wait_ge(var_set, n)
                pool.tensor_tensor(rstd[:, k:k + 1], vare[:, k:k + 1], mhalf[:, k:k + 1], ALU.pow).then_inc(rstd_set, 1)

            for n, k in enumerate(LN_ORDER):
                inv_std(k, 4 + n)
            with pool.Fori(0, DC // 2) as m:
                for s in (3, 4):
                    unit(s, 16 * m + 16)
            for b in range(TB):
                inv_std(b, 12 + b)

        @block.scalar
        def _(act):
            ch = Tally(act, act_chain)
            act.dma_start(xtok[:, :, :], a["x"][0].rearrange("(b p) d -> p b d", p=P)).then_inc(x_in, 16)
            act.dma_start(ctok[:, :, :], a["ctx"][0].rearrange("(b p) d -> p b d", p=P)).then_inc(x_in, 16)
            act.dma_start(rot[:, :, :], a["k_rot"]).then_inc(cst_in, 16)
            act.wait_ge(vec_copied, 1)
            act.activation(silu_t[:, :], vecT[:, 0:2 * DC], ACT.Exp, scale=-1.0).then_inc(silu_exp, 1)
            act.wait_ge(vec_in, 176)
            act.activation(swap[:, :], swap_f[:, :], ACT.Copy).then_inc(swap_set, 1)

            act.wait_ge(one_plus, 1)
            for c in range(DC):
                s = c % 2
                act.wait_ge(h_turned, c + 1)
                if c >= 2:
                    act.wait_ge(h_split, c - 1)
                act.activation(affx[s][:, :], pb[s][:, :], ACT.Identity,
                               scale=modT[:, M_SC1 + c, 0:1], bias=modT[:, M_SH1 + c, 0:1])
                ch.inc(act.activation(affc[s][:, :], pb[2 + s][:, 0:TC], ACT.Identity,
                                      scale=modT[:, M_SC1 + c, 1:2], bias=modT[:, M_SH1 + c, 1:2]))
                act.wait_ge(act_chain, ch.at)
                act.activation(hxh[:, c, :], affx[s][:, :], ACT.Copy)
                act.activation(hch[:, c, :], affc[s][:, :], ACT.Copy).then_inc(h_hi, 1)

            def w_split(b, s, at, n=DC):
                act.wait_ge(w_in_[s], at)
                if not isinstance(b, int) or b >= 2:
                    act.wait_ge(w_used, b - 1)
                act.activation(wh[s][:, 0:n, :], wraw[s][:, 0:n, :], ACT.Copy).then_inc(w_hi, 1)

            def col_of(n):
                return vecT[:, bass.ds(n, 1)]

            def px_store(b, s, n, slot, func):
                act.wait_ge(w_used, b + 1)
                if not isinstance(n, int) or n >= 2:
                    act.wait_ge(st_done[slot], (n - slot) * 8)
                act.activation(stg[slot][:, :], pb[s][:, :], func, bias=col_of(b - 5 + V_BR)).then_inc(w_out_, 1)
                act.wait_ge(w_out_, b + 1)
                act.sem_inc(stg_set, 1)

            w_split(0, 0, w_loaded(0))
            for b in range(11):
                s = b % 2
                w_split(b + 1, (b + 1) % 2, w_loaded(b + 1))
                if b < 5:
                    dst = ckv[:, b, :] if b < 4 else kr[:, :]
                    act.wait_ge(w_used, b + 1)
                    bias = vecT[:, V_BKV + b:V_BKV + b + 1]
                    act.activation(dst[:, 0:T], pb[s][:, :], ACT.Identity, bias=bias)
                    act.activation(dst[:, T:NKEY], pb[2 + s][:, 0:TC], ACT.Identity, bias=bias).then_inc(w_out_, 1)
                elif b < 9:
                    act.wait_ge(w_used, b + 1)
                    act.activation(cq[:, b - 5, :], pb[s][:, :], ACT.Identity, bias=col_of(b - 5 + V_BR)).then_inc(w_out_, 1)
                else:
                    px_store(b, s, b - FIRST_ST, b - FIRST_ST, ACT.Identity)
                if b == 4:
                    act.wait_ge(w_out_, 5)
                    act.wait_ge(vec_copied, 1)
                    act.activation(krh[:, :], kr[:, :], ACT.Copy).then_inc(kr_hi, 1)
                if b == 6:
                    act.wait_ge(kr_roped, 1)
                    act.activation(krh[:, :], kr[:, :], ACT.Copy).then_inc(kr_hi, 1)
                if b == 7:
                    for k in range(LC):
                        act.wait_ge(lora_scaled, k + 1)
                        act.activation(ckvh[:, k, :], ckv[:, k, :], ACT.Copy).then_inc(lora_hi, 1)
                if b == 10:
                    for k in range(LC):
                        act.wait_ge(lora_scaled, LC + k + 1)
                        act.activation(cqh[:, k, :], cq[:, k, :], ACT.Copy).then_inc(lora_hi, 1)
            with act.Fori(0, 3) as i:
                for u in range(2):
                    w_split(2 * i + 12 + u, u, 16 * i + 16 * 7 + (16 if u == 0 else 0))
                    px_store(2 * i + 11 + u, 1 - u, 2 * i + 2 + u, u, ACT.Identity)
            with act.Fori(0, 15) as i:
                for u in range(2):
                    w_split(2 * i + 18 + u, u, 16 * i + 16 * 10 + (16 if u == 0 else 0))
                    px_store(2 * i + 17 + u, 1 - u, 2 * i + 8 + u, u, ACT.Sigmoid)
            w_split(48, 0, w_loaded(48))
            px_store(47, 1, 38, 0, ACT.Sigmoid)
            px_store(48, 0, 39, 1, ACT.Sigmoid)

            def pair_split(p, which):
                act.wait_ge(pw_in, 32 * p + 32)
                if which == 0:
                    for src, c0, c1 in q_parts:
                        ins = act.activation(pqh[:, :, c0:c1].rearrange("p c (h n) -> p c h n", h=2), src, ACT.Copy)
                    ins.then_inc(pw_hi, 1)
                else:
                    act.activation(pkh[:, :, :], praw_kv[:, :, :], ACT.Copy).then_inc(pw_hi, 1)

            def tile_hi(p, n, dst, src):
                act.wait_ge(pj_done, 10 * p + n + 1)
                act.activation(dst, src, ACT.Copy).then_inc(pj_hi, 1)

            def attention_pair(p, last=False):
                B = (pb[4], pb[5])
                tile_hi(p, 0, qrh[:, :], B[0][:, :])
                for h in range(2):
                    tile_hi(p, 1 + h, qh[:, h, :], B[(1 + h) % 2][:, :])
                act.wait_ge(rope_set, p + 1)
                tile_hi(p, 3, qrh[:, :], rt[0][:, :])
                for h in range(2):
                    tile_hi(p, 4 + h, kTh[:, h, 0:T], B[h][:, :])
                tile_hi(p, 6, kTh[:, :, T:NKEY], B[0][:, :].rearrange("p (h t) -> p h t", h=2))
                for v in range(3):
                    tile_hi(p, 7 + v, vh[:, 2 * v:2 * v + 2, :, :],
                            B[(7 + v) % 2][:, :].rearrange("p (b h d) -> p b h d", b=2, h=2))

                def turned_hi(n):
                    act.wait_ge(p_turned, 8 * p + n + 1)
                    if n % 4 == 0 and (n > 0 or not isinstance(p, int) or p > 0):
                        act.wait_ge(pv_done, 2 * p + n // 4)
                    act.activation(pTh[:, :, P * (n % 4):P * (n % 4) + P],
                                   pp[3][:, 0:NKEY].rearrange("p (k t) -> p k t", k=KB), ACT.Copy).then_inc(pT_hi, 1)

                def keep_out(h):
                    act.wait_ge(pv_done, 2 * p + h + 1)
                    act.activation(oT[:, bass.ds(2 * p + h, 1), :].rearrange("p a t -> p (a t)"), pb[4 + h][:, :],
                                   ACT.Copy).then_inc(o_set, 1)

                for n in range(8):
                    act.wait_ge(nmx_set, 8 * p + n + 1)
                    if n >= 2 or not isinstance(p, int) or p > 0:
                        act.wait_ge(p_turned, 8 * p + n - 1)
                    act.activation(prob[n % 2][:, :], pp[n % 2][:, 0:NKEY], ACT.Exp, bias=nmx[:, n:n + 1], scale=SS,
                                   accum_out=rsum[:, n:n + 1]).then_inc(exp_done, 1)
                    if n >= 1:
                        turned_hi(n - 1)
                    if n == 6:
                        keep_out(0)
                    if n in (2, 3) and not last:
                        pair_split(p + 1, n - 2)
                turned_hi(7)
                keep_out(1)

            act.wait_ge(w_used, NPX)
            pair_split(0, 0)
            pair_split(0, 1)
            for ss in st_done:
                act.wait_ge(ss, 16 * ((NPX - FIRST_ST) // 2))
            attention_pair(0)
            with act.Fori(1, HEADS // 2 - 1) as p:
                attention_pair(p)
            attention_pair(HEADS // 2 - 1, True)

            act.wait_ge(dft_in, 32)
            act.wait_ge(pj_done, 10 * (HEADS // 2))
            for w in range(2):
                act.activation(dth[:, w, :, :], dtraw[:, w, :, :], ACT.Copy)
            act.activation(dch[:, :, :, :], dcraw[:, :, :, :], ACT.Copy).then_inc(dft_hi, 1)
            act.wait_ge(pv_done, HEADS)
            act.wait_ge(o_set, HEADS)
            for c in range(4):
                act.activation(oh[:, 4 * c:4 * c + 4, :], oT[:, 4 * c:4 * c + 4, :], ACT.Copy).then_inc(o_hi, 1)
            with act.Fori(0, FG) as g:
                for cb in range(2):
                    act.wait_ge(f_turned, 2 * g + cb + 1)
                    act.activation(fh[:, :, P * cb:P * cb + P], pb[cb][:, :].rearrange("p (b c) -> p b c", b=TB),
                                   ACT.Copy).then_inc(f_hi, 1)
                for n in range(4):
                    act.wait_ge(g_done, 4 * g + n + 1)
                    act.activation(gh[:, n % 2, n // 2, :], pb[2 + n][:, :], ACT.Copy).then_inc(g_hi, 1)
                for k in range(2):
                    act.wait_ge(y_done, 2 * g + k + 1)
                    act.activation(yh[:, bass.ds(2 * g + k, 1), :].rearrange("p a t -> p (a t)"), pb[6 + k][:, :],
                                   ACT.Copy).then_inc(y_hi, 1)

            NM, NO = NPX + 2 * DC, NPX + 3 * DC
            act.wait_ge(y_done, FD // P)

            def wo_hi(m):
                w_split(2 * m + NPX, 1, 16 * m + 16 * 25)

            def wf_hi(m):
                w_split(2 * m + NPX + 1, 0, 16 * m + 16 * 27, FD // P)

            with act.Fori(0, DC) as m:
                wo_hi(m)
                wf_hi(m)
            act.wait_ge(w_used, NM)
            w_split(NM, 1, 16 * 41)
            for c in range(4):
                act.wait_ge(merged_set, 4 * c + 4)
                act.activation(mh[:, 4 * c:4 * c + 4, :], merged[:, 4 * c:4 * c + 4, :], ACT.Copy).then_inc(m_hi, 1)

            def out_block(n, s):
                act.wait_ge(w_used, n + NM + 1)
                if not isinstance(n, int) or n >= 2:
                    act.wait_ge(y_turned, n - 1)
                act.activation(ybuf[1 - s][:, :], pb[s][:, :], ACT.Identity,
                               scale=modT[:, bass.ds(n + M_G1, 1), 0:1].rearrange("p a b -> p (a b)")).then_inc(w_out_, 1)

            act.wait_ge(mu_set, 1)
            w_split(NM + 1, 0, 16 * 43)
            out_block(0, 1)
            w_split(NM + 2, 1, 16 * 42)
            out_block(1, 0)
            with act.Fori(1, DC // 2 - 1) as i:
                w_split(2 * i + NM + 1, 0, 16 * i + 16 * 43)
                out_block(2 * i, 1)
                w_split(2 * i + NM + 2, 1, 16 * i + 16 * 42)
                out_block(2 * i + 1, 0)
            w_split(NM + 15, 0, 16 * 50)
            out_block(14, 1)
            out_block(15, 0)

            act.wait_ge(mu_set, 3)
            for c in range(DC):
                s = c % 2
                act.wait_ge(h2_turned, c + 1)
                if c >= 2:
                    act.wait_ge(h2_split, c - 1)
                act.activation(aff2[s][:, :], pb[s][:, :], ACT.Identity, scale=modT[:, M_SC2 + c, 0:1],
                               bias=modT[:, M_SH2 + c, 0:1]).then_inc(h2_affine, 1)
                act.wait_ge(h2_affine, c + 1)
                act.activation(h2h[:, c, :], aff2[s][:, :], ACT.Copy).then_inc(h2_hi, 1)

            for k in range(4):
                act.wait_ge(keys_turned, k + 1)
                act.activation(keyh[:, 4 * k:4 * k + 4, :], pb[4 + k][:, :].rearrange("p (n k) -> p n k", n=4),
                               ACT.Copy).then_inc(key_hi, 1)
            act.wait_ge(x1_stored, 16 * TB)

            def q_split(b, s, at):
                act.wait_ge(w_in_[s], at)
                act.wait_ge(w_used, b - 1)
                act.activation(w2h[s][:, :, :], w2raw[s][:, :, :], ACT.Copy).then_inc(w_hi, 1)

            def q_block(n, s):
                act.wait_ge(w_used, n + NO + 1)
                if not isinstance(n, int) or n >= 2:
                    act.wait_ge(sc_done, n - 1)
                act.activation(pq[0][s][:, :], pb[s][:, :], ACT.Copy).then_inc(pq_hi, 1)

            def keep_score(n, s):
                act.wait_ge(sc_done, n + 1)
                act.activation(score[:, :, bass.ds(n, 1), :].rearrange("p b a k -> p b (a k)"),
                               pb[2 + s][:, :].rearrange("p (b k) -> p b k", b=TB), ACT.Copy).then_inc(sc_set, 1)

            act.wait_ge(h2_split, DC)
            q_split(NO, 1, 16 * 49)
            q_split(NO + 1, 0, 16 * 51)
            q_block(0, 1)
            with act.Fori(0, DC // 2 - 1) as i:
                q_split(2 * i + NO + 2, 1, 16 * i + 16 * 50)
                q_block(2 * i + 1, 0)
                keep_score(2 * i, 1)
                q_split(2 * i + NO + 3, 0, 16 * i + 16 * 52)
                q_block(2 * i + 2, 1)
                keep_score(2 * i + 1, 0)
            q_block(15, 0)
            keep_score(14, 1)
            keep_score(15, 0)

            with act.Fori(0, TB) as b:
                act.wait_ge(tk_diff, b + 1)
                act.activation(best[:, :, :], best[:, :, :], ACT.Exp).then_inc(tk_exp, 1)
            act.wait_ge(ch_set, TB)
            act.activation(chwh[:, :], chT[:, 2, :], ACT.Copy).then_inc(chw_hi, 1)

            def keep_route(g, k, slot, q):
                act.wait_ge(r_done, g + 1)
                act.activation(route[slot][:, :, 4 * q:4 * q + 4].rearrange("p i t -> p t i"),
                               pb[k][:, :].rearrange("p (t i) -> p t i", t=4), ACT.Copy).then_inc(r_set, 1)

            with act.Fori(0, T // RT // 2) as i:
                for s in range(2):
                    act.wait_ge(r_stored[s], 16 * i + 16)
                    for q in range(16):
                        keep_route(32 * i + 16 * s + q, q % 4, s, q)

            def expert_u(i):
                act.wait_ge(u_turned, i + 1)
                if not isinstance(i, int) or i >= 1:
                    act.wait_ge(a_done, i)
                for k in range(2):
                    act.activation(uTh[:, 8 * k:8 * k + 8, :], pp[k][:, :].rearrange("p (c j) -> p c j", c=8),
                                   ACT.Copy).then_inc(u_hi, 1)

            def expert_gelu(i, u):
                act.wait_ge(a_done, i + 1)
                if not isinstance(i, int) or i >= 1:
                    act.wait_ge(co_lo, i)
                act.activation(act_g[:, :], pb[4][:, :], ACT.Gelu).then_inc(gelu_set, 1)

            def expert_coef(i, slot):
                act.wait_ge(co_set, i + 1)
                act.activation(coh[slot][:, :], act_g[:, :], ACT.Copy).then_inc(co_hi, 1)

            def expert_v(i, u):
                act.wait_ge(v_in[u], 8 * (i - u) + 16)
                if not isinstance(i, int) or i >= 2:
                    act.wait_ge(e_done, 8 * (i - u))
                act.activation(v2h[:, u, :], vraw[u][:, :], ACT.Copy).then_inc(v_hi, 1)

            def expert_group(g, par, first=False, last=False):
                if not first:
                    expert_v(2 * g - 2, 0)
                    expert_v(2 * g - 1, 1)
                for u in range(2):
                    expert_gelu(2 * g + u, u)
                    if not (last and u == 1):
                        expert_u(2 * g + u + 1)
                    expert_coef(2 * g + u, 2 * par + u)

            act.wait_ge(r_done, P)
            expert_u(0)
            expert_group(0, 0, first=True)
            expert_group(1, 1)
            with act.Fori(1, NK // 4 - 1) as i:
                expert_group(2 * i, 0)
                expert_group(2 * i + 1, 1)
            expert_group(NK // 2 - 2, 0)
            expert_group(NK // 2 - 1, 1, last=True)
            expert_v(NK - 2, 0)
            expert_v(NK - 1, 1)

            for k in range(4):
                act.wait_ge(g2_done, k + 1)
                act.activation(g2row[:, 512 * k:512 * k + 512], pb[k][:, :], ACT.Copy).then_inc(g2_copied, 1)

        @block.vector
        def _(dve):
            ch = Tally(dve, dve_chain)
            dve.wait_ge(vec_turned, 1)
            dve.tensor_copy(vecT[:, :], pb[4][:, 0:V_ROWS])
            dve.tensor_copy(bmodT[:, :], pb[5][:, 0:96]).then_inc(vec_copied, 1)
            dve.wait_ge(vec_copied, 1)
            dve.wait_ge(silu_exp, 1)
            ch.link(dve.tensor_scalar(silu_t[:, :], silu_t[:, :], 1.0, None, ALU.add))
            ch.link(dve.reciprocal(silu_t[:, :], silu_t[:, :]))
            for w in range(2):
                ins = dve.tensor_tensor(silu[:, :, w], vecT[:, DC * w:DC * w + DC], silu_t[:, DC * w:DC * w + DC], ALU.mult)
            ins.then_inc(silu_set, 1)

            dve.wait_ge(x_in, 32)
            tok = [xtok[:, b, :] for b in range(TB)] + [ctok[:, b, :] for b in range(CB)]
            for n, t in enumerate(tok):
                for q in range(4):
                    ins = dve.bn_stats(stats[:, n, q, :], t[:, 512 * q:512 * q + 512])
            ch.link(ins)
            for n in range(len(tok)):
                ins = dve.bn_aggr(mv[:, n, :], stats[:, n, :, :].rearrange("p q s -> p (q s)"))
            ch.link(ins)
            dve.tensor_scalar(vare[:, 0:6], mv[:, 0:6, 1], EPS, None, ALU.add).then_inc(var_set, 1)
            dve.wait_ge(rstd_set, 1)
            for n, t in enumerate(tok):
                ins = dve.tensor_scalar(t, t, mv[:, n, 0:1], rstd[:, n:n + 1], ALU.subtract, ALU.mult)
            ins.then_inc(xn_set, 1)

            def mod_group(g, s):
                dve.wait_ge(wm_used, g + 1)
                dve.tensor_copy(modrow[:, bass.ts(g, 256)], pb[s][0:2, 0:256]).then_inc(mod_set, 1)

            with dve.Fori(0, MG1 // 2) as i:
                mod_group(2 * i, 0)
                mod_group(2 * i + 1, 1)
            dve.wait_ge(row_turned, 1)
            ch.link(dve.tensor_tensor(modT[:, 0:MU, :], pb[6][:, 0:2 * MU].rearrange("p (n w) -> p n w", w=2),
                                      bmodT[:, 0:MU].unsqueeze(2).to_broadcast([P, MU, 2]), ALU.add))
            dve.tensor_scalar(modT[:, M_SC1:M_SC1 + DC, :], modT[:, M_SC1:M_SC1 + DC, :], 1.0, None,
                              ALU.add).then_inc(one_plus, 1)
            for c in range(DC):
                s = c % 2
                dve.wait_ge(h_hi, c + 1)
                dve.tensor_tensor(hxl[:, c, :], affx[s][:, :], hxh[:, c, :].bitcast(fp32), ALU.subtract)
                dve.tensor_tensor(hcl[:, c, :], affc[s][:, :], hch[:, c, :].bitcast(fp32),
                                  ALU.subtract).then_inc(h_split, 1)

            def w_split(b, s, n=DC):
                dve.wait_ge(w_hi, b + 1)
                dve.tensor_tensor(wl[s][:, 0:n, :], wraw[s][:, 0:n, :], wh[s][:, 0:n, :].bitcast(fp32),
                                  ALU.subtract).then_inc(w_lo, 1)

            def square(k):
                dve.wait_ge(w_out_, k + 1 if k < 4 else k + 2)
                if k >= 2:
                    dve.wait_ge(sq_used, k - 1)
                x = ckv[:, k, :] if k < 4 else cq[:, k - 4, :]
                w = NKEY if k < 4 else T
                dve.tensor_tensor(sq[k % 2][:, 0:w], x, x, ALU.mult).then_inc(sq_set, 1)

            def mean_square(which, nb):
                dve.wait_ge(ssq_done, which + 1)
                if which == 1:
                    dve.wait_ge(bc_done, 1)
                dve.tensor_scalar(vare[:, 0:nb], pb[4 + which][:, 0:2 * nb:2], 1.0 / LORA, EPS,
                                  ALU.mult, ALU.add).then_inc(var_set, 1)
                dve.wait_ge(rstd_set, 2 + which)
                dve.tensor_tensor(diag[:, 0:nb * P].rearrange("p (b t) -> p b t", b=nb),
                                  ident[:, :].unsqueeze(1).to_broadcast([P, nb, P]),
                                  rstd[:, 0:nb].unsqueeze(2).to_broadcast([P, nb, P]),
                                  ALU.mult).then_inc(dg_set, 1)

            def rms_ckv():
                dve.wait_ge(bc_done, 1)
                for k in range(LC):
                    g = vecT[:, V_KVG + k:V_KVG + k + 1]
                    dve.scalar_tensor_tensor(out=ckv[:, k, 0:T], in0=ckv[:, k, 0:T], scalar=g,
                                             in1=pb[6][:, :], op0=ALU.mult, op1=ALU.mult)
                    dve.scalar_tensor_tensor(out=ckv[:, k, T:NKEY], in0=ckv[:, k, T:NKEY], scalar=g,
                                             in1=pb[7][:, 0:TC], op0=ALU.mult, op1=ALU.mult).then_inc(lora_scaled, 1)
                for k in range(LC):
                    dve.wait_ge(lora_hi, k + 1)
                    dve.tensor_tensor(ckvl[:, k, :], ckv[:, k, :], ckvh[:, k, :].bitcast(fp32),
                                      ALU.subtract).then_inc(lora_split, 1)

            def rms_cq():
                dve.wait_ge(bc_done, 2)
                for k in range(LC):
                    dve.scalar_tensor_tensor(out=cq[:, k, :], in0=cq[:, k, :], scalar=vecT[:, V_QG + k:V_QG + k + 1],
                                             in1=pb[6][:, :], op0=ALU.mult, op1=ALU.mult).then_inc(lora_scaled, 1)
                dve.wait_ge(lora_split, LC)
                for k in range(LC):
                    dve.wait_ge(lora_hi, LC + k + 1)
                    dve.tensor_tensor(cql[:, k, :], cq[:, k, :], cqh[:, k, :].bitcast(fp32),
                                      ALU.subtract).then_inc(lora_split, 1)

            w_split(0, 0)
            for b in range(11):
                w_split(b + 1, (b + 1) % 2)
                if b < 4:
                    square(b)
                elif b == 4:
                    dve.wait_ge(kr_hi, 1)
                    dve.tensor_tensor(krl[:, :], kr[:, :], krh[:, :].bitcast(fp32), ALU.subtract).then_inc(kr_ready, 1)
                elif b < 9:
                    square(b - 1)
                if b == 5:
                    mean_square(0, KB)
                    dve.wait_ge(cst_in, 16)
                    dve.wait_ge(kr_swapped, 1)
                    dve.tensor_tensor(tmp[:, 0:T], pb[7][:, :], rot[:, 1, :], ALU.mult)
                    ch.link(dve.tensor_tensor(kr[:, 0:T], kr[:, 0:T], rot[:, 0, :], ALU.mult))
                    dve.tensor_tensor(kr[:, 0:T], kr[:, 0:T], tmp[:, 0:T], ALU.add).then_inc(kr_roped, 1)
                if b == 6:
                    dve.wait_ge(kr_hi, 2)
                    dve.tensor_tensor(krl[:, :], kr[:, :], krh[:, :].bitcast(fp32), ALU.subtract).then_inc(kr_split, 1)
                if b == 7:
                    rms_ckv()
                if b == 9:
                    mean_square(1, TB)
                if b == 10:
                    rms_cq()
            with dve.Fori(0, 3) as i:
                for u in range(2):
                    w_split(2 * i + 12 + u, u)

            def mod_reduce(j, s, r):
                dve.wait_ge(mu_prod, j + 1)
                if not isinstance(j, int) or j >= 2:
                    dve.wait_ge(mu_sum, j - 1)
                dve.tensor_reduce(mred[r][:, :], mbuf[s][:, :, :].rearrange("p c n -> p n c"), AX.X,
                                  ALU.add).then_inc(mu_red, 1)

            def mod_finish(j0, n, bank):
                dve.wait_ge(mu_sum, j0 + n)
                dve.tensor_tensor(modT[:, MU + j0:MU + j0 + n, 0], pb[bank][:, 0:2 * n:2],
                                  bmodT[:, MU + j0:MU + j0 + n], ALU.add).then_inc(mu_set, 1)

            w_split(18, 0)
            mod_reduce(0, 0, 0)
            w_split(19, 1)
            mod_reduce(1, 1, 1)
            with dve.Fori(1, 15) as i:
                for u in range(2):
                    w_split(2 * i + 18 + u, u)
                    mod_reduce(2 * i + u, u, u)
            w_split(48, 0)
            mod_reduce(30, 0, 0)
            mod_reduce(31, 1, 1)
            mod_finish(0, 2 * DC, 4)

            def pair_split(p, which):
                dve.wait_ge(pw_hi, 2 * p + which + 1)
                if which == 0:
                    for src, c0, c1 in q_parts:
                        ins = dve.tensor_tensor(pql[:, :, c0:c1].rearrange("p c (h n) -> p c h n", h=2), src,
                                                pqh[:, :, c0:c1].rearrange("p c (h n) -> p c h n", h=2).bitcast(fp32),
                                                ALU.subtract)
                    ins.then_inc(pw_lo, 1)
                else:
                    dve.tensor_tensor(pkl[:, :, :], praw_kv[:, :, :], pkh[:, :, :].bitcast(fp32), ALU.subtract).then_inc(pw_lo, 1)

            def tile_lo(p, n, dst, src, hi, more=None):
                dve.wait_ge(pj_hi, 10 * p + n + 1)
                ins = dve.tensor_tensor(dst, src, hi.bitcast(fp32), ALU.subtract)
                if more is not None:
                    ins = more()
                ins.then_inc(pj_lo, 1)

            def attention_pair(p, last=False):
                B = (pb[4], pb[5])
                tile_lo(p, 0, qrl[:, :], B[0][:, :], qrh[:, :],
                        lambda: dve.tensor_tensor(rt[0][:, :], B[0][:, :], rot[:, 0, :], ALU.mult))
                for h in range(2):
                    tile_lo(p, 1 + h, ql[:, h, :], B[(1 + h) % 2][:, :], qh[:, h, :])
                dve.wait_ge(pj_done, 10 * p + 4)
                dve.tensor_tensor(rt[1][:, :], B[1][:, :], rot[:, 1, :], ALU.mult).then_inc(rope_mid, 1)
                dve.wait_ge(rope_mid, p + 1)
                dve.tensor_tensor(rt[0][:, :], rt[0][:, :], rt[1][:, :], ALU.add).then_inc(rope_set, 1)
                tile_lo(p, 3, qrl[:, :], rt[0][:, :], qrh[:, :])
                for h in range(2):
                    tile_lo(p, 4 + h, kTl[:, h, 0:T], B[h][:, :], kTh[:, h, 0:T])
                tile_lo(p, 6, kTl[:, :, T:NKEY], B[0][:, :].rearrange("p (h t) -> p h t", h=2), kTh[:, :, T:NKEY])
                for v in range(3):
                    tile_lo(p, 7 + v, vl[:, 2 * v:2 * v + 2, :, :],
                            B[(7 + v) % 2][:, :].rearrange("p (b h d) -> p b h d", b=2, h=2),
                            vh[:, 2 * v:2 * v + 2, :, :])

                def row_max(n):
                    dve.wait_ge(s_done, 8 * p + n + 1)
                    dve.reduce_max(rmx[:, n:n + 1], pp[n % 2][:, 0:NKEY], AX.X).then_inc(mx_set, 1)
                    dve.wait_ge(mx_set, 8 * p + n + 1)
                    dve.tensor_scalar(nmx[:, n:n + 1], rmx[:, n:n + 1], -SS, None, ALU.mult).then_inc(nmx_set, 1)

                def normalise(n):
                    dve.wait_ge(exp_done, 8 * p + n + 1)
                    dve.reciprocal(rinv[:, n:n + 1], rsum[:, n:n + 1]).then_inc(inv_set, 1)
                    dve.wait_ge(inv_set, 8 * p + n + 1)
                    dve.tensor_scalar(prob[n % 2][:, :], prob[n % 2][:, :], rinv[:, n:n + 1], None,
                                      ALU.mult).then_inc(prob_set, 1)

                def turned_lo(n):
                    dve.wait_ge(pT_hi, 8 * p + n + 1)
                    t = slice(P * (n % 4), P * (n % 4) + P)
                    dve.tensor_tensor(pTl[:, :, t], pp[3][:, 0:NKEY].rearrange("p (k t) -> p k t", k=KB),
                                      pTh[:, :, t].bitcast(fp32), ALU.subtract).then_inc(pT_lo, 1)

                for n in range(10):
                    if n < 8:
                        row_max(n)
                    if 1 <= n <= 8:
                        normalise(n - 1)
                    if n >= 2:
                        turned_lo(n - 2)
                    if n in (3, 4) and not last:
                        pair_split(p + 1, n - 3)

            pair_split(0, 0)
            pair_split(0, 1)
            dve.wait_ge(kr_split, 1)
            for ss in st_done:
                dve.wait_ge(ss, 16 * ((NPX - FIRST_ST) // 2))
            attention_pair(0)
            with dve.Fori(1, HEADS // 2 - 1) as p:
                attention_pair(p)
            attention_pair(HEADS // 2 - 1, True)

            def lo(dst, src, hi):
                return dve.tensor_tensor(dst, src, hi.bitcast(fp32), ALU.subtract)

            dve.wait_ge(dft_hi, 1)
            for w in range(2):
                lo(dtl[:, w, :, :], dtraw[:, w, :, :], dth[:, w, :, :])
            lo(dcl[:, :, :, :], dcraw[:, :, :, :], dch[:, :, :, :]).then_inc(dft_split, 1)
            with dve.Fori(0, FG) as g:
                for cb in range(2):
                    dve.wait_ge(f_hi, 2 * g + cb + 1)
                    lo(fl[:, :, P * cb:P * cb + P], pb[cb][:, :].rearrange("p (b c) -> p b c", b=TB),
                       fh[:, :, P * cb:P * cb + P]).then_inc(f_lo, 1)
                for n in range(4):
                    dve.wait_ge(g_hi, 4 * g + n + 1)
                    lo(gl[:, n % 2, n // 2, :], pb[2 + n][:, :], gh[:, n % 2, n // 2, :]).then_inc(g_lo, 1)
                for k in range(2):
                    dve.wait_ge(y_hi, 2 * g + k + 1)
                    lo(yl[:, bass.ds(2 * g + k, 1), :].rearrange("p a t -> p (a t)"), pb[6 + k][:, :],
                       yh[:, bass.ds(2 * g + k, 1), :].rearrange("p a t -> p (a t)")).then_inc(y_lo, 1)

            NM, NO = NPX + 2 * DC, NPX + 3 * DC
            w_split(NPX, 1)
            w_split(NPX + 1, 0, FD // P)
            dve.wait_ge(o_hi, 4)
            dve.wait_ge(y_done, FD // P)
            for c in range(4):
                lo(ol[:, 4 * c:4 * c + 4, :], oT[:, 4 * c:4 * c + 4, :], oh[:, 4 * c:4 * c + 4, :]).then_inc(o_lo, 1)
            dve.wait_ge(o_lo, 4)

            def merge(m, s, last=False):
                mod_reduce(m + 32, 2, s)
                dve.wait_ge(w_lo, 2 * m + NPX + 2)
                dve.wait_ge(gate_in[s], 16 * (m - s) + 32)
                dve.wait_ge(w_used, 2 * m + NPX + 1)
                dve.tensor_tensor(mt[0][:, :], pb[1][:, :], gate[s][:, 0, :], ALU.mult).then_inc(w_out_, 1)
                w_split(2 * m + NPX + 2, 1)
                dve.wait_ge(w_used, 2 * m + NPX + 2)
                dve.tensor_tensor(mt[1][:, :], pb[0][:, :], gate[s][:, 1, :], ALU.mult).then_inc(w_out_, 1)
                dve.wait_ge(w_out_, 2 * m + NPX + 2)
                dve.tensor_tensor(merged[:, bass.ds(m, 1), :].rearrange("p a t -> p (a t)"), mt[0][:, :], mt[1][:, :],
                                  ALU.add).then_inc(merged_set, 1)
                if not last:
                    w_split(2 * m + NPX + 3, 0, FD // P)

            with dve.Fori(0, DC // 2 - 1) as i:
                merge(2 * i, 0)
                merge(2 * i + 1, 1)
            merge(DC - 2, 0)
            merge(DC - 1, 1, last=True)
            mod_finish(2 * DC, DC, 6)
            dve.wait_ge(mu_set, 2)
            dve.tensor_scalar(modT[:, M_SC2:M_SC2 + DC, 0], modT[:, M_SC2:M_SC2 + DC, 0], 1.0, None,
                              ALU.add).then_inc(mu_set, 1)
            for c in range(4):
                dve.wait_ge(m_hi, c + 1)
                for k in range(4):
                    lo(ml[:, 4 * c + k, :], merged[:, 4 * c + k, :], mh[:, 4 * c + k, :]).then_inc(m_lo, 1)

            def residual(n, y):
                dve.wait_ge(y_turned, n + 1)
                xs = xres[:, :, bass.ts(n, P)]
                dve.scalar_tensor_tensor(out=xs, in0=xs, scalar=ALPHA,
                                         in1=pb[2 + y][:, :].rearrange("p (b d) -> p b d", b=TB),
                                         op0=ALU.mult, op1=ALU.add).then_inc(y_added, 1)

            w_split(NM + 1, 0)
            dve.wait_ge(res_in, 16)
            with dve.Fori(0, DC // 2 - 1) as i:
                w_split(2 * i + NM + 2, 1)
                residual(2 * i, 0)
                w_split(2 * i + NM + 3, 0)
                residual(2 * i + 1, 1)
            residual(DC - 2, 0)
            residual(DC - 1, 1)

            def variance(k, t):
                for q in range(4):
                    ins = dve.bn_stats(stats[:, k, q, :], t[:, 512 * q:512 * q + 512])
                ch.link(ins)
                ch.link(dve.bn_aggr(mv[:, k, :], stats[:, k, :, :].rearrange("p q s -> p (q s)")))
                dve.tensor_scalar(vare[:, k:k + 1], mv[:, k, 1:2], EPS, None, ALU.add).then_inc(var_set, 1)

            def affine(t, k, g, b, done):
                ch.link(dve.scalar_tensor_tensor(out=t, in0=t, scalar=mv[:, k, 0:1], in1=g[:, :], op0=ALU.subtract,
                                                 op1=ALU.mult))
                dve.scalar_tensor_tensor(out=t, in0=t, scalar=rstd[:, k:k + 1], in1=b[:, :], op0=ALU.mult,
                                         op1=ALU.add).then_inc(done, 1)

            def norm1(b):
                variance(b, xres[:, b, :])

            def norm1_out(b):
                dve.wait_ge(rstd_set, 4 + LN_ORDER.index(b))
                affine(xres[:, b, :], b, ln_g, ln_b, x1_set)
                dve.wait_ge(x1_set, b + 1)
                variance(4 + b, xres[:, b, :])

            def norm2(b):
                k = 4 + b
                dve.wait_ge(rstd_set, 4 + LN_ORDER.index(k))
                dve.tensor_scalar(xn2[:, b, :], xres[:, b, :], mv[:, k, 0:1], rstd[:, k:k + 1], ALU.subtract,
                                  ALU.mult).then_inc(xn2_set, 1)

            dve.wait_ge(y_added, DC)
            dve.wait_ge(ln_in, 32)
            norm1(0)
            norm1(1)
            norm1_out(0)
            norm1(2)
            norm1_out(1)
            norm2(0)
            norm1(3)
            norm1_out(2)
            norm2(1)
            norm1_out(3)
            norm2(2)
            norm2(3)
            for c in range(DC):
                dve.wait_ge(h2_hi, c + 1)
                lo(h2l[:, c, :], aff2[c % 2][:, :], h2h[:, c, :]).then_inc(h2_split, 1)

            for k in range(4):
                dve.wait_ge(key_hi, k + 1)
                lo(keyl[:, 4 * k:4 * k + 4, :], pb[4 + k][:, :].rearrange("p (n k) -> p n k", n=4),
                   keyh[:, 4 * k:4 * k + 4, :]).then_inc(key_lo, 1)

            def q_split(b, s):
                dve.wait_ge(w_hi, b + 1)
                lo(w2l[s][:, :, :], w2raw[s][:, :, :], w2h[s][:, :, :]).then_inc(w_lo, 1)

            def q_block(n, s):
                dve.wait_ge(pq_hi, n + 1)
                lo(pq[1][s][:, :], pb[s][:, :], pq[0][s][:, :]).then_inc(w_out_, 1)

            q_split(NO, 1)
            q_split(NO + 1, 0)
            q_block(0, 1)
            mod_reduce(48, 3, 0)
            with dve.Fori(0, DC // 2 - 1) as i:
                q_split(2 * i + NO + 2, 1)
                q_block(2 * i + 1, 0)
                mod_reduce(2 * i + 49, 4, 1)
                q_split(2 * i + NO + 3, 0)
                q_block(2 * i + 2, 1)
                mod_reduce(2 * i + 50, 3, 0)
            q_block(15, 0)
            mod_reduce(63, 4, 1)
            mod_finish(3 * DC, DC, 6)

            G2 = 2 * PH

            def top16(vals, spare, best_v, best_i, n, tk):
                dve.memset(wait_pad[:, :], 0.0)
                for g in range(n):
                    ins = dve.max(best_v[:, g, 0:8], vals[:, g, :])
                tk.link(ins)
                dve.memset(wait_pad[:, :], 0.0)
                for g in range(n):
                    dve.max_index(best_i[:, g, 0:8], best_v[:, g, 0:8], vals[:, g, :])
                    ins = dve.match_replace(spare[:, g, :], best_v[:, g, 0:8], vals[:, g, :], -3.0e38)
                tk.link(ins)
                dve.memset(wait_pad[:, :], 0.0)
                for g in range(n):
                    ins = dve.max(best_v[:, g, 8:16], spare[:, g, :])
                tk.link(ins)
                dve.memset(wait_pad[:, :], 0.0)
                for g in range(n):
                    ins = dve.max_index(best_i[:, g, 8:16], best_v[:, g, 8:16], spare[:, g, :])
                tk.link(ins)
                dve.memset(wait_pad[:, :], 0.0)

            dve.wait_ge(sc_set, G2)
            dve.wait_ge(iota_in, 16)
            LINKS = 21
            with dve.Fori(0, TB) as b:
                tk = Tally(dve, tk_chain)
                tk.at = b * LINKS
                tk.link(dve.tensor_copy(sc1[:, :, :], score[:, bass.ds(b, 1), :, :].rearrange("p a g k -> p (a g) k")))
                top16(sc1, sc2, top, topi, G2, tk)
                dve.tensor_copy(topf[:, :, :], topi[:, :, :])
                tv = top[:, :, :].rearrange("p (h w) k -> p w h k", w=2)
                tk.link(dve.tensor_tensor(cand[:, :, :].rearrange("p h (a b) -> p h a b", a=TOPK),
                                          tv[:, 0].unsqueeze(3).to_broadcast([P, PH, TOPK, TOPK]),
                                          tv[:, 1].unsqueeze(2).to_broadcast([P, PH, TOPK, TOPK]), ALU.add))
                top16(cand, cand2, best, besti, PH, tk)
                dve.tensor_scalar(bpos[:, 0, :, :], besti[:, :, :], 4, None, ALU.logical_shift_right)
                tk.link(dve.tensor_scalar(bpos[:, 1, :, :], besti[:, :, :], 15, None, ALU.bitwise_and))
                dve.tensor_copy(smalls[:, 0, :], best[:, :, 0])
                tk.link(dve.tensor_copy(bposf[:, :, :, :], bpos[:, :, :, :]))
                dve.tensor_tensor(best[:, :, :], best[:, :, :], smalls[:, 0, :].unsqueeze(2).to_broadcast([P, PH, TOPK]),
                                  ALU.subtract).then_inc(tk_diff, 1)
                for w in range(2):
                    tk.link(dve.tensor_tensor(
                        pick[:, :, :], bposf[:, w, :, :].rearrange("p h k -> p (h k)").unsqueeze(2).to_broadcast([P, PH * TOPK, TOPK]),
                        iota[:, 0:TOPK].unsqueeze(1).to_broadcast([P, PH * TOPK, TOPK]), ALU.is_equal))
                    pv = pick[:, :, :].rearrange("p (h k) m -> p h k m", h=PH)
                    tf = topf[:, :, :].rearrange("p (h w) k -> p w h k", w=2)
                    tk.link(dve.tensor_tensor(pv, pv, tf[:, w].unsqueeze(2).to_broadcast([P, PH, TOPK, TOPK]), ALU.mult))
                    tk.link(dve.tensor_reduce(chosen[:, w, :], pick[:, :, :], AX.X, ALU.add))
                dve.wait_ge(tk_exp, b + 1)
                tk.link(dve.tensor_reduce(smalls[:, 1, :], best[:, :, :], AX.X, ALU.add))
                tk.link(dve.reciprocal(smalls[:, 2, :], smalls[:, 1, :]))
                tk.link(dve.tensor_tensor(chosen[:, 2, :].rearrange("p (h k) -> p h k", h=PH), best[:, :, :],
                                          smalls[:, 2, :].unsqueeze(2).to_broadcast([P, PH, TOPK]), ALU.mult))
                dve.sem_inc(tk_chosen, 1)
                dve.wait_ge(ch_turned, b + 1)
                dve.tensor_copy(chT[:, :, bass.ts(b, P)], pb[7][:, 0:3 * P].rearrange("p (w t) -> p w t", w=3)).then_inc(ch_set, 1)
            assert tk.n == LINKS, tk.n
            dve.wait_ge(chw_hi, 1)
            lo(chwl[:, :], chT[:, 2, :], chwh[:, :]).then_inc(chw_set, 1)
            dve.wait_ge(chw_set, 1)

            def one_hots(g, s):
                if not isinstance(g, int) or g >= 2:
                    dve.wait_ge(r_done, g - 1)
                for t in range(4):
                    tok = bass.ds(4 * g + t, 1)
                    dve.tensor_scalar(oneI[s][:, t, :], iota[:, :], chT[:, 0, tok], None, ALU.is_equal)
                    dve.tensor_scalar(oneJh[s][:, t, :], iota[:, :], chT[:, 1, tok], chwh[:, tok].bitcast(fp32),
                                      ALU.is_equal, ALU.mult)
                    ins = dve.tensor_scalar(oneJl[s][:, t, :], iota[:, :], chT[:, 1, tok], chwl[:, tok].bitcast(fp32),
                                            ALU.is_equal, ALU.mult)
                ins.then_inc(one_set, 1)

            one_hots(0, 0)
            one_hots(1, 1)
            with dve.Fori(1, T // 8) as i:
                one_hots(2 * i, 0)
                one_hots(2 * i + 1, 1)

            def expert_u(i, k):
                dve.wait_ge(u_hi, 2 * i + k + 1)
                lo(uTl[:, 8 * k:8 * k + 8, :], pp[k][:, :].rearrange("p (c j) -> p c j", c=8),
                   uTh[:, 8 * k:8 * k + 8, :]).then_inc(u_lo, 1)

            def expert_coef(i, u):
                dve.wait_ge(gelu_set, i + 1)
                dve.wait_ge(wt_in[u], 8 * (i - u) + 16)
                dve.tensor_tensor(act_g[:, :], act_g[:, :], wt[u][:, :], ALU.mult).then_inc(co_set, 1)

            def expert_coef_lo(i, slot):
                dve.wait_ge(co_hi, i + 1)
                lo(col[slot][:, :], act_g[:, :], coh[slot][:, :]).then_inc(co_lo, 1)

            def expert_v(i, u):
                dve.wait_ge(v_hi, i + 1)
                lo(v2l[:, u, :], vraw[u][:, :], v2h[:, u, :]).then_inc(v_lo, 1)

            def add_tiles(g, n0, n1):
                for n in range(n0, n1):
                    dve.wait_ge(e_done, 16 * g + n + 1)
                    t = acc[:, n // 4, 512 * (n % 4):512 * (n % 4) + 512]
                    dve.tensor_tensor(t, t, pb[5 + n % 3][:, :], ALU.add).then_inc(e_added, 1)

            def expert_group(g, par, first=False, last=False):
                if not first:
                    expert_v(2 * g - 2, 0)
                    expert_v(2 * g - 1, 1)
                for u in range(2):
                    n = 8 * u
                    expert_coef(2 * g + u, u)
                    if not first:
                        add_tiles(g - 1, n, n + 2)
                    if not (last and u == 1):
                        expert_u(2 * g + u + 1, 0)
                    if not first:
                        add_tiles(g - 1, n + 2, n + 3)
                    if not (last and u == 1):
                        expert_u(2 * g + u + 1, 1)
                    if not first:
                        add_tiles(g - 1, n + 3, n + 5)
                    expert_coef_lo(2 * g + u, 2 * par + u)
                    if not first:
                        add_tiles(g - 1, n + 5, n + 8)

            dve.wait_ge(r_stored[1], 16 * (T // RT // 2) + 16)
            dve.memset(acc[:, :, :], 0.0)
            expert_u(0, 0)
            expert_u(0, 1)
            expert_group(0, 0, first=True)
            expert_group(1, 1)
            with dve.Fori(1, NK // 4 - 1) as i:
                expert_group(2 * i, 0)
                expert_group(2 * i + 1, 1)
            expert_group(NK // 2 - 2, 0)
            expert_group(NK // 2 - 1, 1, last=True)
            expert_v(NK - 2, 0)
            expert_v(NK - 1, 1)
            dve.wait_ge(v_lo, NK)
            for k in range(4):
                if k >= 1:
                    dve.wait_ge(g2_done, k)
                dve.tensor_tensor(diag2[:, :, :], ident[:, :].unsqueeze(1).to_broadcast([P, 4, P]),
                                  modT[:, M_G2 + 4 * k:M_G2 + 4 * k + 4, 0:1].to_broadcast([P, 4, P]),
                                  ALU.mult).then_inc(g2_diag, 1)
            dve.wait_ge(fin_in, 48)

            def last_sum(b):
                add_tiles(NK // 2 - 1, 4 * b, 4 * b + 4)
                t = acc[:, b, :]
                dve.wait_ge(e_added, 16 * (NK // 2 - 1) + 4 * b + 4)
                dve.wait_ge(g2_copied, 4)
                ch.link(dve.tensor_tensor(t, t, g2row[:, :], ALU.mult))
                ch.link(dve.scalar_tensor_tensor(out=t, in0=xfin[:, b, :], scalar=ALPHA, in1=t, op0=ALU.mult,
                                                 op1=ALU.add))
                variance(b, t)

            def last_norm(b):
                dve.wait_ge(rstd_set, 12 + b)
                affine(acc[:, b, :], b, ln2_g, ln2_b, fin_set)

            last_sum(0)
            for b in range(1, TB):
                last_sum(b)
                last_norm(b - 1)
            last_norm(TB - 1)

        @block.tensor
        def _(pe):
            pe.wait_ge(vec_in, 176)
            pe.transpose(pb[4][:, 0:V_ROWS], vrows[0:V_ROWS, :], ident[0:V_ROWS, 0:V_ROWS])
            pe.transpose(pb[5][:, 0:96], mrows[0:96, :], ident[0:96, 0:96]).then_inc(vec_turned, 1)
            pe.wait_ge(silu_set, 1)

            def mod_group(g, s, i):
                pe.wait_ge(wm_in[s], 16 * i + 16)
                if not isinstance(g, int) or g >= 2:
                    pe.wait_ge(mod_set, g - 1)
                for c in range(DC):
                    mm = pe.matmul(pb[s][0:2, 0:256], silu[:, c, :], wm[s][:, c, :], start=c == 0, stop=c == DC - 1)
                mm.then_inc(wm_used, 1)

            mod_group(0, 0, 0)
            mod_group(1, 1, 0)
            with pe.Fori(1, MG1 // 2) as i:
                mod_group(2 * i, 0, i)
                mod_group(2 * i + 1, 1, i)
            pe.wait_ge(mod_set, MG1)
            for n in range(MU):
                mm = pe.transpose(pb[6][:, 2 * n:2 * n + 2], modrow[:, P * n:P * n + P], ident[0:2, 0:2])
            mm.then_inc(row_turned, 1)
            pe.wait_ge(one_plus, 1)
            pe.wait_ge(xn_set, 1)
            for c in range(DC):
                s = c % 2
                if c >= 2:
                    pe.wait_ge(act_chain, c - 1)
                for b in range(TB):
                    pe.transpose(pb[s][:, P * b:P * b + P], xtok[:, b, P * c:P * c + P], ident[:, :])
                for b in range(CB):
                    mm = pe.transpose(pb[2 + s][:, P * b:P * b + P], ctok[:, b, P * c:P * c + P], ident[:, :])
                mm.then_inc(h_turned, 1)

            def px_block(b, s, context=False):
                pe.wait_ge(w_lo, b + 1)
                if not isinstance(b, int) or b >= 2:
                    pe.wait_ge(w_out_, b - 1)
                for c in range(DC):
                    mm = mm3(pe, pb[s][:, :], wh[s][:, c, :], wl[s][:, c, :], hxh[:, c, :], hxl[:, c, :],
                             c == 0, c == DC - 1)
                if context:
                    for c in range(DC):
                        mm = mm3(pe, pb[2 + s][:, 0:TC], wh[s][:, c, :], wl[s][:, c, :], hch[:, c, :],
                                 hcl[:, c, :], c == 0, c == DC - 1)
                mm.then_inc(w_used, 1)

            def sum_squares(k):
                w, q = k // LC, k % LC
                pe.wait_ge(sq_set, k + 1)
                for b in range(TB if w else KB):
                    mm = pe.matmul(pb[4 + w][:, 2 * b:2 * b + 2], sq[k % 2][:, P * b:P * b + P], ones[:, 0:2],
                                   start=q == 0 and b == 0, stop=q == LC - 1, skip_group_check=True)
                mm.then_inc(sq_used, 1)
                if q == LC - 1:
                    pe.wait_ge(sq_used, k + 1)
                    pe.sem_inc(ssq_done, 1)

            pe.wait_ge(act_chain, DC)
            pe.wait_ge(h_split, DC)
            pe.wait_ge(ones_set, 1)
            for b in range(11):
                px_block(b, b % 2, b < 5)
                if 1 <= b <= 4:
                    sum_squares(b - 1)
                if b == 5:
                    pe.wait_ge(swap_set, 1)
                    pe.wait_ge(kr_ready, 1)
                    pe.matmul(pb[7][:, :], swap[:, :], krh[:, 0:T], start=True, stop=False)
                    pe.matmul(pb[7][:, :], swap[:, :], krl[:, 0:T], start=False, stop=True).then_inc(kr_swapped, 1)
                if b == 6:
                    pe.wait_ge(dg_set, 1)
                    pe.wait_ge(kr_roped, 1)
                    pe.matmul(pb[6][:, :], ones[:, :], diag[:, 0:T], start=True, stop=True)
                    pe.matmul(pb[7][:, 0:TC], ones[:, :], diag[:, T:NKEY], start=True, stop=True).then_inc(bc_done, 1)
                if 6 <= b <= 9:
                    sum_squares(b - 2)
                if b == 10:
                    pe.wait_ge(dg_set, 2)
                    pe.wait_ge(lora_scaled, LC)
                    pe.matmul(pb[6][:, :], ones[:, :], diag[:, 0:T], start=True, stop=True).then_inc(bc_done, 1)
            with pe.Fori(0, 3) as i:
                px_block(2 * i + 11, 1)
                px_block(2 * i + 12, 0)

            def mod_sum(j, r, bank, at):
                pe.wait_ge(mu_red, j + 1)
                pe.matmul(pb[bank][:, bass.ds(at, 2)], mred[r][:, :], ones[:, 0:2], start=True, stop=True).then_inc(mu_sum, 1)

            with pe.Fori(0, 16) as i:
                px_block(2 * i + 17, 1)
                mod_sum(2 * i, 0, 4, 4 * i)
                px_block(2 * i + 18, 0)
                mod_sum(2 * i + 1, 1, 4, 4 * i + 2)

            def tile(p, n, width, parts, out_):
                if n >= 2:
                    pe.wait_ge(pj_lo, 10 * p + n - 1)
                for c in range(LC):
                    mm = mm3(pe, out_, *parts(c), c == 0, c == LC - 1)
                return mm

            def attention_pair(p):
                B = (pb[4], pb[5])
                pe.wait_ge(pw_lo, 2 * p + 1)
                if not isinstance(p, int) or p > 0:
                    pe.wait_ge(o_set, 2 * p)
                tile(p, 0, T, lambda c: (pqh[:, c, 2 * NOPE:], pql[:, c, 2 * NOPE:], cqh[:, c, :], cql[:, c, :]),
                     B[0][:, :]).then_inc(pj_done, 1)
                for h in range(2):
                    cols = slice(NOPE * h, NOPE * h + NOPE)
                    tile(p, 1 + h, T, lambda c: (pqh[:, c, cols], pql[:, c, cols], cqh[:, c, :], cql[:, c, :]),
                         B[(1 + h) % 2][:, :]).then_inc(pj_done, 1)
                pe.wait_ge(pj_lo, 10 * p + 2)
                pe.matmul(B[1][:, :], swap[:, :], qrh[:, :], start=True, stop=False)
                pe.matmul(B[1][:, :], swap[:, :], qrl[:, :], start=False, stop=True).then_inc(pj_done, 1)
                pe.wait_ge(pw_lo, 2 * p + 2)
                for h in range(2):
                    cols = slice(256 * h, 256 * h + NOPE)
                    tile(p, 4 + h, T, lambda c: (pkh[:, c, cols], pkl[:, c, cols], ckvh[:, c, 0:T], ckvl[:, c, 0:T]),
                         B[h][:, :]).then_inc(pj_done, 1)
                for h in range(2):
                    cols = slice(256 * h, 256 * h + NOPE)
                    mm = tile(p, 6, TC, lambda c: (pkh[:, c, cols], pkl[:, c, cols], ckvh[:, c, T:NKEY], ckvl[:, c, T:NKEY]),
                              B[0][:, TC * h:TC * h + TC])
                mm.then_inc(pj_done, 1)
                for v in range(3):
                    for k in range(2):
                        ks = slice(P * (2 * v + k), P * (2 * v + k) + P)
                        vv = lambda t, c: t[:, c, :].rearrange("p (h n) -> p h n", h=2)[:, :, NOPE:NOPE + VD]
                        if k == 0:
                            pe.wait_ge(pj_lo, 10 * p + 6 + v)
                        for c in range(LC):
                            o = B[(7 + v) % 2][:, 256 * k:256 * k + 256]
                            pe.matmul(o, ckvh[:, c, ks], vv(pkh, c), start=c == 0, stop=False)
                            pe.matmul(o, ckvh[:, c, ks], vv(pkl, c), start=False, stop=False)
                            mm = pe.matmul(o, ckvl[:, c, ks], vv(pkh, c), start=False, stop=c == LC - 1)
                    mm.then_inc(pj_done, 1)

                def scores(n):
                    h, b = n // 4, n % 4
                    if n >= 2 or not isinstance(p, int) or p > 0:
                        pe.wait_ge(exp_done, 8 * p + n - 1)
                    t = slice(P * b, P * b + P)
                    r = slice(ROPE * h, ROPE * h + ROPE)
                    for k0, k1 in ((0, T), (T, NKEY)):
                        o = pp[n % 2][:, k0:k1]
                        mm3(pe, o, qh[:, h, t], ql[:, h, t], kTh[:, h, k0:k1], kTl[:, h, k0:k1], True, False)
                        mm = mm3(pe, o, qrh[r, t], qrl[r, t], krh[r, k0:k1], krl[r, k0:k1], False, True)
                    mm.then_inc(s_done, 1)

                def turn(n):
                    pe.wait_ge(prob_set, 8 * p + n + 1)
                    if n >= 1 or not isinstance(p, int) or p > 0:
                        pe.wait_ge(pT_lo, 8 * p + n)
                    for k in range(KB):
                        mm = pe.transpose(pp[3][:, P * k:P * k + P], prob[n % 2][:, P * k:P * k + P], ident[:, :])
                    mm.then_inc(p_turned, 1)

                def values(h):
                    pe.wait_ge(pT_lo, 8 * p + 4 * h + 4)
                    for k in range(KB):
                        mm = mm3(pe, pb[4 + h][:, :], vh[:, k, h, :], vl[:, k, h, :], pTh[:, k, :], pTl[:, k, :],
                                 k == 0, k == KB - 1)
                    mm.then_inc(pv_done, 1)

                pe.wait_ge(pj_lo, 10 * p + 10)
                scores(0)
                for n in range(1, 8):
                    scores(n)
                    if n == 5:
                        values(0)
                    turn(n - 1)
                turn(7)
                values(1)

            attention_pair(0)
            with pe.Fori(1, HEADS // 2) as p:
                attention_pair(p)

            pe.wait_ge(dft_split, 1)
            pe.wait_ge(o_set, HEADS)
            pe.wait_ge(exp_done, 8 * (HEADS // 2))
            pe.wait_ge(pT_lo, 8 * (HEADS // 2))

            def fourier_group(g):
                pe.wait_ge(f_in, 16 * g + 16)
                for cb in range(2):
                    if not isinstance(g, int) or g > 0:
                        pe.wait_ge(f_lo, 2 * g - 1 + cb)
                    for b in range(TB):
                        mm = pe.transpose(pb[cb][:, P * b:P * b + P], fT[:, cb, P * b:P * b + P], ident[:, :])
                    mm.then_inc(f_turned, 1)
                for n in range(4):
                    w, cb = n % 2, n // 2
                    if w == 0:
                        pe.wait_ge(f_lo, 2 * g + cb + 1)
                    if not isinstance(g, int) or g > 0:
                        pe.wait_ge(g_lo, 4 * g - 3 + n)
                    for b in range(TB):
                        cs = slice(P * cb, P * cb + P)
                        mm = mm3(pe, pb[2 + n][:, :], fh[:, b, cs], fl[:, b, cs], dth[:, w, b, :], dtl[:, w, b, :],
                                 b == 0, b == TB - 1)
                    mm.then_inc(g_done, 1)
                pe.wait_ge(g_lo, 4 * g + 4)
                for k in range(2):
                    if not isinstance(g, int) or g > 0:
                        pe.wait_ge(y_lo, 2 * g - 1 + k)
                    for n in range(4):
                        w, cb = n % 2, n // 2
                        cs = slice(P * k, P * k + P)
                        mm = mm3(pe, pb[6 + k][:, :], dch[:, w, cb, cs], dcl[:, w, cb, cs], gh[:, w, cb, :],
                                 gl[:, w, cb, :], n == 0, n == 3)
                    mm.then_inc(y_done, 1)

            fourier_group(0)
            with pe.Fori(1, FG) as g:
                fourier_group(g)

            NM, NO = NPX + 2 * DC, NPX + 3 * DC
            pe.wait_ge(y_lo, FD // P)
            pe.wait_ge(f_lo, 2 * FG)
            pe.wait_ge(o_lo, 4)

            def merge(m, s, at):
                pe.wait_ge(w_lo, 2 * m + NPX + 1)
                pe.wait_ge(w_out_, 2 * m + NPX - 1)
                for c in range(DC):
                    mm = mm3(pe, pb[1][:, :], wh[1][:, c, :], wl[1][:, c, :], oh[:, c, :], ol[:, c, :], c == 0, c == DC - 1)
                mm.then_inc(w_used, 1)
                mod_sum(m + 32, s, 6, at)
                pe.wait_ge(w_lo, 2 * m + NPX + 2)
                pe.wait_ge(w_out_, 2 * m + NPX)
                for c in range(FD // P):
                    mm = mm3(pe, pb[0][:, :], wh[0][:, c, :], wl[0][:, c, :], yh[:, c, :], yl[:, c, :], c == 0,
                             c == FD // P - 1)
                mm.then_inc(w_used, 1)

            with pe.Fori(0, DC // 2) as i:
                for u in range(2):
                    merge(2 * i + u, u, 4 * i + 2 * u)

            def out_block(n, s, first=False):
                pe.wait_ge(w_lo, n + NM + 1)
                pe.wait_ge(w_out_, n + NM - 1)
                for c in range(DC):
                    if first:
                        pe.wait_ge(m_lo, c + 1)
                    mm = mm3(pe, pb[s][:, :], wh[s][:, c, :], wl[s][:, c, :], mh[:, c, :], ml[:, c, :], c == 0, c == DC - 1)
                mm.then_inc(w_used, 1)

            def out_turn(n, y):
                pe.wait_ge(w_out_, n + NM + 1)
                if not isinstance(n, int) or n >= 2:
                    pe.wait_ge(y_added, n - 1)
                for b in range(TB):
                    mm = pe.transpose(pb[2 + y][:, P * b:P * b + P], ybuf[y][:, P * b:P * b + P], ident[:, :])
                mm.then_inc(y_turned, 1)

            out_block(0, 1, True)
            out_block(1, 0)
            out_turn(0, 0)
            out_block(2, 1)
            out_turn(1, 1)
            with pe.Fori(1, DC // 2 - 1) as i:
                out_block(2 * i + 1, 0)
                out_turn(2 * i, 0)
                out_block(2 * i + 2, 1)
                out_turn(2 * i + 1, 1)
            out_block(DC - 1, 0)
            out_turn(DC - 2, 0)
            out_turn(DC - 1, 1)

            pe.wait_ge(xn2_set, TB)
            for c in range(DC):
                if c >= 2:
                    pe.wait_ge(h2_affine, c - 1)
                for b in range(TB):
                    mm = pe.transpose(pb[c % 2][:, P * b:P * b + P], xn2[:, b, P * c:P * c + P], ident[:, :])
                mm.then_inc(h2_turned, 1)

            pe.wait_ge(keys_in, 16)
            for k in range(4):
                for n in range(4):
                    mm = pe.transpose(pb[4 + k][:, P * n:P * n + P], keys[:, 4 * k + n, :], ident[:, :])
                mm.then_inc(keys_turned, 1)
            pe.wait_ge(h2_affine, DC)
            pe.wait_ge(h2_split, DC)
            pe.wait_ge(key_lo, 4)

            def q_block(n, s):
                pe.wait_ge(w_lo, n + NO + 1)
                pe.wait_ge(w_out_, n + NO - 1)
                for c in range(DC):
                    mm = mm3(pe, pb[s][:, :], w2h[s][:, c, :], w2l[s][:, c, :], h2h[:, c, :], h2l[:, c, :], c == 0,
                             c == DC - 1)
                mm.then_inc(w_used, 1)

            def key_scores(n, s):
                pe.wait_ge(w_out_, n + NO + 1)
                if not isinstance(n, int) or n >= 2:
                    pe.wait_ge(sc_set, n - 1)
                kk = bass.ds(n, 1)
                for b in range(TB):
                    t = slice(P * b, P * b + P)
                    mm = mm3(pe, pb[2 + s][:, t], pq[0][s][:, t], pq[1][s][:, t],
                             keyh[:, kk, :].rearrange("p a k -> p (a k)"), keyl[:, kk, :].rearrange("p a k -> p (a k)"),
                             True, True)
                mm.then_inc(sc_done, 1)

            q_block(0, 1)
            q_block(1, 0)
            key_scores(0, 1)
            mod_sum(48, 0, 6, 0)
            q_block(2, 1)
            key_scores(1, 0)
            mod_sum(49, 1, 6, 2)
            with pe.Fori(1, DC // 2 - 1) as i:
                q_block(2 * i + 1, 0)
                key_scores(2 * i, 1)
                mod_sum(2 * i + 48, 0, 6, 4 * i)
                q_block(2 * i + 2, 1)
                key_scores(2 * i + 1, 0)
                mod_sum(2 * i + 49, 1, 6, 4 * i + 2)
            q_block(DC - 1, 0)
            key_scores(DC - 2, 1)
            mod_sum(62, 0, 6, 28)
            key_scores(DC - 1, 0)
            mod_sum(63, 1, 6, 30)

            with pe.Fori(0, TB) as b:
                pe.wait_ge(tk_chosen, b + 1)
                pe.wait_ge(key_lo, 4)
                for w in range(3):
                    mm = pe.transpose(pb[7][:, P * w:P * w + P], chosen[:, w, :], ident[:, :])
                mm.then_inc(ch_turned, 1)

            def routing(g, s, k):
                pe.wait_ge(one_set, g + 1)
                if not isinstance(g, int) or g >= 4:
                    pe.wait_ge(r_set, g - 3)
                for t in range(4):
                    o = pb[k][:, P * t:P * t + P]
                    pe.matmul(o, oneJh[s][:, t, :], oneI[s][:, t, :], start=True, stop=False)
                    mm = pe.matmul(o, oneJl[s][:, t, :], oneI[s][:, t, :], start=False, stop=True)
                mm.then_inc(r_done, 1)

            for g in range(4):
                routing(g, g % 2, g)
            with pe.Fori(1, T // 16) as i:
                for q in range(4):
                    routing(4 * i + q, q % 2, q)

            def turn_u(i, s):
                pe.wait_ge(u_in[s], 8 * (i - s) + 16)
                if not isinstance(i, int) or i >= 1:
                    pe.wait_ge(u_lo, 2 * i)
                for c in range(DC):
                    mm = pe.transpose(pb[c // 4][:, P * (c % 4):P * (c % 4) + P], uraw[s][:, P * c:P * c + P], ident[:, :])
                mm.then_inc(u_turned, 1)

            def up(i):
                pe.wait_ge(u_lo, 2 * i + 2)
                if not isinstance(i, int) or i >= 1:
                    pe.wait_ge(gelu_set, i)
                for c in range(DC):
                    mm = mm3(pe, pb[4][:, :], uTh[:, c, :], uTl[:, c, :], h2h[:, c, :], h2l[:, c, :], c == 0,
                             c == DC - 1)
                mm.then_inc(a_done, 1)

            def down(g, par, n0, n1):
                for n in range(n0, n1):
                    if n == 0:
                        pe.wait_ge(co_lo, 2 * g + 2)
                        pe.wait_ge(v_lo, 2 * g + 2)
                    if n >= 3:
                        pe.wait_ge(e_added, 16 * g + n - 2)
                    elif n == 0 and (not isinstance(g, int) or g > 0):
                        pe.wait_ge(e_added, 16 * g)
                    t, d = slice(P * (n // 4), P * (n // 4) + P), slice(512 * (n % 4), 512 * (n % 4) + 512)
                    for u in range(2):
                        mm = mm3(pe, pb[5 + n % 3][:, :], coh[2 * par + u][:, t], col[2 * par + u][:, t],
                                 v2h[:, u, d], v2l[:, u, d], u == 0, u == 1)
                    mm.then_inc(e_done, 1)

            def expert_group(g, par, first=False, last=False):
                for u in range(2):
                    up(2 * g + u)
                    if not (last and u == 1):
                        turn_u(2 * g + u + 1, 1 - u)
                    if not first:
                        down(g - 1, 1 - par, 8 * u, 8 * u + 8)

            pe.wait_ge(r_set, P)
            turn_u(0, 0)
            expert_group(0, 0, first=True)
            expert_group(1, 1)
            with pe.Fori(1, NK // 4 - 1) as i:
                expert_group(2 * i, 0)
                expert_group(2 * i + 1, 1)
            expert_group(NK // 2 - 2, 0)
            expert_group(NK // 2 - 1, 1, last=True)
            for k in range(4):
                pe.wait_ge(g2_diag, k + 1)
                pe.matmul(pb[k][:, :], ones[:, :], diag2[:, :, :].rearrange("p a t -> p (a t)"), start=True,
                          stop=True).then_inc(g2_done, 1)
            down(NK // 2 - 1, 1, 0, 16)


_INS = ['x', 'c', 'ctx', 'c_ctx', 'w_mod', 'b_mod', 'w_in', 'b_in', 'q_norm_g', 'w_uq', 'kv_norm_g', 'w_ukv',
        'w_o_mla', 'w_fourier', 'w_out', 'ln1_g', 'ln1_b', 'peer_wq', 'peer_keys', 'peer_u', 'peer_v',
        'ln2_g', 'ln2_b']


def kernel(**inputs):
    import numpy as _np
    import concourse.bacc as _bacc
    from concourse import mybir as _mybir
    from concourse.bass_utils import run_bass_kernel_spmd as _run

    nc = _bacc.Bacc("TRN2", target_bir_lowering=False, num_devices=1)
    arrays, aps = {}, {}
    tables = constants()
    for name in _INS + list(tables):
        x = _np.ascontiguousarray(inputs[name] if name in inputs else tables[name])
        arrays[f"in_{name}_dram"] = x
        aps[name] = nc.dram_tensor(f"in_{name}_dram", x.shape, _mybir.dt.from_np(x.dtype),
                                   kind="ExternalInput").ap()
    out = nc.dram_tensor("out_0_dram", (1, T, D), _mybir.dt.float32, kind="ExternalOutput").ap()
    layer_kernel(nc, aps, out)
    r = _run(nc, [arrays], core_ids=[0])
    return r.results[0]["out_0_dram"]
```

```python
import concourse.bass as bass
from concourse import mybir
import numpy as np
from contextlib import ExitStack

fp32 = mybir.dt.float32
f32r = mybir.dt.float32r
u32 = mybir.dt.uint32
ALU = mybir.AluOpType
ACT = mybir.ActivationFunctionType
AX = mybir.AxisListType

P = 128
D, T, TC = 2048, 512, 256
DC, TB, CB = D // P, T // P, TC // P
NKEY = T + TC
KB = NKEY // P
HEADS, NOPE, ROPE, VD = 16, 128, 64, 128
LORA = 512
LC = LORA // P
QK = NOPE + ROPE
FD, FG, GD = 1024, 4, 256
PH, NK, TOPK = 8, 128, 16
EPS = 1e-6
ALPHA = 2.0 ** 0.25
GRID_W = 64
C_KR = LORA
C_CQ = LORA + ROPE
C_F = C_CQ + LORA
C_GA = C_F + FD
M_SH1, M_SC1, M_G1, M_SH2, M_SC2, M_G2 = (DC * k for k in range(6))
V_C, V_CC, V_QG, V_KVG, V_BKV, V_BKR, V_BR = 0, 16, 32, 36, 40, 44, 45
V_ROWS = V_BR + 44
PRE_TK = 4
RI = 4
PRE_END = 4
PRE = PRE_TK * TB + T // (4 * RI) + PRE_END
LN_ORDER = (0, 1, 4, 2, 5, 3, 6, 7)


def constants():
    ident = np.eye(P, dtype=np.float32)
    swap = np.zeros((P, P), np.float32)
    for a in range(0, P, 2):
        swap[a + 1, a] = -1.0
        swap[a, a + 1] = 1.0
    half = ROPE // 2
    inv = 10000.0 ** (-np.arange(0, half, 2, dtype=np.float32) / np.float32(half))
    pos = np.arange(T)
    row = (pos // GRID_W).astype(np.float32)
    col = (pos % GRID_W).astype(np.float32)
    ang = np.concatenate([row[:, None] * inv, col[:, None] * inv], -1).astype(np.float32)
    ang = np.repeat(ang.T, 2, axis=0)
    rot = np.stack([np.tile(np.cos(ang), (2, 1)), np.tile(np.sin(ang), (2, 1))], 1).astype(np.float32)
    k = np.arange(T)
    w = 2 * np.pi * ((k[:, None] * k[None]) % T) / T
    dft_t = np.stack([np.cos(w), np.sin(w)]) / np.sqrt(T)
    k = np.arange(GD)
    w = 2 * np.pi * ((k[:, None] * k[None]) % GD) / GD
    dft_c = np.stack([np.cos(w), -np.sin(w)]) / np.sqrt(GD)
    iota = np.tile(np.arange(P, dtype=np.float32), (P, 1))
    return {"k_ident": ident, "k_swap": swap, "k_rot": rot, "k_dft_t": dft_t.astype(np.float32),
            "k_dft_c": dft_c.astype(np.float32), "k_iota": iota}


class Tally:

    def __init__(self, eng, sem):
        self.eng, self.sem, self.at, self.n = eng, sem, 0, 0

    def inc(self, ins):
        ins.then_inc(self.sem, 1)
        self.at, self.n = self.at + 1, self.n + 1

    def link(self, ins):
        self.inc(ins)
        self.eng.wait_ge(self.sem, self.at)


def mm3(pe, out, lh, ll, rh, rl, first, last):
    pe.matmul(out, lh, rh, start=first, stop=False)
    pe.matmul(out, lh, rl, start=False, stop=False)
    return pe.matmul(out, ll, rh, start=False, stop=last)


def layer_kernel(nc, a, out):
    ctx = ExitStack()
    BASE = 16640

    def sb(name, kb, shape, dt=fp32):
        return nc.alloc_sbuf_tensor_at(name, shape, dt, offset=BASE + int(kb * 1024))

    def sem(name):
        return ctx.enter_context(nc.semaphore(name))

    with ctx:
        px_d = nc.dram_tensor("px_scratch", [FD // P + 2 * DC, P, T], fp32, kind="Internal").ap()
        x1_d = nc.dram_tensor("x1_scratch", [T, D], fp32, kind="Internal").ap()
        gelu_d = nc.dram_tensor("gelu_scratch", [PRE, P, T], fp32, kind="Internal").ap()
        route_d = nc.dram_tensor("route_scratch", [NK, NK, T], fp32, kind="Internal").ap()

        ident = sb("ident", 0, [P, P])
        vecT = sb("vecT", 0.5, [P, V_ROWS])
        bmodT = sb("bmodT", 1, [P, 96])
        modT = sb("modT", 1.5, [P, 96, 2])
        ones = sb("ones", 2.25, [P, P])
        swap = sb("swap", 2.75, [P, P], f32r)
        silu = sb("silu", 3.25, [P, DC, 2])
        stats = sb("stats", 3.375, [P, 8, 4, 6])
        mv = sb("mv", 4.125, [P, 8, 2])
        vare = sb("vare", 4.1875, [P, 8])
        rstd = sb("rstd", 4.21875, [P, 8])
        mhalf = sb("mhalf", 4.25, [P, 8])
        rmx = sb("rmx", 4.28125, [P, 8])
        nmx = sb("nmx", 4.3125, [P, 8])
        rsum = sb("rsum", 4.34375, [P, 8])
        rinv = sb("rinv", 4.375, [P, 8])
        silu_t = sb("silu_t", 4.5, [P, 2 * DC])
        xtok = sb("xtok", 8, [P, TB, D])
        ctok = sb("ctok", 40, [P, CB, D])
        wm = [sb(f"wm{s}", 56 + 16 * s, [P, DC, 256]) for s in range(2)]
        hxh, hxl = sb("hxh", 96, [P, DC, T], f32r), sb("hxl", 128, [P, DC, T], f32r)
        hch, hcl = sb("hch", 160, [P, DC, TC], f32r), sb("hcl", 176, [P, DC, TC], f32r)
        affx = [sb(f"affx{s}", 192 + 2 * s, [P, T]) for s in range(2)]
        vrows = sb("vrows", 196, [P, P])
        mrows = sb("mrows", 196.5, [P, P])
        swap_f = sb("swap_f", 197, [P, P])
        modrow = sb("modrow", 96, [2, 32 * P])
        mbuf = [sb(f"mbuf{s}", (64, 72, 88, 96, 88)[s], [P, DC, P]) for s in range(5)]
        mred = [sb(f"mred{s}", 206 + s / 2, [P, P]) for s in range(2)]
        wraw = [sb(f"wraw{s}", 8 + 8 * s, [P, DC, P]) for s in range(2)]
        wh = [sb(f"wh{s}", 24 + 8 * s, [P, DC, P], f32r) for s in range(2)]
        wl = [sb(f"wl{s}", 40 + 8 * s, [P, DC, P], f32r) for s in range(2)]
        ckv = sb("ckv", 56, [P, LC, NKEY])
        kr = sb("kr", 68, [P, NKEY])
        cq = sb("cq", 71, [P, LC, T])
        stg = [sb(f"stg{s}", 85 + 2 * s, [P, T]) for s in range(2)]
        sq = [sb(f"sq{s}", 79 + 3 * s, [P, NKEY]) for s in range(2)]
        rot = sb("rot", 89, [P, 2, T])
        diag = sb("diag", 93, [P, NKEY])
        krh, krl = sb("krh", 192, [P, NKEY], f32r), sb("krl", 195, [P, NKEY], f32r)
        tmp = sb("tmp", 198, [P, NKEY])
        ckvh, ckvl = sb("ckvh", 160, [P, LC, NKEY], f32r), sb("ckvl", 172, [P, LC, NKEY], f32r)
        cqh = sb("cqh", 184, [P, LC, T], f32r)
        cql = sb("cql", 56, [P, LC, T], f32r)
        oT = sb("oT", 96, [P, HEADS, T])
        praw_q = sb("praw_q", 8, [P, LC, 2 * QK])
        praw_kv = sb("praw_kv", 14, [P, LC, 512])
        pqh, pql = sb("pqh", 22, [P, LC, 2 * QK], f32r), sb("pql", 28, [P, LC, 2 * QK], f32r)
        pkh, pkl = sb("pkh", 34, [P, LC, 512], f32r), sb("pkl", 42, [P, LC, 512], f32r)
        qh, ql = sb("qh", 50, [P, 2, T], f32r), sb("ql", 64, [P, 2, T], f32r)
        qrh, qrl = sb("qrh", 54, [P, T], f32r), sb("qrl", 68, [P, T], f32r)
        rt = [sb(f"rt{s}", 70 + 2 * s, [P, T]) for s in range(2)]
        kTh, kTl = sb("kTh", 74, [P, 2, NKEY], f32r), sb("kTl", 80, [P, 2, NKEY], f32r)
        vh, vl = sb("vh", 128, [P, KB, 2, P], f32r), sb("vl", 199, [P, KB, 2, P], f32r)
        prob = [sb("prob0", 86, [P, NKEY]), sb("prob1", 93, [P, NKEY])]
        pTh, pTl = sb("pTh", 134, [P, KB, T], f32r), sb("pTl", 146, [P, KB, T], f32r)
        dtraw = sb("dtraw", 8, [P, 2, TB, T])
        dth, dtl = sb("dth", 24, [P, 2, TB, T], f32r), sb("dtl", 40, [P, 2, TB, T], f32r)
        dcraw = sb("dcraw", 56, [P, 2, 2, GD])
        dch, dcl = sb("dch", 60, [P, 2, 2, GD], f32r), sb("dcl", 64, [P, 2, 2, GD], f32r)
        fT = sb("fT", 68, [P, 2, T])
        fh, fl = sb("fh", 72, [P, TB, GD], f32r), sb("fl", 76, [P, TB, GD], f32r)
        gh, gl = sb("gh", 80, [P, 2, 2, T], f32r), sb("gl", 88, [P, 2, 2, T], f32r)
        yh, yl = sb("yh", 160, [P, FD // P, T], f32r), sb("yl", 176, [P, FD // P, T], f32r)
        oh = sb("oh", 128, [P, HEADS, T], f32r)
        ol = sb("ol", 56, [P, HEADS, T], f32r)
        gate = [sb(f"gate{s}", 192 + 4 * s, [P, 2, T]) for s in range(2)]
        mt = [sb(f"mt{s}", 200 + 2 * s, [P, T]) for s in range(2)]
        merged = sb("merged", 96, [P, DC, T])
        mh, ml = sb("mh", 128, [P, DC, T], f32r), sb("ml", 160, [P, DC, T], f32r)
        xres = sb("xres", 56, [P, TB, D])
        ybuf = [sb(f"ybuf{s}", 192 + 2 * s, [P, T]) for s in range(2)]
        ln_g, ln_b = sb("ln_g", 88, [P, D]), sb("ln_b", 96, [P, D])
        stats1 = sb("stats1", 5.5, [P, TB, DC, 6])
        xn2 = sb("xn2", 160, [P, TB, D])
        h2h, h2l = sb("h2h", 104, [P, DC, T], f32r), sb("h2l", 8, [P, DC, T], f32r)
        aff2 = [sb(f"aff2_{s}", 40 + 2 * s, [P, T]) for s in range(2)]
        w2raw = [sb(f"w2raw{s}", 40 + 8 * s, [P, DC, P]) for s in range(2)]
        w2h = [sb(f"w2h{s}", 56 + 8 * s, [P, DC, P], f32r) for s in range(2)]
        w2l = [sb(f"w2l{s}", 72 + 8 * s, [P, DC, P], f32r) for s in range(2)]
        keys = sb("keys", 88, [P, 2 * PH, P])
        keyh, keyl = sb("keyh", 136, [P, 2 * PH, P], f32r), sb("keyl", 144, [P, 2 * PH, P], f32r)
        pq = [[sb(f"pq{p}{s}", 152 + 4 * s + 2 * p, [P, T], f32r) for s in range(2)] for p in range(2)]
        score = sb("score", 168, [P, TB, 2 * PH, NK])
        sc1 = sb("tk_sc1", 40, [P, 2 * PH, NK])
        sc2 = sb("tk_sc2", 48, [P, 2 * PH, NK])
        top = sb("tk_top", 56, [P, 2 * PH, TOPK])
        topi = sb("tk_topi", 57, [P, 2 * PH, TOPK], u32)
        topf = sb("tk_topf", 58, [P, 2 * PH, TOPK])
        cand = sb("tk_cand", 59, [P, PH, 256])
        cand2 = sb("tk_cand2", 67, [P, PH, 256])
        best = sb("tk_best", 75, [P, PH, TOPK])
        besti = sb("tk_besti", 75.5, [P, PH, TOPK], u32)
        bpos = sb("tk_bpos", 76, [P, 2, PH, TOPK], u32)
        bposf = sb("tk_bposf", 77, [P, 2, PH, TOPK])
        pick = sb("tk_pick", 78, [P, PH * TOPK, TOPK])
        chosen = sb("tk_chosen", 86, [P, 3, PH * TOPK])
        smalls = sb("tk_smalls", 87.5, [P, 3, PH])
        wait_pad = sb("wait_pad", 87.875, [P, 1])
        iota = sb("iota", 88, [P, P])
        chT = sb("chT", 89, [P, 3, T])
        chwh, chwl = sb("chwh", 200, [P, T], f32r), sb("chwl", 202, [P, T], f32r)
        oneI = [sb(f"oneI{s}", 40 + 2 * s, [P, 4, P], f32r) for s in range(2)]
        oneJh = [sb(f"oneJh{s}", 44 + 2 * s, [P, 4, P], f32r) for s in range(2)]
        oneJl = [sb(f"oneJl{s}", 48 + 2 * s, [P, 4, P], f32r) for s in range(2)]
        RT = 64
        route = [sb(f"route{s}", (168, 52)[s], [P, NK, RT]) for s in range(2)]
        pu = [sb(f"pu{s}", 136 + 8 * s, [P, D]) for s in range(2)]
        pT = sb("pT", 96, [P, DC, P])
        pTuh, pTul = sb("pTuh", 152, [P, DC, P], f32r), sb("pTul", 160, [P, DC, P], f32r)
        uraw = [sb(f"uraw{s}", 40 + 8 * s, [P, D]) for s in range(2)]
        vraw = [sb(f"vraw{s}", 56 + 8 * s, [P, D]) for s in range(2)]
        uTh, uTl = sb("uTh", 72, [P, DC, P], f32r), sb("uTl", 80, [P, DC, P], f32r)
        wt = [sb(f"wt{s}", 88 + 2 * s, [P, T]) for s in range(2)]
        act_g = [sb(f"act_g{s}", (5.5, 204)[s], [P, T]) for s in range(2)]
        coh = [sb(f"coh{s}", 92 + 2 * s, [P, T], f32r) for s in range(4)]
        col = [sb(f"col{s}", (100, 102, 136, 138)[s], [P, T], f32r) for s in range(4)]
        v2h, v2l = sb("v2h", 140, [P, 2, D], f32r), sb("v2l", 156, [P, 2, D], f32r)
        v3h, v3l = sb("v3h", 40, [P, 2, D], f32r), sb("v3l", 72, [P, 2, D], f32r)
        vs = [(v3h, v3l), (v2h, v2l)]
        acc = sb("acc", 172, [P, TB, D])
        xfin = sb("xfin", 8, [P, TB, D])
        g2row, ln2_g, ln2_b = sb("g2row", 40, [P, D]), sb("ln2_g_b", 48, [P, D]), sb("ln2_b_b", 56, [P, D])
        diag2 = sb("diag2", 204, [P, 4, P])
        affc = [sb(f"affc{s}", 5.5 + s, [P, TC]) for s in range(2)]

        pp = [ctx.enter_context(nc.psum_tensor(f"pp{k}", [P, 1024], fp32)) for k in range(4)]
        raw_q = praw_q[:, :, :].rearrange("p c (h n) -> p c h n", h=2)
        q_parts = [(raw_q[:, :, :, 0:NOPE], 0, 2 * NOPE), (raw_q[:, :, :, NOPE:QK], 2 * NOPE, 2 * QK)]

        pb = [pp[k // 2][:, 512 * (k % 2):512 * (k % 2) + 512] for k in range(8)]

        vec_in, x_in, cst_in = sem("vec_in"), sem("x_in"), sem("cst_in")
        wm_in = [sem(f"wm_in{s}") for s in range(2)]
        fill_set = sem("fill_set")
        vec_turned, vec_copied = sem("vec_turned"), sem("vec_copied")
        silu_exp, silu_set = sem("silu_exp"), sem("silu_set")
        wm_used, mod_set = sem("wm_used"), sem("mod_set")
        var_set, rstd_set, xn_set = sem("var_set"), sem("rstd_set"), sem("xn_set")
        h_turned, h_split = sem("h_turned"), sem("h_split")
        swap_set = sem("swap_set")
        w_in_ = [sem(f"w_in{s}") for s in range(2)]
        w_hi, w_lo, w_used, w_out_ = sem("w_hi"), sem("w_lo"), sem("w_used"), sem("w_out_done")
        dve_chain, act_chain = sem("dve_chain"), sem("act_chain")
        sq_set, sq_used = sem("sq_set"), sem("sq_used")
        ssq_done = sem("ssq_done")
        dg_set, lora_scaled, lora_split = sem("dg_set"), sem("lora_scaled"), sem("lora_split")
        h_hi, one_plus, stg_set = sem("h_hi"), sem("one_plus"), sem("stg_set")
        st_done = [sem(f"st_done{s}") for s in range(2)]
        bc_done, lora_hi, kr_hi = sem("bc_done"), sem("lora_hi"), sem("kr_hi")
        mu_in = [sem(f"mu_in{s}") for s in range(5)]
        mu_prod, mu_red, mu_sum, mu_set = sem("mu_prod"), sem("mu_red"), sem("mu_sum"), sem("mu_set")
        pw_in, pw_hi, pw_lo = sem("pw_in"), sem("pw_hi"), sem("pw_lo")
        pj_done, pj_hi, pj_lo, rope_set = sem("pj_done"), sem("pj_hi"), sem("pj_lo"), sem("rope_set")
        s_done, rope_mid, mx_set, nmx_set, exp_done, inv_set, prob_set = (
            sem(n) for n in ("s_done", "rope_mid", "mx_set", "nmx_set", "exp_done", "inv_set", "prob_set"))
        p_turned, pT_hi, pT_lo, pv_done, o_set = (
            sem(n) for n in ("p_turned", "pT_hi", "pT_lo", "pv_done", "o_set"))
        dft_in, dft_hi, dft_split, f_in = sem("dft_in"), sem("dft_hi"), sem("dft_split"), sem("f_in")
        f_turned, f_hi, f_lo = sem("f_turned"), sem("f_hi"), sem("f_lo")
        g_done, g_hi, g_lo, y_done, y_hi, y_lo = (sem(n) for n in ("g_done", "g_hi", "g_lo", "y_done", "y_hi", "y_lo"))
        o_hi, o_lo = sem("o_hi"), sem("o_lo")
        gate_in = [sem(f"gate_in{s}") for s in range(2)]
        merged_set, m_hi, m_lo = sem("merged_set"), sem("m_hi"), sem("m_lo")
        res_in, y_turned, y_added, ln_in = sem("res_in"), sem("y_turned"), sem("y_added"), sem("ln_in")
        g2_prod = sem("g2_prod")
        x1_set, x1_stored, xn2_set = sem("x1_set"), sem("x1_stored"), sem("xn2_set")
        h2_turned, h2_affine, h2_hi, h2_split = (sem(n) for n in ("h2_turned", "h2_affine", "h2_hi", "h2_split"))
        keys_in, keys_turned, key_hi, key_lo = (sem(n) for n in ("keys_in", "keys_turned", "key_hi", "key_lo"))
        pq_hi, sc_done, sc_set = sem("pq_hi"), sem("sc_done"), sem("sc_set")
        tk_chain, iota_in, tk_diff, tk_exp, tk_chosen, ch_turned, ch_set, chw_hi, chw_set = (
            sem(n) for n in ("tk_chain", "iota_in", "tk_diff", "tk_exp", "tk_chosen", "ch_turned", "ch_set", "chw_hi", "chw_set"))
        one_set, r_done, r_set = sem("one_set"), sem("r_done"), sem("r_set")
        r_stored = [sem(f"r_stored{s}") for s in range(2)]
        u_half, pre_raw = sem("u_half"), sem("pre_raw")
        g_stored = [sem(f"g_stored{s}") for s in range(2)]
        g_in = [sem(f"g_in{s}") for s in range(2)]
        u_in = [sem(f"u_in{s}") for s in range(2)]
        v_in = [sem(f"v_in{s}") for s in range(2)]
        wt_in = [sem(f"wt_in{s}") for s in range(2)]
        u_turned, u_hi, u_lo, a_done, gelu_set = (sem(n) for n in ("u_turned", "u_hi", "u_lo", "a_done", "gelu_set"))
        co_set, co_hi, co_lo, v_hi, v_lo, e_done, e_added = (
            sem(n) for n in ("co_set", "co_hi", "co_lo", "v_hi", "v_lo", "e_done", "e_added"))
        fin_in, fin_set, fin_stored, g2_diag, g2_done, g2_copied = (
            sem(n) for n in ("fin_in", "fin_set", "fin_stored", "g2_diag", "g2_done", "g2_copied"))
        kr_ready, kr_swapped, kr_roped, kr_split = (sem(n) for n in
                                                    ("kr_ready", "kr_swapped", "kr_roped", "kr_split"))

        block = ctx.enter_context(nc.Block())

        wmod_v = a["w_mod"][0].rearrange("(c p) n -> p c n", p=P)
        win_v = a["w_in"][0].rearrange("(c p) n -> p c n", p=P)
        NPX = 49
        FIRST_ST = 9
        MG1 = 16
        MU = 2 * MG1
        SS = QK ** -0.5

        @block.sync
        def _(sp):
            def row(n0, n1, src):
                sp.dma_start(vrows[n0:n1, :], src).then_inc(vec_in, 16)

            row(V_C, V_CC, a["c"][0].rearrange("(r n) -> r n", n=P))
            row(V_CC, V_QG, a["c_ctx"].rearrange("(r n) -> r n", n=P))
            row(V_QG, V_KVG, a["q_norm_g"][0].rearrange("(r n) -> r n", n=P))
            row(V_KVG, V_BKV, a["kv_norm_g"][0].rearrange("(r n) -> r n", n=P))
            row(V_BKV, V_BKR, a["b_in"][0, 0:C_KR].rearrange("(r n) -> r n", n=P))
            row(V_BR, V_ROWS, a["b_in"][0, C_CQ:].rearrange("(r n) -> r n", n=P))
            for h in range(2):
                sp.dma_start(vrows[V_BKR:V_BKR + 1, ROPE * h:ROPE * h + ROPE],
                             a["b_in"][0:1, C_KR:C_CQ]).then_inc(vec_in, 16)
            sp.dma_start(mrows[0:96, :], a["b_mod"][0].rearrange("(r n) -> r n", n=P)).then_inc(vec_in, 16)
            sp.dma_start(ident[:, :], a["k_ident"]).then_inc(vec_in, 16)
            sp.dma_start(swap_f[:, :], a["k_swap"]).then_inc(vec_in, 16)

            def mod_group(g, s):
                if not isinstance(g, int) or g >= 2:
                    sp.wait_ge(wm_used, g - 1)
                sp.dma_start(wm[s][:, :, :], wmod_v[:, :, bass.ts(g, 256)]).then_inc(wm_in[s], 16)

            mod_group(0, 0)
            mod_group(1, 1)
            with sp.Fori(1, MG1 // 2) as i:
                mod_group(2 * i, 0)
                mod_group(2 * i + 1, 1)

            sp.wait_ge(h_turned, DC)

            def px_block(b, s):
                if not isinstance(b, int) or b >= 2:
                    sp.wait_ge(w_lo, b - 1)
                if isinstance(b, int) and b == 4:
                    for h in range(2):
                        sp.dma_start(wraw[s][:, :, ROPE * h:ROPE * h + ROPE],
                                     win_v[:, :, C_KR:C_CQ]).then_inc(w_in_[s], 16)
                    return
                at = b * P if isinstance(b, int) and b < 4 else (b - 5) * P + C_CQ
                sp.dma_start(wraw[s][:, :, :], win_v[:, :, bass.ds(at, P)]).then_inc(w_in_[s], 16)

            def mod_unit(j, s, wait=None):
                if wait is not None:
                    sp.wait_ge(mu_red, wait)
                sp.dma_start(mbuf[s][:, :, :], wmod_v[:, :, bass.ds((j + MU) * P, P)]).then_inc(mu_in[s], 16)

            for b in range(17):
                px_block(b, b % 2)
            sp.wait_ge(lora_split, 2 * LC)
            mod_unit(0, 0)
            mod_unit(1, 1)
            px_block(17, 1)
            px_block(18, 0)
            with sp.Fori(1, 16) as i:
                px_block(2 * i + 17, 1)
                mod_unit(2 * i, 0, 2 * i - 1)
                px_block(2 * i + 18, 0)
                mod_unit(2 * i + 1, 1, 2 * i)

            uq_v = a["w_uq"][0].rearrange("(c p) n -> p c n", p=P)
            ukv_v = a["w_ukv"][0].rearrange("(c p) n -> p c n", p=P)
            sp.wait_ge(w_lo, NPX)

            def pair_loads(p):
                sp.dma_start(praw_q[:, :, :], uq_v[:, :, bass.ds(p * (2 * QK), 2 * QK)]).then_inc(pw_in, 16)
                sp.dma_start(praw_kv[:, :, :], ukv_v[:, :, bass.ds(p * 512, 512)]).then_inc(pw_in, 16)

            pair_loads(0)
            with sp.Fori(1, HEADS // 2) as p:
                sp.wait_ge(pw_lo, 2 * p)
                pair_loads(p)

            sp.wait_ge(pw_lo, HEADS)
            sp.wait_ge(pj_done, 10 * (HEADS // 2 - 1) + 3)
            sp.dma_start(dtraw[:, :, :, :], a["k_dft_t"].rearrange("w (b p) s -> p w b s", p=P)).then_inc(dft_in, 16)
            sp.wait_ge(s_done, 4 * HEADS)
            for ss in st_done:
                sp.wait_ge(ss, 16 * ((NPX - FIRST_ST) // 2))
            sp.dma_start(dcraw[:, :, :, :], a["k_dft_c"].rearrange("w (b p) c -> p w b c", p=P)).then_inc(dft_in, 16)
            sp.dma_start(fT[:, :, :], px_d[0:2].rearrange("k p t -> p k t")).then_inc(f_in, 16)
            with sp.Fori(1, FG) as g:
                sp.wait_ge(f_turned, g * 2)
                sp.dma_start(fT[:, :, :], px_d[bass.ds(2 * g, 2)].rearrange("k p t -> p k t")).then_inc(f_in, 16)

            wo_v = a["w_o_mla"][0].rearrange("(c p) n -> p c n", p=P)
            wf_v = a["w_fourier"][0].rearrange("(c p) n -> p c n", p=P)
            wout_v = a["w_out"][0].rearrange("(c p) n -> p c n", p=P)
            sp.wait_ge(dft_split, 1)

            def merge_loads(m, s):
                sp.wait_ge(w_lo, 2 * m + NPX - 1)
                sp.dma_start(wraw[1][:, :, :], wo_v[:, :, bass.ts(m, P)]).then_inc(w_in_[1], 16)
                sp.wait_ge(w_lo, 2 * m + NPX)
                sp.dma_start(wraw[0][:, 0:FD // P, :], wf_v[:, :, bass.ts(m, P)]).then_inc(w_in_[0], 16)
                if not isinstance(m, int) or m >= 2:
                    sp.wait_ge(merged_set, m - 1)
                sp.dma_start(gate[s][:, 0, :], px_d[bass.ds(m + 8, 1)].rearrange("a p t -> (a p) t")).then_inc(gate_in[s], 16)
                sp.dma_start(gate[s][:, 1, :], px_d[bass.ds(m + 24, 1)].rearrange("a p t -> (a p) t")).then_inc(gate_in[s], 16)
                if isinstance(m, int) and m == 0:
                    sp.wait_ge(y_done, FD // P)
                mod_unit(m + 32, 2, m + 32)

            merge_loads(0, 0)
            merge_loads(1, 1)
            with sp.Fori(1, DC // 2) as i:
                merge_loads(2 * i, 0)
                merge_loads(2 * i + 1, 1)
            NM = NPX + 2 * DC
            sp.wait_ge(w_lo, NM - 1)
            sp.dma_start(wraw[1][:, :, :], wout_v[:, :, 0:P]).then_inc(w_in_[1], 16)
            sp.wait_ge(w_lo, NM)
            sp.dma_start(wraw[0][:, :, :], wout_v[:, :, P:2 * P]).then_inc(w_in_[0], 16)
            sp.wait_ge(w_used, NM)
            sp.dma_start(xres[:, :, :], a["x"][0].rearrange("(b p) d -> p b d", p=P)).then_inc(res_in, 16)
            sp.wait_ge(m_lo, DC)
            sp.wait_ge(mu_red, 48)
            sp.dma_start(ln_g[:, :], a["ln1_g"][0:1, :].to_broadcast([P, D])).then_inc(ln_in, 16)
            sp.dma_start(ln_b[:, :], a["ln1_b"][0:1, :].to_broadcast([P, D])).then_inc(ln_in, 16)
            with sp.Fori(1, DC // 2) as i:
                sp.wait_ge(w_lo, 2 * i + NM - 1)
                sp.dma_start(wraw[1][:, :, :], wout_v[:, :, bass.ds(i * (2 * P), P)]).then_inc(w_in_[1], 16)
                sp.wait_ge(w_lo, 2 * i + NM)
                sp.dma_start(wraw[0][:, :, :], wout_v[:, :, bass.ds(i * (2 * P) + P, P)]).then_inc(w_in_[0], 16)
            for b in range(TB):
                sp.wait_ge(x1_set, b + 1)
                sp.dma_start(x1_d[P * b:P * b + P, :], xres[:, b, :]).then_inc(x1_stored, 16)
            wq_v = a["peer_wq"][0].rearrange("(c p) n -> p c n", p=P)
            NO = NM + DC
            sp.wait_ge(x1_set, TB)
            sp.dma_start(keys[:, :, :], a["peer_keys"][0].rearrange("h p k d -> k (h p) d")).then_inc(keys_in, 16)
            sp.wait_ge(h2_split, DC)
            sp.wait_ge(keys_turned, 4)
            with sp.Fori(0, DC // 2) as i:
                for s in (1, 0):
                    sp.wait_ge(w_lo, 2 * i + NO - s)
                    sp.dma_start(w2raw[s][:, :, :], wq_v[:, :, bass.ds(i * (2 * P) + (1 - s) * P, P)]).then_inc(w_in_[s], 16)
                    mod_unit(2 * i + 49 - s, 4 - s, 2 * i + 48 - s)

            sp.wait_ge(mu_red, 64)
            sp.dma_start(iota[:, :], a["k_iota"]).then_inc(iota_in, 16)
            u_v = a["peer_u"][0].rearrange("(i j) d -> i j d", j=NK)
            v_v = a["peer_v"][0].rearrange("(i j) d -> i j d", j=NK)
            flat = lambda t, k: t[bass.ds(k, 1)].rearrange("a j d -> (a j) d")
            for ss in g_stored:
                sp.sem_inc(ss, 16)

            def pre_load(i, s):
                if not isinstance(i, int) or i >= 2:
                    sp.wait_ge(u_turned, 2 * i - 2)
                sp.dma_start(pu[s][:, :], flat(u_v, i)).then_inc(u_in[s], 16)

            def pre_store(i, s):
                sp.wait_ge(gelu_set, i + 1)
                sp.dma_start(flat(gelu_d, i), act_g[s][:, :]).then_inc(g_stored[s], 16)

            def route_store(n, s, k):
                if k == 0:
                    sp.wait_ge(r_set, n)
                i = slice(32 * k, 32 * k + 32)
                sp.dma_start(route_d[:, i, bass.ds(4 * (n - 16), RT)], route[s][:, i, :]).then_inc(r_stored[s], 16)

            sp.wait_ge(sc_done, 2 * PH)
            pre_load(0, 0)
            pre_load(1, 1)
            with sp.Fori(0, PRE_TK * TB // 2) as i:
                for s in range(2):
                    pre_load(2 * i + 2 + s, s)
                    pre_store(2 * i + s, s)
            sp.wait_ge(ch_set, TB)
            for ss in r_stored:
                sp.sem_inc(ss, 16)

            def route_steps(r, first=False):
                for k in range(8):
                    i = 8 * r + PRE_TK * TB + k
                    pre_load(i + 2, k % 2)
                    if k >= 4:
                        route_store(32 * r + 16, 0, k - 4)
                    elif not first:
                        route_store(32 * r, 1, k)
                    pre_store(i, k % 2)

            route_steps(0, first=True)
            with sp.Fori(1, T // RT // 2) as r:
                route_steps(r)
            for k in range(2):
                pre_load(PRE - 2 + k, k)
                route_store(P, 1, 2 * k)
                route_store(P, 1, 2 * k + 1)
                pre_store(PRE - 4 + k, k)
            for ss in r_stored:
                sp.wait_ge(ss, 64 * (T // RT // 2) + 16)

            sp.wait_ge(r_done, P)

            def u_load(i, s):
                if not isinstance(i, int) or i >= PRE + 2:
                    sp.wait_ge(u_turned, i - 1 + PRE)
                sp.dma_start(uraw[s][:, :], flat(u_v, i)).then_inc(u_in[s], 16)

            def coef_loads(i, s, at=None):
                at = i if at is None else at
                if not isinstance(i, int) or i >= 2:
                    sp.wait_ge(co_set, i - 1)
                sp.dma_start(wt[s][:, :], route_d[:, bass.ds(at, 1), :].rearrange("j a t -> j (a t)")).then_inc(wt_in[s], 16)
                if not isinstance(i, int) or i >= 2:
                    sp.wait_ge(v_lo, i - 1)
                sp.dma_start(vraw[s][:, :], flat(v_v, at)).then_inc(v_in[s], 16)

            def early_loads(i, s):
                coef_loads(i, s, i - 2)
                sp.wait_ge(co_lo, i - 1)
                sp.dma_start(act_g[s][:, :], flat(gelu_d, i - 2)).then_inc(g_in[s], 16)

            coef_loads(0, 0, PRE - 2)
            coef_loads(1, 1, PRE - 1)
            for ss in g_stored:
                sp.wait_ge(ss, 8 * (PRE - 2) + 16)
            sp.wait_ge(a_done, PRE)
            with sp.Fori(1, PRE // 2) as i:
                early_loads(2 * i, 0)
                early_loads(2 * i + 1, 1)
            sp.wait_ge(e_done, 8 * (PRE - 2))
            u_load(PRE, 0)
            u_load(PRE + 1, 1)
            coef_loads(PRE, 0)
            u_load(PRE + 2, 0)
            coef_loads(PRE + 1, 1)
            with sp.Fori(PRE // 2 + 1, NK // 2 - 1) as i:
                u_load(2 * i + 1, 1)
                coef_loads(2 * i, 0)
                u_load(2 * i + 2, 0)
                coef_loads(2 * i + 1, 1)
            u_load(NK - 1, 1)
            coef_loads(NK - 2, 0)
            coef_loads(NK - 1, 1)
            sp.wait_ge(a_done, NK)
            sp.wait_ge(x1_stored, 16 * TB)
            sp.dma_start(xfin[:, :, :], x1_d.rearrange("(b p) d -> p b d", p=P)).then_inc(fin_in, 16)
            sp.wait_ge(v_lo, NK)
            sp.dma_start(ln2_g[:, :], a["ln2_g"][0:1, :].to_broadcast([P, D])).then_inc(fin_in, 16)
            sp.dma_start(ln2_b[:, :], a["ln2_b"][0:1, :].to_broadcast([P, D])).then_inc(fin_in, 16)
            for b in range(TB):
                sp.wait_ge(fin_set, b + 1)
                sp.dma_start(out[0, P * b:P * b + P, :], acc[:, b, :]).then_inc(fin_stored, 16)
            sp.wait_ge(fin_stored, 16 * TB)
            for ss in st_done:
                sp.wait_ge(ss, 16 * ((NPX - FIRST_ST) // 2))

        def w_loaded(b):
            if isinstance(b, int):
                return 16 * (b // 2 + 1) + (16 if b % 2 == 0 and b >= 4 else 0)
            raise AssertionError

        @block.gpsimd
        def _(pool):
            pool.memset(ones[:, :], 1.0).then_inc(fill_set, 1)
            pool.memset(mhalf[:, :], -0.5).then_inc(fill_set, 1)
            for b in range(TB + CB):
                pool.wait_ge(wm_in[0], 16 * b + 16)
                src, dst, k = (a["x"], xtok, b) if b < TB else (a["ctx"], ctok, b - TB)
                pool.dma_start(dst[:, k, :], src[0, P * k:P * k + P, :]).then_inc(x_in, 16)
            pool.wait_ge(fill_set, 2)
            pool.wait_ge(var_set, 1)
            pool.tensor_tensor(rstd[:, 0:6], vare[:, 0:6], mhalf[:, 0:6], ALU.pow).then_inc(rstd_set, 1)
            pool.wait_ge(var_set, 2)
            pool.tensor_tensor(rstd[:, 0:6], vare[:, 0:6], mhalf[:, 0:6], ALU.pow).then_inc(rstd_set, 1)
            pool.wait_ge(var_set, 3)
            pool.tensor_tensor(rstd[:, 0:4], vare[:, 0:4], mhalf[:, 0:4], ALU.pow).then_inc(rstd_set, 1)

            def store(n, s):
                pool.wait_ge(stg_set, n + 1)
                pool.dma_start(px_d[bass.ds(n, 1)].rearrange("a p t -> (a p) t"), stg[s][:, :]).then_inc(st_done[s], 16)

            def unit(s, at):
                pool.wait_ge(mu_in[s], at)
                pool.tensor_tensor(mbuf[s][:, :, :], mbuf[s][:, :, :], silu[:, :, 0:1].to_broadcast([P, DC, P]),
                                   ALU.mult).then_inc(mu_prod, 1)

            with pool.Fori(0, 4) as i:
                store(2 * i, 0)
                store(2 * i + 1, 1)
            with pool.Fori(0, 16) as i:
                for s in range(2):
                    unit(s, 16 * i + 16)
                    store(2 * i + 8 + s, s)
            with pool.Fori(0, DC) as m:
                unit(2, 16 * m + 16)
            def inv_std(k, n):
                pool.wait_ge(var_set, n)
                pool.tensor_tensor(rstd[:, k:k + 1], vare[:, k:k + 1], mhalf[:, k:k + 1], ALU.pow).then_inc(rstd_set, 1)

            for n, k in enumerate(LN_ORDER):
                inv_std(k, 4 + n)
            with pool.Fori(0, DC // 2) as m:
                for s in (3, 4):
                    unit(s, 16 * m + 16)
            with pool.Fori(0, PRE) as i:
                for h in range(2):
                    c = slice(8 * h, 8 * h + 8)
                    pool.wait_ge(u_hi, 2 * i + h + 1)
                    pool.tensor_tensor(pTul[:, c, :], pT[:, c, :], pTuh[:, c, :].bitcast(fp32),
                                       ALU.subtract).then_inc(u_lo, 1)
            def gated(b):
                pool.wait_ge(e_added, 16 * (NK // 2 - 1) + 4 * b + 4)
                pool.tensor_tensor(acc[:, b, :], acc[:, b, :], g2row[:, :], ALU.mult).then_inc(g2_prod, 1)

            pool.wait_ge(g2_copied, 4)
            gated(0)
            for b in range(TB):
                if b + 1 < TB:
                    gated(b + 1)
                inv_std(b, 12 + b)

        @block.scalar
        def _(act):
            ch = Tally(act, act_chain)
            act.dma_start(rot[:, :, :], a["k_rot"]).then_inc(cst_in, 16)
            act.wait_ge(vec_copied, 1)
            act.activation(silu_t[:, :], vecT[:, 0:2 * DC], ACT.Exp, scale=-1.0).then_inc(silu_exp, 1)
            act.wait_ge(vec_in, 176)
            act.activation(swap[:, :], swap_f[:, :], ACT.Copy).then_inc(swap_set, 1)

            def mod_group(g, s):
                act.wait_ge(wm_used, g + 1)
                act.activation(modrow[:, bass.ts(g, 256)], pb[s][0:2, 0:256], ACT.Copy).then_inc(mod_set, 1)

            with act.Fori(0, MG1 // 2) as i:
                mod_group(2 * i, 0)
                mod_group(2 * i + 1, 1)

            act.wait_ge(one_plus, 1)
            for c in range(DC):
                s = c % 2
                act.wait_ge(h_turned, c + 1)
                if c >= 2:
                    act.wait_ge(h_split, c - 1)
                act.activation(affx[s][:, :], pb[s][:, :], ACT.Identity,
                               scale=modT[:, M_SC1 + c, 0:1], bias=modT[:, M_SH1 + c, 0:1])
                ch.inc(act.activation(affc[s][:, :], pb[2 + s][:, 0:TC], ACT.Identity,
                                      scale=modT[:, M_SC1 + c, 1:2], bias=modT[:, M_SH1 + c, 1:2]))
                act.wait_ge(act_chain, ch.at)
                act.activation(hxh[:, c, :], affx[s][:, :], ACT.Copy)
                act.activation(hch[:, c, :], affc[s][:, :], ACT.Copy).then_inc(h_hi, 1)

            def w_split(b, s, at, n=DC):
                act.wait_ge(w_in_[s], at)
                if not isinstance(b, int) or b >= 2:
                    act.wait_ge(w_used, b - 1)
                act.activation(wh[s][:, 0:n, :], wraw[s][:, 0:n, :], ACT.Copy).then_inc(w_hi, 1)

            def col_of(n):
                return vecT[:, bass.ds(n, 1)]

            def px_store(b, s, n, slot, func):
                act.wait_ge(w_used, b + 1)
                if not isinstance(n, int) or n >= 2:
                    act.wait_ge(st_done[slot], (n - slot) * 8)
                act.activation(stg[slot][:, :], pb[s][:, :], func, bias=col_of(b - 5 + V_BR)).then_inc(w_out_, 1)
                act.wait_ge(w_out_, b + 1)
                act.sem_inc(stg_set, 1)

            w_split(0, 0, w_loaded(0))
            for b in range(11):
                s = b % 2
                w_split(b + 1, (b + 1) % 2, w_loaded(b + 1))
                if b < 5:
                    dst = ckv[:, b, :] if b < 4 else kr[:, :]
                    act.wait_ge(w_used, b + 1)
                    bias = vecT[:, V_BKV + b:V_BKV + b + 1]
                    act.activation(dst[:, 0:T], pb[s][:, :], ACT.Identity, bias=bias)
                    act.activation(dst[:, T:NKEY], pb[2 + s][:, 0:TC], ACT.Identity, bias=bias).then_inc(w_out_, 1)
                elif b < 9:
                    act.wait_ge(w_used, b + 1)
                    act.activation(cq[:, b - 5, :], pb[s][:, :], ACT.Identity, bias=col_of(b - 5 + V_BR)).then_inc(w_out_, 1)
                else:
                    px_store(b, s, b - FIRST_ST, b - FIRST_ST, ACT.Identity)
                if b == 4:
                    act.wait_ge(w_out_, 5)
                    act.wait_ge(vec_copied, 1)
                    act.activation(krh[:, :], kr[:, :], ACT.Copy).then_inc(kr_hi, 1)
                if b == 6:
                    act.wait_ge(kr_roped, 1)
                    act.activation(krh[:, :], kr[:, :], ACT.Copy).then_inc(kr_hi, 1)
                if b == 7:
                    for k in range(LC):
                        act.wait_ge(lora_scaled, k + 1)
                        act.activation(ckvh[:, k, :], ckv[:, k, :], ACT.Copy).then_inc(lora_hi, 1)
                if b == 10:
                    for k in range(LC):
                        act.wait_ge(lora_scaled, LC + k + 1)
                        act.activation(cqh[:, k, :], cq[:, k, :], ACT.Copy).then_inc(lora_hi, 1)
            with act.Fori(0, 3) as i:
                for u in range(2):
                    w_split(2 * i + 12 + u, u, 16 * i + 16 * 7 + (16 if u == 0 else 0))
                    px_store(2 * i + 11 + u, 1 - u, 2 * i + 2 + u, u, ACT.Identity)
            with act.Fori(0, 15) as i:
                for u in range(2):
                    w_split(2 * i + 18 + u, u, 16 * i + 16 * 10 + (16 if u == 0 else 0))
                    px_store(2 * i + 17 + u, 1 - u, 2 * i + 8 + u, u, ACT.Sigmoid)
            w_split(48, 0, w_loaded(48))
            px_store(47, 1, 38, 0, ACT.Sigmoid)
            px_store(48, 0, 39, 1, ACT.Sigmoid)

            def pair_split(p, which):
                act.wait_ge(pw_in, 32 * p + 32)
                if which == 0:
                    for src, c0, c1 in q_parts:
                        ins = act.activation(pqh[:, :, c0:c1].rearrange("p c (h n) -> p c h n", h=2), src, ACT.Copy)
                    ins.then_inc(pw_hi, 1)
                else:
                    act.activation(pkh[:, :, :], praw_kv[:, :, :], ACT.Copy).then_inc(pw_hi, 1)

            def tile_hi(p, n, dst, src):
                act.wait_ge(pj_done, 10 * p + n + 1)
                act.activation(dst, src, ACT.Copy).then_inc(pj_hi, 1)

            def queries(p, after0=None, after1=None):
                tile_hi(p, 0, qrh[:, :], pb[4][:, :])
                if after0:
                    after0()
                tile_hi(p, 1, qh[:, 0, :], pb[0][:, :])
                if after1:
                    after1()
                tile_hi(p, 2, qh[:, 1, :], pb[1][:, :])
                if after1:
                    pair_split(p, 1)
                act.wait_ge(rope_set, p + 1)
                tile_hi(p, 3, qrh[:, :], rt[0][:, :])

            def attention_pair(p, last=False):
                B = (pb[4], pb[5])
                for h in range(2):
                    tile_hi(p, 4 + h, kTh[:, h, 0:T], B[h][:, :])
                tile_hi(p, 6, kTh[:, :, T:NKEY], B[0][:, :].rearrange("p (h t) -> p h t", h=2))

                def turned_hi(n):
                    act.wait_ge(p_turned, 8 * p + n + 1)
                    if n % 4 == 0 and (n > 0 or not isinstance(p, int) or p > 0):
                        act.wait_ge(pv_done, 2 * p + n // 4)
                    act.activation(pTh[:, :, P * (n % 4):P * (n % 4) + P],
                                   pp[3][:, 0:NKEY].rearrange("p (k t) -> p k t", k=KB), ACT.Copy).then_inc(pT_hi, 1)

                def keep_out(h):
                    act.wait_ge(pv_done, 2 * p + h + 1)
                    act.activation(oT[:, bass.ds(2 * p + h, 1), :].rearrange("p a t -> p (a t)"), pb[4 + h][:, :],
                                   ACT.Copy).then_inc(o_set, 1)

                for n in range(8):
                    if n >= 2 and n != 6:
                        turned_hi(n - 2)
                    act.wait_ge(nmx_set, 8 * p + n + 1)
                    if n >= 2 or not isinstance(p, int) or p > 0:
                        act.wait_ge(p_turned, 8 * p + n - 1)
                    act.activation(prob[n % 2][:, :], pp[n % 2][:, 0:NKEY], ACT.Exp, bias=nmx[:, n:n + 1], scale=SS,
                                   accum_out=rsum[:, n:n + 1]).then_inc(exp_done, 1)
                    if n in (1, 3, 5):
                        v = n // 2
                        tile_hi(p, 7 + v, vh[:, 2 * v:2 * v + 2, :, :],
                                B[(7 + v) % 2][:, :].rearrange("p (b h d) -> p b h d", b=2, h=2))
                    if n == 2 and not last:
                        pair_split(p + 1, 0)
                    if n == 6:
                        keep_out(0)
                        turned_hi(4)
                if last:
                    turned_hi(6)
                    turned_hi(7)
                    act.wait_ge(dft_in, 32)
                    act.wait_ge(pj_done, 10 * (HEADS // 2))
                    for w in range(2):
                        act.activation(dth[:, w, :, :], dtraw[:, w, :, :], ACT.Copy)
                    act.activation(dch[:, :, :, :], dcraw[:, :, :, :], ACT.Copy).then_inc(dft_hi, 1)
                else:
                    queries(p + 1, lambda: turned_hi(6), lambda: turned_hi(7))
                keep_out(1)

            act.wait_ge(w_used, NPX)
            pair_split(0, 0)
            pair_split(0, 1)
            for ss in st_done:
                act.wait_ge(ss, 16 * ((NPX - FIRST_ST) // 2))
            queries(0)
            attention_pair(0)
            with act.Fori(1, HEADS // 2 - 1) as p:
                attention_pair(p)
            attention_pair(HEADS // 2 - 1, True)

            def fourier_group(g):
                for cb in range(2):
                    act.wait_ge(f_turned, 2 * g + cb + 1)
                    act.activation(fh[:, :, P * cb:P * cb + P], pb[cb][:, :].rearrange("p (b c) -> p b c", b=TB),
                                   ACT.Copy).then_inc(f_hi, 1)
                for n in range(4):
                    act.wait_ge(g_done, 4 * g + n + 1)
                    act.activation(gh[:, n % 2, n // 2, :], pb[2 + n][:, :], ACT.Copy).then_inc(g_hi, 1)
                for k in range(2):
                    act.wait_ge(y_done, 2 * g + k + 1)
                    kk = bass.ds(2 * g + k, 1)
                    act.activation(yh[:, kk, :].rearrange("p a t -> p (a t)"), pb[6 + k][:, :],
                                   ACT.Copy).then_inc(y_hi, 1)

            def split_out(c):
                act.activation(oh[:, 4 * c:4 * c + 4, :], oT[:, 4 * c:4 * c + 4, :], ACT.Copy).then_inc(o_hi, 1)

            fourier_group(0)
            act.wait_ge(pv_done, HEADS)
            act.wait_ge(o_set, HEADS)
            split_out(0)
            split_out(1)
            fourier_group(1)
            split_out(2)
            split_out(3)
            with act.Fori(2, FG) as g:
                fourier_group(g)

            NM, NO = NPX + 2 * DC, NPX + 3 * DC
            act.wait_ge(y_done, FD // P)

            def wo_hi(m):
                w_split(2 * m + NPX, 1, 16 * m + 16 * 25)

            def wf_hi(m):
                w_split(2 * m + NPX + 1, 0, 16 * m + 16 * 27, FD // P)

            with act.Fori(0, DC) as m:
                wo_hi(m)
                wf_hi(m)
            act.wait_ge(w_used, NM)
            w_split(NM, 1, 16 * 41)
            for c in range(4):
                act.wait_ge(merged_set, 4 * c + 4)
                act.activation(mh[:, 4 * c:4 * c + 4, :], merged[:, 4 * c:4 * c + 4, :], ACT.Copy).then_inc(m_hi, 1)

            def out_block(n, s):
                act.wait_ge(w_used, n + NM + 1)
                if not isinstance(n, int) or n >= 2:
                    act.wait_ge(y_turned, n - 1)
                act.activation(ybuf[1 - s][:, :], pb[s][:, :], ACT.Identity,
                               scale=modT[:, bass.ds(n + M_G1, 1), 0:1].rearrange("p a b -> p (a b)")).then_inc(w_out_, 1)

            act.wait_ge(mu_set, 1)
            w_split(NM + 1, 0, 16 * 43)
            out_block(0, 1)
            w_split(NM + 2, 1, 16 * 42)
            out_block(1, 0)
            with act.Fori(1, DC // 2 - 1) as i:
                w_split(2 * i + NM + 1, 0, 16 * i + 16 * 43)
                out_block(2 * i, 1)
                w_split(2 * i + NM + 2, 1, 16 * i + 16 * 42)
                out_block(2 * i + 1, 0)
            w_split(NM + 15, 0, 16 * 50)
            out_block(14, 1)
            out_block(15, 0)

            act.wait_ge(mu_set, 3)
            for c in range(DC):
                s = c % 2
                act.wait_ge(h2_turned, c + 1)
                if c >= 2:
                    act.wait_ge(h2_split, c - 1)
                act.activation(aff2[s][:, :], pb[s][:, :], ACT.Identity, scale=modT[:, M_SC2 + c, 0:1],
                               bias=modT[:, M_SH2 + c, 0:1]).then_inc(h2_affine, 1)
                act.wait_ge(h2_affine, c + 1)
                act.activation(h2h[:, c, :], aff2[s][:, :], ACT.Copy).then_inc(h2_hi, 1)

            for k in range(4):
                act.wait_ge(keys_turned, k + 1)
                act.activation(keyh[:, 4 * k:4 * k + 4, :], pb[4 + k][:, :].rearrange("p (n k) -> p n k", n=4),
                               ACT.Copy).then_inc(key_hi, 1)
            act.wait_ge(x1_stored, 16 * TB)

            def q_split(b, s, at):
                act.wait_ge(w_in_[s], at)
                act.wait_ge(w_used, b - 1)
                act.activation(w2h[s][:, :, :], w2raw[s][:, :, :], ACT.Copy).then_inc(w_hi, 1)

            def q_block(n, s):
                act.wait_ge(w_used, n + NO + 1)
                if not isinstance(n, int) or n >= 2:
                    act.wait_ge(sc_done, n - 1)
                act.activation(pq[0][s][:, :], pb[s][:, :], ACT.Copy).then_inc(pq_hi, 1)

            def keep_score(n, s):
                act.wait_ge(sc_done, n + 1)
                act.activation(score[:, :, bass.ds(n, 1), :].rearrange("p b a k -> p b (a k)"),
                               pb[2 + s][:, :].rearrange("p (b k) -> p b k", b=TB), ACT.Copy).then_inc(sc_set, 1)

            act.wait_ge(h2_split, DC)
            q_split(NO, 1, 16 * 49)
            q_split(NO + 1, 0, 16 * 51)
            q_block(0, 1)
            with act.Fori(0, DC // 2 - 1) as i:
                q_split(2 * i + NO + 2, 1, 16 * i + 16 * 50)
                q_block(2 * i + 1, 0)
                keep_score(2 * i, 1)
                q_split(2 * i + NO + 3, 0, 16 * i + 16 * 52)
                q_block(2 * i + 2, 1)
                keep_score(2 * i + 1, 0)
            q_block(15, 0)
            keep_score(14, 1)
            keep_score(15, 0)

            def pre_copy(i, h):
                act.wait_ge(u_turned, 2 * i + h + 1)
                if not isinstance(i, int) or i >= 1:
                    act.wait_ge(u_lo, 2 * i - 1 + h)
                act.activation(pT[:, 8 * h:8 * h + 8, :], pp[h][:, :].rearrange("p (c j) -> p c j", c=8),
                               ACT.Copy).then_inc(pre_raw, 1)

            def pre_hi(i, h):
                act.wait_ge(pre_raw, 2 * i + h + 1)
                if not isinstance(i, int) or i >= 1:
                    act.wait_ge((u_half, a_done)[h], i)
                act.activation(pTuh[:, 8 * h:8 * h + 8, :], pT[:, 8 * h:8 * h + 8, :], ACT.Copy).then_inc(u_hi, 1)

            def pre_gelu(i, s):
                act.wait_ge(a_done, i + 1)
                act.wait_ge(g_stored[s], 8 * (i - s) + 16)
                act.activation(act_g[s][:, :], pb[4 + s][:, :], ACT.Gelu).then_inc(gelu_set, 1)

            act.wait_ge(mu_red, 64)
            for h in range(2):
                pre_copy(0, h)
                pre_hi(0, h)

            with act.Fori(0, TB) as b:
                for k in range(PRE_TK):
                    i = b * PRE_TK + k
                    pre_copy(i + 1, 0)
                    pre_hi(i + 1, 0)
                    if k == 2:
                        act.wait_ge(tk_diff, b + 1)
                        act.activation(best[:, :, :], best[:, :, :], ACT.Exp).then_inc(tk_exp, 1)
                    pre_copy(i + 1, 1)
                    pre_gelu(i, k % 2)
                    pre_hi(i + 1, 1)
            act.wait_ge(ch_set, TB)
            act.activation(chwh[:, :], chT[:, 2, :], ACT.Copy).then_inc(chw_hi, 1)

            def keep_route(g, k, slot, q):
                act.wait_ge(r_done, g + 1)
                act.activation(route[slot][:, :, 4 * q:4 * q + 4].rearrange("p i t -> p t i"),
                               pb[k][:, :].rearrange("p (t i) -> p t i", t=4), ACT.Copy).then_inc(r_set, 1)

            def route_part(r):
                for k in range(8):
                    slot, i = k // 4, 8 * r + PRE_TK * TB + k
                    if k % 4 == 0:
                        act.wait_ge(r_stored[slot], 64 * r + 16)
                    for q in range(RI):
                        if q % 2 == 1:
                            pre_copy(i + 1, q // 2)
                        if q == 3:
                            pre_gelu(i, k % 2)
                        if q % 2 == 1:
                            pre_hi(i + 1, q // 2)
                        keep_route(32 * r + 4 * k + q, 6 + q % 2, slot, 4 * (k % 4) + q)

            with act.Fori(0, T // RT // 2) as r:
                route_part(r)
            for i in range(PRE - PRE_END, PRE - 1):
                pre_copy(i + 1, 0)
                pre_hi(i + 1, 0)
                pre_copy(i + 1, 1)
                pre_gelu(i, i % 2)
                pre_hi(i + 1, 1)

            def expert_u(i):
                act.wait_ge(u_turned, i + 1 + PRE)
                act.wait_ge(a_done, i)
                for k in range(2):
                    act.activation(uTh[:, 8 * k:8 * k + 8, :], pp[k][:, :].rearrange("p (c j) -> p c j", c=8),
                                   ACT.Copy).then_inc(u_hi, 1)

            def expert_gelu(i, u):
                act.wait_ge(a_done, i + 1)
                if not isinstance(i, int) or i >= 1:
                    act.wait_ge(co_lo, i)
                act.activation(act_g[0][:, :], pb[4][:, :], ACT.Gelu).then_inc(gelu_set, 1)

            def expert_coef(i, slot, s=0):
                act.wait_ge(co_set, i + 1)
                act.activation(coh[slot][:, :], act_g[s][:, :], ACT.Copy).then_inc(co_hi, 1)

            def expert_v(i, u):
                act.wait_ge(v_in[u], 8 * (i - u) + 16)
                act.wait_ge(e_done, 8 * (i - u))
                act.activation(v2h[:, u, :], vraw[u][:, :], ACT.Copy).then_inc(v_hi, 1)

            def early_v(g, par, u):
                act.wait_ge(v_in[u], 16 * g + 16)
                if not isinstance(g, int) or g >= 2:
                    act.wait_ge(e_done, 16 * (g - 1))
                act.activation(vs[par][0][:, u, :], vraw[u][:, :], ACT.Copy).then_inc(v_hi, 1)

            def early_group(g, par):
                for u in range(2):
                    early_v(g, par, u)
                    expert_coef(2 * g + u, 2 * par + u, u)

            def expert_group(g, par, first=False, last=False):
                if not first:
                    expert_v(2 * g - 2, 0)
                    expert_v(2 * g - 1, 1)
                for u in range(2):
                    expert_gelu(2 * g + u, u)
                    if not (last and u == 1):
                        expert_u(2 * g + u + 1)
                    expert_coef(2 * g + u, 2 * par + u)

            early_v(0, 0, 0)
            early_v(0, 0, 1)
            expert_coef(0, 0, 0)
            pre_gelu(PRE - 1, 1)
            expert_coef(1, 1, 1)
            early_group(1, 1)
            with act.Fori(1, PRE // 4) as i:
                early_group(2 * i, 0)
                early_group(2 * i + 1, 1)
            expert_u(PRE)
            expert_group(PRE // 2, 0, first=True)
            expert_group(PRE // 2 + 1, 1)
            with act.Fori(PRE // 4 + 1, NK // 4 - 1) as i:
                expert_group(2 * i, 0)
                expert_group(2 * i + 1, 1)
            expert_group(NK // 2 - 2, 0)
            expert_group(NK // 2 - 1, 1, last=True)
            for k in range(4):
                act.wait_ge(g2_done, k + 1)
                act.activation(g2row[:, 512 * k:512 * k + 512], pb[k][:, :], ACT.Copy).then_inc(g2_copied, 1)
            expert_v(NK - 2, 0)
            expert_v(NK - 1, 1)

        @block.vector
        def _(dve):
            ch = Tally(dve, dve_chain)
            dve.wait_ge(vec_turned, 1)
            dve.tensor_copy(vecT[:, :], pb[4][:, 0:V_ROWS])
            dve.tensor_copy(bmodT[:, :], pb[5][:, 0:96]).then_inc(vec_copied, 1)
            dve.wait_ge(vec_copied, 1)
            dve.wait_ge(silu_exp, 1)
            ch.link(dve.tensor_scalar(silu_t[:, :], silu_t[:, :], 1.0, None, ALU.add))
            ch.link(dve.reciprocal(silu_t[:, :], silu_t[:, :]))
            for w in range(2):
                ins = dve.tensor_tensor(silu[:, :, w], vecT[:, DC * w:DC * w + DC], silu_t[:, DC * w:DC * w + DC], ALU.mult)
            ins.then_inc(silu_set, 1)

            dve.wait_ge(x_in, 16 * (TB + CB))
            tok = [xtok[:, b, :] for b in range(TB)] + [ctok[:, b, :] for b in range(CB)]
            for n, t in enumerate(tok):
                for q in range(4):
                    ins = dve.bn_stats(stats[:, n, q, :], t[:, 512 * q:512 * q + 512])
            ch.link(ins)
            for n in range(len(tok)):
                ins = dve.bn_aggr(mv[:, n, :], stats[:, n, :, :].rearrange("p q s -> p (q s)"))
            ch.link(ins)
            dve.tensor_scalar(vare[:, 0:6], mv[:, 0:6, 1], EPS, None, ALU.add).then_inc(var_set, 1)
            dve.wait_ge(rstd_set, 1)
            for n, t in enumerate(tok):
                ins = dve.tensor_scalar(t, t, mv[:, n, 0:1], rstd[:, n:n + 1], ALU.subtract, ALU.mult)
            ins.then_inc(xn_set, 1)

            dve.wait_ge(vec_turned, 2)
            ch.link(dve.tensor_tensor(modT[:, 0:MU, :], pb[6][:, 0:2 * MU].rearrange("p (n w) -> p n w", w=2),
                                      bmodT[:, 0:MU].unsqueeze(2).to_broadcast([P, MU, 2]), ALU.add))
            dve.tensor_scalar(modT[:, M_SC1:M_SC1 + DC, :], modT[:, M_SC1:M_SC1 + DC, :], 1.0, None,
                              ALU.add).then_inc(one_plus, 1)
            for c in range(DC):
                s = c % 2
                dve.wait_ge(h_hi, c + 1)
                dve.tensor_tensor(hxl[:, c, :], affx[s][:, :], hxh[:, c, :].bitcast(fp32), ALU.subtract)
                dve.tensor_tensor(hcl[:, c, :], affc[s][:, :], hch[:, c, :].bitcast(fp32),
                                  ALU.subtract).then_inc(h_split, 1)

            def w_split(b, s, n=DC):
                dve.wait_ge(w_hi, b + 1)
                dve.tensor_tensor(wl[s][:, 0:n, :], wraw[s][:, 0:n, :], wh[s][:, 0:n, :].bitcast(fp32),
                                  ALU.subtract).then_inc(w_lo, 1)

            def square(k):
                dve.wait_ge(w_out_, k + 1 if k < 4 else k + 2)
                if k >= 2:
                    dve.wait_ge(sq_used, k - 1)
                x = ckv[:, k, :] if k < 4 else cq[:, k - 4, :]
                w = NKEY if k < 4 else T
                dve.tensor_tensor(sq[k % 2][:, 0:w], x, x, ALU.mult).then_inc(sq_set, 1)

            def mean_square(which, nb):
                dve.wait_ge(ssq_done, which + 1)
                if which == 1:
                    dve.wait_ge(bc_done, 1)
                dve.tensor_scalar(vare[:, 0:nb], pb[4 + which][:, 0:2 * nb:2], 1.0 / LORA, EPS,
                                  ALU.mult, ALU.add).then_inc(var_set, 1)
                dve.wait_ge(rstd_set, 2 + which)
                dve.tensor_tensor(diag[:, 0:nb * P].rearrange("p (b t) -> p b t", b=nb),
                                  ident[:, :].unsqueeze(1).to_broadcast([P, nb, P]),
                                  rstd[:, 0:nb].unsqueeze(2).to_broadcast([P, nb, P]),
                                  ALU.mult).then_inc(dg_set, 1)

            def rms_ckv():
                dve.wait_ge(bc_done, 1)
                for k in range(LC):
                    g = vecT[:, V_KVG + k:V_KVG + k + 1]
                    dve.scalar_tensor_tensor(out=ckv[:, k, 0:T], in0=ckv[:, k, 0:T], scalar=g,
                                             in1=pb[6][:, :], op0=ALU.mult, op1=ALU.mult)
                    dve.scalar_tensor_tensor(out=ckv[:, k, T:NKEY], in0=ckv[:, k, T:NKEY], scalar=g,
                                             in1=pb[7][:, 0:TC], op0=ALU.mult, op1=ALU.mult).then_inc(lora_scaled, 1)
                for k in range(LC):
                    dve.wait_ge(lora_hi, k + 1)
                    dve.tensor_tensor(ckvl[:, k, :], ckv[:, k, :], ckvh[:, k, :].bitcast(fp32),
                                      ALU.subtract).then_inc(lora_split, 1)

            def rms_cq():
                dve.wait_ge(bc_done, 2)
                for k in range(LC):
                    dve.scalar_tensor_tensor(out=cq[:, k, :], in0=cq[:, k, :], scalar=vecT[:, V_QG + k:V_QG + k + 1],
                                             in1=pb[6][:, :], op0=ALU.mult, op1=ALU.mult).then_inc(lora_scaled, 1)
                dve.wait_ge(lora_split, LC)
                for k in range(LC):
                    dve.wait_ge(lora_hi, LC + k + 1)
                    dve.tensor_tensor(cql[:, k, :], cq[:, k, :], cqh[:, k, :].bitcast(fp32),
                                      ALU.subtract).then_inc(lora_split, 1)

            w_split(0, 0)
            for b in range(11):
                w_split(b + 1, (b + 1) % 2)
                if b < 4:
                    square(b)
                elif b == 4:
                    dve.wait_ge(kr_hi, 1)
                    dve.tensor_tensor(krl[:, :], kr[:, :], krh[:, :].bitcast(fp32), ALU.subtract).then_inc(kr_ready, 1)
                elif b < 9:
                    square(b - 1)
                if b == 5:
                    mean_square(0, KB)
                    dve.wait_ge(cst_in, 16)
                    dve.wait_ge(kr_swapped, 1)
                    dve.tensor_tensor(tmp[:, 0:T], pb[7][:, :], rot[:, 1, :], ALU.mult)
                    ch.link(dve.tensor_tensor(kr[:, 0:T], kr[:, 0:T], rot[:, 0, :], ALU.mult))
                    dve.tensor_tensor(kr[:, 0:T], kr[:, 0:T], tmp[:, 0:T], ALU.add).then_inc(kr_roped, 1)
                if b == 6:
                    dve.wait_ge(kr_hi, 2)
                    dve.tensor_tensor(krl[:, :], kr[:, :], krh[:, :].bitcast(fp32), ALU.subtract).then_inc(kr_split, 1)
                if b == 7:
                    rms_ckv()
                if b == 9:
                    mean_square(1, TB)
                if b == 10:
                    rms_cq()
            with dve.Fori(0, 3) as i:
                for u in range(2):
                    w_split(2 * i + 12 + u, u)

            def mod_reduce(j, s, r):
                dve.wait_ge(mu_prod, j + 1)
                if not isinstance(j, int) or j >= 2:
                    dve.wait_ge(mu_sum, j - 1)
                dve.tensor_reduce(mred[r][:, :], mbuf[s][:, :, :].rearrange("p c n -> p n c"), AX.X,
                                  ALU.add).then_inc(mu_red, 1)

            def mod_finish(j0, n, bank):
                dve.wait_ge(mu_sum, j0 + n)
                dve.tensor_tensor(modT[:, MU + j0:MU + j0 + n, 0], pb[bank][:, 0:2 * n:2],
                                  bmodT[:, MU + j0:MU + j0 + n], ALU.add).then_inc(mu_set, 1)

            w_split(18, 0)
            mod_reduce(0, 0, 0)
            w_split(19, 1)
            mod_reduce(1, 1, 1)
            with dve.Fori(1, 15) as i:
                for u in range(2):
                    w_split(2 * i + 18 + u, u)
                    mod_reduce(2 * i + u, u, u)
            w_split(48, 0)
            mod_reduce(30, 0, 0)
            mod_reduce(31, 1, 1)
            mod_finish(0, 2 * DC, 4)

            def pair_split(p, which):
                dve.wait_ge(pw_hi, 2 * p + which + 1)
                if which == 0:
                    for src, c0, c1 in q_parts:
                        ins = dve.tensor_tensor(pql[:, :, c0:c1].rearrange("p c (h n) -> p c h n", h=2), src,
                                                pqh[:, :, c0:c1].rearrange("p c (h n) -> p c h n", h=2).bitcast(fp32),
                                                ALU.subtract)
                    ins.then_inc(pw_lo, 1)
                else:
                    dve.tensor_tensor(pkl[:, :, :], praw_kv[:, :, :], pkh[:, :, :].bitcast(fp32), ALU.subtract).then_inc(pw_lo, 1)

            def tile_lo(p, n, dst, src, hi, more=None):
                dve.wait_ge(pj_hi, 10 * p + n + 1)
                ins = dve.tensor_tensor(dst, src, hi.bitcast(fp32), ALU.subtract)
                if more is not None:
                    ins = more()
                ins.then_inc(pj_lo, 1)

            def rope_part(p):
                tile_lo(p, 0, qrl[:, :], pb[4][:, :], qrh[:, :],
                        lambda: dve.tensor_tensor(rt[0][:, :], pb[4][:, :], rot[:, 0, :], ALU.mult))

            def queries(p, after0=None, after1=None):
                rope_part(p)
                if after0:
                    after0()
                tile_lo(p, 1, ql[:, 0, :], pb[0][:, :], qh[:, 0, :])
                if after1:
                    after1()
                tile_lo(p, 2, ql[:, 1, :], pb[1][:, :], qh[:, 1, :])
                dve.wait_ge(pj_done, 10 * p + 4)
                dve.tensor_tensor(rt[1][:, :], pb[0][:, :], rot[:, 1, :], ALU.mult).then_inc(rope_mid, 1)
                dve.wait_ge(rope_mid, p + 1)
                dve.tensor_tensor(rt[0][:, :], rt[0][:, :], rt[1][:, :], ALU.add).then_inc(rope_set, 1)
                tile_lo(p, 3, qrl[:, :], rt[0][:, :], qrh[:, :])
                if after1:
                    pair_split(p, 1)

            def attention_pair(p, last=False):
                B = (pb[4], pb[5])
                for h in range(2):
                    tile_lo(p, 4 + h, kTl[:, h, 0:T], B[h][:, :], kTh[:, h, 0:T])
                tile_lo(p, 6, kTl[:, :, T:NKEY], B[0][:, :].rearrange("p (h t) -> p h t", h=2), kTh[:, :, T:NKEY])
                def row_max(n):
                    dve.wait_ge(s_done, 8 * p + n + 1)
                    dve.reduce_max(rmx[:, n:n + 1], pp[n % 2][:, 0:NKEY], AX.X).then_inc(mx_set, 1)
                    dve.wait_ge(mx_set, 8 * p + n + 1)
                    dve.tensor_scalar(nmx[:, n:n + 1], rmx[:, n:n + 1], -SS, None, ALU.mult).then_inc(nmx_set, 1)

                def normalise(n):
                    dve.wait_ge(exp_done, 8 * p + n + 1)
                    dve.reciprocal(rinv[:, n:n + 1], rsum[:, n:n + 1]).then_inc(inv_set, 1)
                    dve.wait_ge(inv_set, 8 * p + n + 1)
                    dve.tensor_scalar(prob[n % 2][:, :], prob[n % 2][:, :], rinv[:, n:n + 1], None,
                                      ALU.mult).then_inc(prob_set, 1)

                def turned_lo(n):
                    dve.wait_ge(pT_hi, 8 * p + n + 1)
                    t = slice(P * (n % 4), P * (n % 4) + P)
                    dve.tensor_tensor(pTl[:, :, t], pp[3][:, 0:NKEY].rearrange("p (k t) -> p k t", k=KB),
                                      pTh[:, :, t].bitcast(fp32), ALU.subtract).then_inc(pT_lo, 1)

                for n in range(8):
                    row_max(n)
                    if n >= 1:
                        normalise(n - 1)
                    if n >= 2:
                        turned_lo(n - 2)
                    if n in (1, 3, 5):
                        v = n // 2
                        tile_lo(p, 7 + v, vl[:, 2 * v:2 * v + 2, :, :],
                                B[(7 + v) % 2][:, :].rearrange("p (b h d) -> p b h d", b=2, h=2),
                                vh[:, 2 * v:2 * v + 2, :, :])
                    if n == 2 and not last:
                        pair_split(p + 1, 0)
                normalise(7)
                if last:
                    turned_lo(6)
                    turned_lo(7)
                else:
                    queries(p + 1, lambda: turned_lo(6), lambda: turned_lo(7))

            pair_split(0, 0)
            pair_split(0, 1)
            dve.wait_ge(kr_split, 1)
            for ss in st_done:
                dve.wait_ge(ss, 16 * ((NPX - FIRST_ST) // 2))
            queries(0)
            attention_pair(0)
            with dve.Fori(1, HEADS // 2 - 1) as p:
                attention_pair(p)
            attention_pair(HEADS // 2 - 1, True)

            def lo(dst, src, hi):
                return dve.tensor_tensor(dst, src, hi.bitcast(fp32), ALU.subtract)

            dve.wait_ge(dft_hi, 1)
            for w in range(2):
                lo(dtl[:, w, :, :], dtraw[:, w, :, :], dth[:, w, :, :])
            lo(dcl[:, :, :, :], dcraw[:, :, :, :], dch[:, :, :, :]).then_inc(dft_split, 1)
            with dve.Fori(0, FG) as g:
                for cb in range(2):
                    dve.wait_ge(f_hi, 2 * g + cb + 1)
                    lo(fl[:, :, P * cb:P * cb + P], pb[cb][:, :].rearrange("p (b c) -> p b c", b=TB),
                       fh[:, :, P * cb:P * cb + P]).then_inc(f_lo, 1)
                for n in range(4):
                    dve.wait_ge(g_hi, 4 * g + n + 1)
                    lo(gl[:, n % 2, n // 2, :], pb[2 + n][:, :], gh[:, n % 2, n // 2, :]).then_inc(g_lo, 1)
                for k in range(2):
                    dve.wait_ge(y_hi, 2 * g + k + 1)
                    lo(yl[:, bass.ds(2 * g + k, 1), :].rearrange("p a t -> p (a t)"), pb[6 + k][:, :],
                       yh[:, bass.ds(2 * g + k, 1), :].rearrange("p a t -> p (a t)")).then_inc(y_lo, 1)

            NM, NO = NPX + 2 * DC, NPX + 3 * DC
            w_split(NPX, 1)
            dve.wait_ge(o_hi, 4)
            dve.wait_ge(y_done, FD // P)
            for c in range(4):
                lo(ol[:, 4 * c:4 * c + 4, :], oT[:, 4 * c:4 * c + 4, :], oh[:, 4 * c:4 * c + 4, :]).then_inc(o_lo, 1)
            w_split(NPX + 1, 0, FD // P)
            dve.wait_ge(o_lo, 4)

            def merge(m, s, last=False):
                mod_reduce(m + 32, 2, s)
                dve.wait_ge(w_lo, 2 * m + NPX + 2)
                dve.wait_ge(gate_in[s], 16 * (m - s) + 32)
                dve.wait_ge(w_used, 2 * m + NPX + 1)
                dve.tensor_tensor(mt[0][:, :], pb[1][:, :], gate[s][:, 0, :], ALU.mult).then_inc(w_out_, 1)
                w_split(2 * m + NPX + 2, 1)
                dve.wait_ge(w_used, 2 * m + NPX + 2)
                dve.tensor_tensor(mt[1][:, :], pb[0][:, :], gate[s][:, 1, :], ALU.mult).then_inc(w_out_, 1)
                dve.wait_ge(w_out_, 2 * m + NPX + 2)
                dve.tensor_tensor(merged[:, bass.ds(m, 1), :].rearrange("p a t -> p (a t)"), mt[0][:, :], mt[1][:, :],
                                  ALU.add).then_inc(merged_set, 1)
                if not last:
                    w_split(2 * m + NPX + 3, 0, FD // P)

            with dve.Fori(0, DC // 2 - 1) as i:
                merge(2 * i, 0)
                merge(2 * i + 1, 1)
            merge(DC - 2, 0)
            merge(DC - 1, 1, last=True)
            mod_finish(2 * DC, DC, 6)
            dve.wait_ge(mu_set, 2)
            dve.tensor_scalar(modT[:, M_SC2:M_SC2 + DC, 0], modT[:, M_SC2:M_SC2 + DC, 0], 1.0, None,
                              ALU.add).then_inc(mu_set, 1)
            for c in range(4):
                dve.wait_ge(m_hi, c + 1)
                for k in range(4):
                    lo(ml[:, 4 * c + k, :], merged[:, 4 * c + k, :], mh[:, 4 * c + k, :]).then_inc(m_lo, 1)

            def residual(n, y):
                dve.wait_ge(y_turned, n + 1)
                xs = xres[:, :, bass.ts(n, P)]
                dve.scalar_tensor_tensor(out=xs, in0=xs, scalar=ALPHA,
                                         in1=pb[2 + y][:, :].rearrange("p (b d) -> p b d", b=TB),
                                         op0=ALU.mult, op1=ALU.add).then_inc(y_added, 1)
                dve.wait_ge(y_added, n + 1)
                for b in range(TB):
                    ins = dve.bn_stats(stats1[:, b, bass.ds(n, 1), :].rearrange("p a s -> p (a s)"),
                                       xres[:, b, bass.ts(n, P)])
                return ins

            w_split(NM + 1, 0)
            dve.wait_ge(res_in, 16)
            with dve.Fori(0, DC // 2 - 1) as i:
                w_split(2 * i + NM + 2, 1)
                residual(2 * i, 0)
                w_split(2 * i + NM + 3, 0)
                residual(2 * i + 1, 1)
            residual(DC - 2, 0)
            ch.link(residual(DC - 1, 1))

            def variance(k, t, parts=None):
                if parts is None:
                    parts = stats[:, k, :, :]
                    for q in range(4):
                        ins = dve.bn_stats(stats[:, k, q, :], t[:, 512 * q:512 * q + 512])
                    ch.link(ins)
                ch.link(dve.bn_aggr(mv[:, k, :], parts.rearrange("p q s -> p (q s)")))
                dve.tensor_scalar(vare[:, k:k + 1], mv[:, k, 1:2], EPS, None, ALU.add).then_inc(var_set, 1)

            def affine(t, k, g, b, done):
                ch.link(dve.scalar_tensor_tensor(out=t, in0=t, scalar=mv[:, k, 0:1], in1=g[:, :], op0=ALU.subtract,
                                                 op1=ALU.mult))
                dve.scalar_tensor_tensor(out=t, in0=t, scalar=rstd[:, k:k + 1], in1=b[:, :], op0=ALU.mult,
                                         op1=ALU.add).then_inc(done, 1)

            def norm1(b):
                variance(b, None, stats1[:, b, :, :])

            def norm1_out(b):
                dve.wait_ge(rstd_set, 4 + LN_ORDER.index(b))
                affine(xres[:, b, :], b, ln_g, ln_b, x1_set)
                dve.wait_ge(x1_set, b + 1)
                variance(4 + b, xres[:, b, :])

            def norm2(b):
                k = 4 + b
                dve.wait_ge(rstd_set, 4 + LN_ORDER.index(k))
                dve.tensor_scalar(xn2[:, b, :], xres[:, b, :], mv[:, k, 0:1], rstd[:, k:k + 1], ALU.subtract,
                                  ALU.mult).then_inc(xn2_set, 1)

            dve.wait_ge(y_added, DC)
            dve.wait_ge(ln_in, 32)
            norm1(0)
            norm1(1)
            norm1_out(0)
            norm1(2)
            norm1_out(1)
            norm2(0)
            norm1(3)
            norm1_out(2)
            norm2(1)
            norm1_out(3)
            norm2(2)
            norm2(3)
            for c in range(DC):
                dve.wait_ge(h2_hi, c + 1)
                lo(h2l[:, c, :], aff2[c % 2][:, :], h2h[:, c, :]).then_inc(h2_split, 1)

            for k in range(4):
                dve.wait_ge(key_hi, k + 1)
                lo(keyl[:, 4 * k:4 * k + 4, :], pb[4 + k][:, :].rearrange("p (n k) -> p n k", n=4),
                   keyh[:, 4 * k:4 * k + 4, :]).then_inc(key_lo, 1)

            def q_split(b, s):
                dve.wait_ge(w_hi, b + 1)
                lo(w2l[s][:, :, :], w2raw[s][:, :, :], w2h[s][:, :, :]).then_inc(w_lo, 1)

            def q_block(n, s):
                dve.wait_ge(pq_hi, n + 1)
                lo(pq[1][s][:, :], pb[s][:, :], pq[0][s][:, :]).then_inc(w_out_, 1)

            q_split(NO, 1)
            q_split(NO + 1, 0)
            q_block(0, 1)
            mod_reduce(48, 3, 0)
            with dve.Fori(0, DC // 2 - 1) as i:
                q_split(2 * i + NO + 2, 1)
                q_block(2 * i + 1, 0)
                mod_reduce(2 * i + 49, 4, 1)
                q_split(2 * i + NO + 3, 0)
                q_block(2 * i + 2, 1)
                mod_reduce(2 * i + 50, 3, 0)
            q_block(15, 0)
            mod_reduce(63, 4, 1)
            mod_finish(3 * DC, DC, 6)

            G2 = 2 * PH

            def top16(vals, spare, best_v, best_i, n, tk):
                dve.memset(wait_pad[:, :], 0.0)
                for g in range(n):
                    ins = dve.max(best_v[:, g, 0:8], vals[:, g, :])
                tk.link(ins)
                dve.memset(wait_pad[:, :], 0.0)
                for g in range(n):
                    dve.max_index(best_i[:, g, 0:8], best_v[:, g, 0:8], vals[:, g, :])
                    ins = dve.match_replace(spare[:, g, :], best_v[:, g, 0:8], vals[:, g, :], -3.0e38)
                tk.link(ins)
                dve.memset(wait_pad[:, :], 0.0)
                for g in range(n):
                    ins = dve.max(best_v[:, g, 8:16], spare[:, g, :])
                tk.link(ins)
                dve.memset(wait_pad[:, :], 0.0)
                for g in range(n):
                    ins = dve.max_index(best_i[:, g, 8:16], best_v[:, g, 8:16], spare[:, g, :])
                tk.link(ins)
                dve.memset(wait_pad[:, :], 0.0)

            dve.wait_ge(sc_set, G2)
            dve.wait_ge(iota_in, 16)
            LINKS = 21
            with dve.Fori(0, TB) as b:
                tk = Tally(dve, tk_chain)
                tk.at = b * LINKS
                tk.link(dve.tensor_copy(sc1[:, :, :], score[:, bass.ds(b, 1), :, :].rearrange("p a g k -> p (a g) k")))
                top16(sc1, sc2, top, topi, G2, tk)
                dve.tensor_copy(topf[:, :, :], topi[:, :, :])
                tv = top[:, :, :].rearrange("p (h w) k -> p w h k", w=2)
                tk.link(dve.tensor_tensor(cand[:, :, :].rearrange("p h (a b) -> p h a b", a=TOPK),
                                          tv[:, 0].unsqueeze(3).to_broadcast([P, PH, TOPK, TOPK]),
                                          tv[:, 1].unsqueeze(2).to_broadcast([P, PH, TOPK, TOPK]), ALU.add))
                top16(cand, cand2, best, besti, PH, tk)
                dve.tensor_scalar(bpos[:, 0, :, :], besti[:, :, :], 4, None, ALU.logical_shift_right)
                tk.link(dve.tensor_scalar(bpos[:, 1, :, :], besti[:, :, :], 15, None, ALU.bitwise_and))
                dve.tensor_copy(smalls[:, 0, :], best[:, :, 0])
                tk.link(dve.tensor_copy(bposf[:, :, :, :], bpos[:, :, :, :]))
                dve.tensor_tensor(best[:, :, :], best[:, :, :], smalls[:, 0, :].unsqueeze(2).to_broadcast([P, PH, TOPK]),
                                  ALU.subtract).then_inc(tk_diff, 1)
                for w in range(2):
                    tk.link(dve.tensor_tensor(
                        pick[:, :, :], bposf[:, w, :, :].rearrange("p h k -> p (h k)").unsqueeze(2).to_broadcast([P, PH * TOPK, TOPK]),
                        iota[:, 0:TOPK].unsqueeze(1).to_broadcast([P, PH * TOPK, TOPK]), ALU.is_equal))
                    pv = pick[:, :, :].rearrange("p (h k) m -> p h k m", h=PH)
                    tf = topf[:, :, :].rearrange("p (h w) k -> p w h k", w=2)
                    tk.link(dve.tensor_tensor(pv, pv, tf[:, w].unsqueeze(2).to_broadcast([P, PH, TOPK, TOPK]), ALU.mult))
                    tk.link(dve.tensor_reduce(chosen[:, w, :], pick[:, :, :], AX.X, ALU.add))
                dve.wait_ge(tk_exp, b + 1)
                tk.link(dve.tensor_reduce(smalls[:, 1, :], best[:, :, :], AX.X, ALU.add))
                tk.link(dve.reciprocal(smalls[:, 2, :], smalls[:, 1, :]))
                tk.link(dve.tensor_tensor(chosen[:, 2, :].rearrange("p (h k) -> p h k", h=PH), best[:, :, :],
                                          smalls[:, 2, :].unsqueeze(2).to_broadcast([P, PH, TOPK]), ALU.mult))
                dve.sem_inc(tk_chosen, 1)
                dve.wait_ge(ch_turned, b + 1)
                dve.tensor_copy(chT[:, :, bass.ts(b, P)], pb[7][:, 0:3 * P].rearrange("p (w t) -> p w t", w=3)).then_inc(ch_set, 1)
            assert tk.n == LINKS, tk.n
            dve.wait_ge(chw_hi, 1)
            lo(chwl[:, :], chT[:, 2, :], chwh[:, :]).then_inc(chw_set, 1)
            dve.wait_ge(chw_set, 1)

            def one_hots(g, s):
                if not isinstance(g, int) or g >= 2:
                    dve.wait_ge(r_done, g - 1)
                for t in range(4):
                    tok = bass.ds(4 * g + t, 1)
                    dve.tensor_scalar(oneI[s][:, t, :], iota[:, :], chT[:, 0, tok], None, ALU.is_equal)
                    dve.tensor_scalar(oneJh[s][:, t, :], iota[:, :], chT[:, 1, tok], chwh[:, tok].bitcast(fp32),
                                      ALU.is_equal, ALU.mult)
                    ins = dve.tensor_scalar(oneJl[s][:, t, :], iota[:, :], chT[:, 1, tok], chwl[:, tok].bitcast(fp32),
                                            ALU.is_equal, ALU.mult)
                ins.then_inc(one_set, 1)

            one_hots(0, 0)
            one_hots(1, 1)
            with dve.Fori(1, T // 8) as i:
                one_hots(2 * i, 0)
                one_hots(2 * i + 1, 1)

            def expert_u(i, k):
                dve.wait_ge(u_hi, 2 * i + k + 1)
                lo(uTl[:, 8 * k:8 * k + 8, :], pp[k][:, :].rearrange("p (c j) -> p c j", c=8),
                   uTh[:, 8 * k:8 * k + 8, :]).then_inc(u_lo, 1)

            def expert_coef(i, u):
                dve.wait_ge(gelu_set, i + 1)
                dve.wait_ge(wt_in[u], 8 * (i - u) + 16)
                dve.tensor_tensor(act_g[0][:, :], act_g[0][:, :], wt[u][:, :], ALU.mult).then_inc(co_set, 1)

            def expert_coef_lo(i, slot, s=0):
                dve.wait_ge(co_hi, i + 1)
                lo(col[slot][:, :], act_g[s][:, :], coh[slot][:, :]).then_inc(co_lo, 1)

            def early_part(g, par, k):
                u, k = k // 4, k % 4
                i = 2 * g + u
                if k == 0:
                    if isinstance(g, int) and g == 0:
                        dve.wait_ge(gelu_set, PRE - 1 + u)
                    else:
                        dve.wait_ge(g_in[u], 16 * g)
                    dve.wait_ge(wt_in[u], 16 * g + 16)
                    dve.tensor_tensor(act_g[u][:, :], act_g[u][:, :], wt[u][:, :], ALU.mult).then_inc(co_set, 1)
                elif k == 3:
                    expert_coef_lo(i, 2 * par + u, u)
                else:
                    dve.wait_ge(v_hi, i + 1)
                    c = slice(1024 * (k - 1), 1024 * k)
                    ins = lo(vs[par][1][:, u, c], vraw[u][:, c], vs[par][0][:, u, c])
                    if k == 2:
                        ins.then_inc(v_lo, 1)

            def expert_v(i, u):
                dve.wait_ge(v_hi, i + 1)
                lo(v2l[:, u, :], vraw[u][:, :], v2h[:, u, :]).then_inc(v_lo, 1)

            def add_tiles(g, par, n0, n1):
                for n in range(n0, n1):
                    dve.wait_ge(e_done, 16 * g + n + 1)
                    t = acc[:, n // 4, 512 * (n % 4):512 * (n % 4) + 512]
                    dve.tensor_tensor(t, t, pb[5 + (n + par) % 3][:, :], ALU.add).then_inc(e_added, 1)

            def gate_diag(k):
                if k >= 1:
                    dve.wait_ge(g2_done, k)
                dve.tensor_tensor(diag2[:, :, :], ident[:, :].unsqueeze(1).to_broadcast([P, 4, P]),
                                  modT[:, M_G2 + 4 * k:M_G2 + 4 * k + 4, 0:1].to_broadcast([P, 4, P]),
                                  ALU.mult).then_inc(g2_diag, 1)

            def expert_group(g, par, last=False):
                expert_v(2 * g - 2, 0)
                expert_v(2 * g - 1, 1)
                for u in range(2):
                    n = 8 * u
                    expert_coef(2 * g + u, u)
                    if last and u == 1:
                        for k in range(4):
                            gate_diag(k)
                            add_tiles(g - 1, 1 - par, n + 2 * k, n + 2 * k + 2)
                        expert_coef_lo(2 * g + u, 2 * par + u)
                        return
                    add_tiles(g - 1, 1 - par, n, n + 2)
                    expert_u(2 * g + u + 1, 0)
                    add_tiles(g - 1, 1 - par, n + 2, n + 3)
                    expert_u(2 * g + u + 1, 1)
                    add_tiles(g - 1, 1 - par, n + 3, n + 5)
                    expert_coef_lo(2 * g + u, 2 * par + u)
                    add_tiles(g - 1, 1 - par, n + 5, n + 8)

            def early_group(g, par):
                for n in range(8):
                    early_part(g + 1, 1 - par, n)
                    add_tiles(g, par, 2 * n, 2 * n + 2)

            dve.wait_ge(r_stored[0], 64 * (T // RT // 2) + 16)
            dve.wait_ge(one_set, P)
            dve.memset(acc[:, :, :], 0.0)
            for n in (1, 2, 5, 6, 0, 3, 4, 7):
                if n == 3:
                    dve.wait_ge(u_lo, 2 * PRE)
                early_part(0, 0, n)
            with dve.Fori(0, PRE // 4 - 1) as i:
                early_group(2 * i, 0)
                early_group(2 * i + 1, 1)
            early_group(PRE // 2 - 2, 0)
            last = PRE // 2 - 1
            add_tiles(last, 1, 0, 7)
            expert_u(PRE, 0)
            add_tiles(last, 1, 7, 8)
            expert_u(PRE, 1)
            add_tiles(last, 1, 8, 10)
            for u in range(2):
                n = 10 + 3 * u
                expert_coef(PRE + u, u)
                add_tiles(last, 1, n, n + 1)
                expert_u(PRE + u + 1, 0)
                add_tiles(last, 1, n + 1, n + 2)
                expert_u(PRE + u + 1, 1)
                add_tiles(last, 1, n + 2, n + 3)
                expert_coef_lo(PRE + u, u)
            expert_group(PRE // 2 + 1, 1)
            with dve.Fori(PRE // 4 + 1, NK // 4 - 1) as i:
                expert_group(2 * i, 0)
                expert_group(2 * i + 1, 1)
            expert_group(NK // 2 - 2, 0)
            expert_group(NK // 2 - 1, 1, last=True)
            expert_v(NK - 2, 0)
            expert_v(NK - 1, 1)
            dve.wait_ge(fin_in, 48)

            def last_add(b):
                add_tiles(NK // 2 - 1, 1, 4 * b, 4 * b + 4)

            def last_sum(b):
                t = acc[:, b, :]
                dve.wait_ge(g2_prod, b + 1)
                ch.link(dve.scalar_tensor_tensor(out=t, in0=xfin[:, b, :], scalar=ALPHA, in1=t, op0=ALU.mult,
                                                 op1=ALU.add))
                variance(b, t)

            def last_norm(b):
                dve.wait_ge(rstd_set, 12 + b)
                affine(acc[:, b, :], b, ln2_g, ln2_b, fin_set)

            last_add(0)
            last_add(1)
            last_sum(0)
            last_add(2)
            last_sum(1)
            last_norm(0)
            last_add(3)
            last_sum(2)
            last_norm(1)
            last_sum(3)
            last_norm(2)
            last_norm(3)

        @block.tensor
        def _(pe):
            pe.wait_ge(vec_in, 176)
            pe.transpose(pb[4][:, 0:V_ROWS], vrows[0:V_ROWS, :], ident[0:V_ROWS, 0:V_ROWS])
            pe.transpose(pb[5][:, 0:96], mrows[0:96, :], ident[0:96, 0:96]).then_inc(vec_turned, 1)
            pe.wait_ge(silu_set, 1)

            def mod_group(g, s, i):
                pe.wait_ge(wm_in[s], 16 * i + 16)
                if not isinstance(g, int) or g >= 2:
                    pe.wait_ge(mod_set, g - 1)
                for c in range(DC):
                    mm = pe.matmul(pb[s][0:2, 0:256], silu[:, c, :], wm[s][:, c, :], start=c == 0, stop=c == DC - 1)
                mm.then_inc(wm_used, 1)

            mod_group(0, 0, 0)
            mod_group(1, 1, 0)
            with pe.Fori(1, MG1 // 2) as i:
                mod_group(2 * i, 0, i)
                mod_group(2 * i + 1, 1, i)
            pe.wait_ge(mod_set, MG1)
            for n in range(MU):
                mm = pe.transpose(pb[6][:, 2 * n:2 * n + 2], modrow[:, P * n:P * n + P], ident[0:2, 0:2])
            mm.then_inc(vec_turned, 1)
            pe.wait_ge(one_plus, 1)
            pe.wait_ge(xn_set, 1)
            for c in range(DC):
                s = c % 2
                if c >= 2:
                    pe.wait_ge(act_chain, c - 1)
                for b in range(TB):
                    pe.transpose(pb[s][:, P * b:P * b + P], xtok[:, b, P * c:P * c + P], ident[:, :])
                for b in range(CB):
                    mm = pe.transpose(pb[2 + s][:, P * b:P * b + P], ctok[:, b, P * c:P * c + P], ident[:, :])
                mm.then_inc(h_turned, 1)

            def px_block(b, s, context=False):
                pe.wait_ge(w_lo, b + 1)
                if not isinstance(b, int) or b >= 2:
                    pe.wait_ge(w_out_, b - 1)
                for c in range(DC):
                    mm = mm3(pe, pb[s][:, :], wh[s][:, c, :], wl[s][:, c, :], hxh[:, c, :], hxl[:, c, :],
                             c == 0, c == DC - 1)
                if context:
                    for c in range(DC):
                        mm = mm3(pe, pb[2 + s][:, 0:TC], wh[s][:, c, :], wl[s][:, c, :], hch[:, c, :],
                                 hcl[:, c, :], c == 0, c == DC - 1)
                mm.then_inc(w_used, 1)

            def sum_squares(k):
                w, q = k // LC, k % LC
                pe.wait_ge(sq_set, k + 1)
                for b in range(TB if w else KB):
                    mm = pe.matmul(pb[4 + w][:, 2 * b:2 * b + 2], sq[k % 2][:, P * b:P * b + P], ones[:, 0:2],
                                   start=q == 0 and b == 0, stop=q == LC - 1, skip_group_check=True)
                mm.then_inc(sq_used, 1)
                if q == LC - 1:
                    pe.wait_ge(sq_used, k + 1)
                    pe.sem_inc(ssq_done, 1)

            pe.wait_ge(act_chain, DC)
            pe.wait_ge(h_split, DC)
            pe.wait_ge(fill_set, 1)
            for b in range(11):
                px_block(b, b % 2, b < 5)
                if 1 <= b <= 4:
                    sum_squares(b - 1)
                if b == 5:
                    pe.wait_ge(swap_set, 1)
                    pe.wait_ge(kr_ready, 1)
                    pe.matmul(pb[7][:, :], swap[:, :], krh[:, 0:T], start=True, stop=False)
                    pe.matmul(pb[7][:, :], swap[:, :], krl[:, 0:T], start=False, stop=True).then_inc(kr_swapped, 1)
                if b == 6:
                    pe.wait_ge(dg_set, 1)
                    pe.wait_ge(kr_roped, 1)
                    pe.matmul(pb[6][:, :], ones[:, :], diag[:, 0:T], start=True, stop=True)
                    pe.matmul(pb[7][:, 0:TC], ones[:, :], diag[:, T:NKEY], start=True, stop=True).then_inc(bc_done, 1)
                if 6 <= b <= 9:
                    sum_squares(b - 2)
                if b == 10:
                    pe.wait_ge(dg_set, 2)
                    pe.wait_ge(lora_scaled, LC)
                    pe.matmul(pb[6][:, :], ones[:, :], diag[:, 0:T], start=True, stop=True).then_inc(bc_done, 1)
            with pe.Fori(0, 3) as i:
                px_block(2 * i + 11, 1)
                px_block(2 * i + 12, 0)

            def mod_sum(j, r, bank, at):
                pe.wait_ge(mu_red, j + 1)
                pe.matmul(pb[bank][:, bass.ds(at, 2)], mred[r][:, :], ones[:, 0:2], start=True, stop=True).then_inc(mu_sum, 1)

            with pe.Fori(0, 16) as i:
                px_block(2 * i + 17, 1)
                mod_sum(2 * i, 0, 4, 4 * i)
                px_block(2 * i + 18, 0)
                mod_sum(2 * i + 1, 1, 4, 4 * i + 2)

            def tile(p, n, width, parts, out_):
                if n >= 2:
                    pe.wait_ge(pj_lo, 10 * p + n - 1)
                for c in range(LC):
                    mm = mm3(pe, out_, *parts(c), c == 0, c == LC - 1)
                return mm

            def rope_part(p):
                pe.wait_ge(pw_lo, 2 * p + 1)
                tile(p, 0, T, lambda c: (pqh[:, c, 2 * NOPE:], pql[:, c, 2 * NOPE:], cqh[:, c, :], cql[:, c, :]),
                     pb[4][:, :]).then_inc(pj_done, 1)

            def query_part(p, h):
                cols = slice(NOPE * h, NOPE * h + NOPE)
                tile(p, 1 + h, T, lambda c: (pqh[:, c, cols], pql[:, c, cols], cqh[:, c, :], cql[:, c, :]),
                     pb[h][:, :]).then_inc(pj_done, 1)

            def swap_part(p):
                pe.wait_ge(pj_lo, 10 * p + 2)
                pe.matmul(pb[0][:, :], swap[:, :], qrh[:, :], start=True, stop=False)
                pe.matmul(pb[0][:, :], swap[:, :], qrl[:, :], start=False, stop=True).then_inc(pj_done, 1)

            def attention_pair(p, last=False):
                B = (pb[4], pb[5])
                pe.wait_ge(pw_lo, 2 * p + 2)
                for h in range(2):
                    if h == 1 and (not isinstance(p, int) or p > 0):
                        pe.wait_ge(o_set, 2 * p)
                    cols = slice(256 * h, 256 * h + NOPE)
                    tile(p, 4 + h, T, lambda c: (pkh[:, c, cols], pkl[:, c, cols], ckvh[:, c, 0:T], ckvl[:, c, 0:T]),
                         B[h][:, :]).then_inc(pj_done, 1)
                for h in range(2):
                    cols = slice(256 * h, 256 * h + NOPE)
                    mm = tile(p, 6, TC, lambda c: (pkh[:, c, cols], pkl[:, c, cols], ckvh[:, c, T:NKEY], ckvl[:, c, T:NKEY]),
                              B[0][:, TC * h:TC * h + TC])
                mm.then_inc(pj_done, 1)

                def value_rows(kb):
                    v, k = kb // 2, kb % 2
                    ks = slice(P * kb, P * kb + P)
                    vv = lambda t, c: t[:, c, :].rearrange("p (h n) -> p h n", h=2)[:, :, NOPE:NOPE + VD]
                    if k == 0:
                        pe.wait_ge(pj_lo, 10 * p + 6 + v)
                    for c in range(LC):
                        o = B[(7 + v) % 2][:, 256 * k:256 * k + 256]
                        pe.matmul(o, ckvh[:, c, ks], vv(pkh, c), start=c == 0, stop=False)
                        pe.matmul(o, ckvh[:, c, ks], vv(pkl, c), start=False, stop=False)
                        mm = pe.matmul(o, ckvl[:, c, ks], vv(pkh, c), start=False, stop=c == LC - 1)
                    if k == 1:
                        mm.then_inc(pj_done, 1)

                def scores(n):
                    h, b = n // 4, n % 4
                    if n >= 2 or not isinstance(p, int) or p > 0:
                        pe.wait_ge(exp_done, 8 * p + n - 1)
                    t = slice(P * b, P * b + P)
                    r = slice(ROPE * h, ROPE * h + ROPE)
                    for k0, k1 in ((0, T), (T, NKEY)):
                        o = pp[n % 2][:, k0:k1]
                        mm3(pe, o, qh[:, h, t], ql[:, h, t], kTh[:, h, k0:k1], kTl[:, h, k0:k1], True, False)
                        mm = mm3(pe, o, qrh[r, t], qrl[r, t], krh[r, k0:k1], krl[r, k0:k1], False, True)
                    mm.then_inc(s_done, 1)

                def turn(n):
                    pe.wait_ge(prob_set, 8 * p + n + 1)
                    if n >= 1 or not isinstance(p, int) or p > 0:
                        pe.wait_ge(pT_lo, 8 * p + n)
                    for k in range(KB):
                        mm = pe.transpose(pp[3][:, P * k:P * k + P], prob[n % 2][:, P * k:P * k + P], ident[:, :])
                    mm.then_inc(p_turned, 1)

                def values(h):
                    pe.wait_ge(pT_lo, 8 * p + 4 * h + 4)
                    pe.wait_ge(pj_lo, 10 * p + 10)
                    for k in range(KB):
                        mm = mm3(pe, pb[4 + h][:, :], vh[:, k, h, :], vl[:, k, h, :], pTh[:, k, :], pTl[:, k, :],
                                 k == 0, k == KB - 1)
                    mm.then_inc(pv_done, 1)

                pe.wait_ge(pj_lo, 10 * p + 7)
                for n in range(6):
                    scores(n)
                    if n >= 2:
                        turn(n - 2)
                    value_rows(n)
                scores(6)
                values(0)
                turn(4)
                scores(7)
                turn(5)
                if not last:
                    pe.wait_ge(o_set, 2 * p + 1)
                    rope_part(p + 1)
                turn(6)
                if not last:
                    pe.wait_ge(exp_done, 8 * p + 7)
                    query_part(p + 1, 0)
                turn(7)
                if not last:
                    query_part(p + 1, 1)
                    swap_part(p + 1)
                values(1)

            rope_part(0)
            pe.wait_ge(w_out_, NPX)
            query_part(0, 0)
            query_part(0, 1)
            swap_part(0)
            attention_pair(0)
            with pe.Fori(1, HEADS // 2 - 1) as p:
                attention_pair(p)
            attention_pair(HEADS // 2 - 1, True)

            pe.wait_ge(dft_split, 1)
            pe.wait_ge(o_set, HEADS)
            pe.wait_ge(exp_done, 8 * (HEADS // 2))
            pe.wait_ge(pT_lo, 8 * (HEADS // 2))

            def fourier_group(g):
                pe.wait_ge(f_in, 16 * g + 16)
                for cb in range(2):
                    if not isinstance(g, int) or g > 0:
                        pe.wait_ge(f_lo, 2 * g - 1 + cb)
                    for b in range(TB):
                        mm = pe.transpose(pb[cb][:, P * b:P * b + P], fT[:, cb, P * b:P * b + P], ident[:, :])
                    mm.then_inc(f_turned, 1)
                for n in range(4):
                    w, cb = n % 2, n // 2
                    if w == 0:
                        pe.wait_ge(f_lo, 2 * g + cb + 1)
                    if not isinstance(g, int) or g > 0:
                        pe.wait_ge(g_lo, 4 * g - 3 + n)
                    for b in range(TB):
                        cs = slice(P * cb, P * cb + P)
                        mm = mm3(pe, pb[2 + n][:, :], fh[:, b, cs], fl[:, b, cs], dth[:, w, b, :], dtl[:, w, b, :],
                                 b == 0, b == TB - 1)
                    mm.then_inc(g_done, 1)
                pe.wait_ge(g_lo, 4 * g + 4)
                for k in range(2):
                    if not isinstance(g, int) or g > 0:
                        pe.wait_ge(y_lo, 2 * g - 1 + k)
                    for n in range(4):
                        w, cb = n % 2, n // 2
                        cs = slice(P * k, P * k + P)
                        mm = mm3(pe, pb[6 + k][:, :], dch[:, w, cb, cs], dcl[:, w, cb, cs], gh[:, w, cb, :],
                                 gl[:, w, cb, :], n == 0, n == 3)
                    mm.then_inc(y_done, 1)

            fourier_group(0)
            with pe.Fori(1, FG) as g:
                fourier_group(g)

            NM, NO = NPX + 2 * DC, NPX + 3 * DC
            pe.wait_ge(y_lo, FD // P)
            pe.wait_ge(f_lo, 2 * FG)

            def merge(m, s, at, first=False):
                pe.wait_ge(w_lo, 2 * m + NPX + 1)
                pe.wait_ge(w_out_, 2 * m + NPX - 1)
                for c in range(DC):
                    if first and c % 4 == 0:
                        pe.wait_ge(o_lo, c // 4 + 1)
                    mm = mm3(pe, pb[1][:, :], wh[1][:, c, :], wl[1][:, c, :], oh[:, c, :], ol[:, c, :], c == 0, c == DC - 1)
                mm.then_inc(w_used, 1)
                mod_sum(m + 32, s, 6, at)
                pe.wait_ge(w_lo, 2 * m + NPX + 2)
                pe.wait_ge(w_out_, 2 * m + NPX)
                for c in range(FD // P):
                    mm = mm3(pe, pb[0][:, :], wh[0][:, c, :], wl[0][:, c, :], yh[:, c, :], yl[:, c, :], c == 0,
                             c == FD // P - 1)
                mm.then_inc(w_used, 1)

            merge(0, 0, 0, True)
            merge(1, 1, 2)
            with pe.Fori(1, DC // 2) as i:
                for u in range(2):
                    merge(2 * i + u, u, 4 * i + 2 * u)

            def out_block(n, s, first=False):
                pe.wait_ge(w_lo, n + NM + 1)
                pe.wait_ge(w_out_, n + NM - 1)
                for c in range(DC):
                    if first:
                        pe.wait_ge(m_lo, c + 1)
                    mm = mm3(pe, pb[s][:, :], wh[s][:, c, :], wl[s][:, c, :], mh[:, c, :], ml[:, c, :], c == 0, c == DC - 1)
                mm.then_inc(w_used, 1)

            def out_turn(n, y):
                pe.wait_ge(w_out_, n + NM + 1)
                if not isinstance(n, int) or n >= 2:
                    pe.wait_ge(y_added, n - 1)
                for b in range(TB):
                    mm = pe.transpose(pb[2 + y][:, P * b:P * b + P], ybuf[y][:, P * b:P * b + P], ident[:, :])
                mm.then_inc(y_turned, 1)

            out_block(0, 1, True)
            out_block(1, 0)
            out_turn(0, 0)
            out_block(2, 1)
            out_turn(1, 1)
            with pe.Fori(1, DC // 2 - 1) as i:
                out_block(2 * i + 1, 0)
                out_turn(2 * i, 0)
                out_block(2 * i + 2, 1)
                out_turn(2 * i + 1, 1)
            out_block(DC - 1, 0)
            out_turn(DC - 2, 0)
            out_turn(DC - 1, 1)

            pe.wait_ge(xn2_set, TB)
            for c in range(DC):
                if c >= 2:
                    pe.wait_ge(h2_affine, c - 1)
                for b in range(TB):
                    mm = pe.transpose(pb[c % 2][:, P * b:P * b + P], xn2[:, b, P * c:P * c + P], ident[:, :])
                mm.then_inc(h2_turned, 1)

            pe.wait_ge(keys_in, 16)
            for k in range(4):
                for n in range(4):
                    mm = pe.transpose(pb[4 + k][:, P * n:P * n + P], keys[:, 4 * k + n, :], ident[:, :])
                mm.then_inc(keys_turned, 1)
            pe.wait_ge(h2_affine, DC)
            pe.wait_ge(h2_split, DC)
            pe.wait_ge(key_lo, 4)

            def q_block(n, s):
                pe.wait_ge(w_lo, n + NO + 1)
                pe.wait_ge(w_out_, n + NO - 1)
                for c in range(DC):
                    mm = mm3(pe, pb[s][:, :], w2h[s][:, c, :], w2l[s][:, c, :], h2h[:, c, :], h2l[:, c, :], c == 0,
                             c == DC - 1)
                mm.then_inc(w_used, 1)

            def key_scores(n, s):
                pe.wait_ge(w_out_, n + NO + 1)
                if not isinstance(n, int) or n >= 2:
                    pe.wait_ge(sc_set, n - 1)
                kk = bass.ds(n, 1)
                for b in range(TB):
                    t = slice(P * b, P * b + P)
                    mm = mm3(pe, pb[2 + s][:, t], pq[0][s][:, t], pq[1][s][:, t],
                             keyh[:, kk, :].rearrange("p a k -> p (a k)"), keyl[:, kk, :].rearrange("p a k -> p (a k)"),
                             True, True)
                mm.then_inc(sc_done, 1)

            q_block(0, 1)
            q_block(1, 0)
            key_scores(0, 1)
            mod_sum(48, 0, 6, 0)
            q_block(2, 1)
            key_scores(1, 0)
            mod_sum(49, 1, 6, 2)
            with pe.Fori(1, DC // 2 - 1) as i:
                q_block(2 * i + 1, 0)
                key_scores(2 * i, 1)
                mod_sum(2 * i + 48, 0, 6, 4 * i)
                q_block(2 * i + 2, 1)
                key_scores(2 * i + 1, 0)
                mod_sum(2 * i + 49, 1, 6, 4 * i + 2)
            q_block(DC - 1, 0)
            key_scores(DC - 2, 1)
            mod_sum(62, 0, 6, 28)
            key_scores(DC - 1, 0)
            mod_sum(63, 1, 6, 30)

            def pre_turn(i, s, q):
                if q == 0:
                    pe.wait_ge(u_in[s], 8 * (i - s) + 16)
                if q % 2 == 0 and (not isinstance(i, int) or i >= 1):
                    pe.wait_ge(pre_raw, 2 * i - 1 + q // 2)
                for c in range(4 * q, 4 * q + 4):
                    mm = pe.transpose(pb[q][:, P * (c % 4):P * (c % 4) + P], pu[s][:, P * c:P * c + P], ident[:, :])
                if q % 2 == 1:
                    mm.then_inc(u_turned, 1)

            def pre_up(i, s, q):
                if q == 0 and (not isinstance(i, int) or i >= 2):
                    pe.wait_ge(gelu_set, i - 1)
                if q % 2 == 0:
                    pe.wait_ge(u_lo, 2 * i + 1 + q // 2)
                for c in range(4 * q, 4 * q + 4):
                    mm = mm3(pe, pb[4 + s][:, :], pTuh[:, c, :], pTul[:, c, :], h2h[:, c, :], h2l[:, c, :], c == 0,
                             c == DC - 1)
                if q % 2 == 1:
                    mm.then_inc((u_half, a_done)[q // 2], 1)

            def pre_quarter(i, s, q, last=False):
                if not last:
                    pre_turn(i + 1, 1 - s, q)
                pre_up(i, s, q)

            pe.wait_ge(w_out_, NO + DC)
            pe.wait_ge(sc_set, 2 * PH)
            for q in range(4):
                pre_turn(0, 0, q)

            def top_part(b):
                for k in range(PRE_TK):
                    for q in range(4):
                        pre_quarter(PRE_TK * b + k, k % 2, q)
                pe.wait_ge(tk_chosen, b + 1)
                for w in range(3):
                    mm = pe.transpose(pb[7][:, P * w:P * w + P], chosen[:, w, :], ident[:, :])
                mm.then_inc(ch_turned, 1)

            top_part(0)
            with pe.Fori(1, TB) as b:
                top_part(b)

            def routing(g, s):
                pe.wait_ge(one_set, g + 1)
                if not isinstance(g, int) or g >= 2:
                    pe.wait_ge(r_set, g - 1)
                for t in range(4):
                    o = pb[6 + s][:, P * t:P * t + P]
                    pe.matmul(o, oneJh[s][:, t, :], oneI[s][:, t, :], start=True, stop=False)
                    mm = pe.matmul(o, oneJl[s][:, t, :], oneI[s][:, t, :], start=False, stop=True)
                mm.then_inc(r_done, 1)

            def route_part(r):
                for k in range(2):
                    for q in range(RI):
                        pre_quarter(2 * r + PRE_TK * TB + k, k, q)
                        routing(8 * r + 4 * k + q, q % 2)

            pe.wait_ge(ch_set, TB)
            route_part(0)
            with pe.Fori(1, T // (8 * RI)) as r:
                route_part(r)
            for i in range(PRE - PRE_END, PRE):
                for q in range(4):
                    pre_quarter(i, i % 2, q, i == PRE - 1)

            def turn_u(i, s):
                pe.wait_ge(u_in[s], 8 * (i - s) + 16)
                pe.wait_ge(u_lo, 2 * i)
                for c in range(DC):
                    mm = pe.transpose(pb[c // 4][:, P * (c % 4):P * (c % 4) + P], uraw[s][:, P * c:P * c + P], ident[:, :])
                mm.then_inc(u_turned, 1)

            def up(i):
                pe.wait_ge(u_lo, 2 * i + 2)
                pe.wait_ge(gelu_set, i)
                for c in range(DC):
                    mm = mm3(pe, pb[4][:, :], uTh[:, c, :], uTl[:, c, :], h2h[:, c, :], h2l[:, c, :], c == 0,
                             c == DC - 1)
                mm.then_inc(a_done, 1)

            def down(g, par, n0, n1, v=(v2h, v2l)):
                for n in range(n0, n1):
                    if n == 0:
                        pe.wait_ge(co_lo, 2 * g + 2)
                        pe.wait_ge(v_lo, 2 * g + 2)
                    if n >= 3 or (par == 1 and (not isinstance(g, int) or g > 0)):
                        pe.wait_ge(e_added, 16 * g + n - 2)
                    elif n < 2 and (not isinstance(g, int) or g > 0):
                        pe.wait_ge(e_added, 16 * g + n - 1)
                    t, d = slice(P * (n // 4), P * (n // 4) + P), slice(512 * (n % 4), 512 * (n % 4) + 512)
                    for u in range(2):
                        mm = mm3(pe, pb[5 + (n + par) % 3][:, :], coh[2 * par + u][:, t], col[2 * par + u][:, t],
                                 v[0][:, u, d], v[1][:, u, d], u == 0, u == 1)
                    mm.then_inc(e_done, 1)

            def expert_group(g, par, last=False):
                for u in range(2):
                    up(2 * g + u)
                    if last and u == 1:
                        for k in range(4):
                            down(g - 1, 1 - par, 8 + 2 * k, 10 + 2 * k)
                            pe.wait_ge(g2_diag, k + 1)
                            pe.matmul(pb[k][:, :], ones[:, :], diag2[:, :, :].rearrange("p a t -> p (a t)"), start=True,
                                      stop=True).then_inc(g2_done, 1)
                        return
                    turn_u(2 * g + u + 1, 1 - u)
                    down(g - 1, 1 - par, 8 * u, 8 * u + 8)

            pe.wait_ge(r_set, P)
            pe.wait_ge(gelu_set, PRE)
            down(0, 0, 0, 16, vs[0])
            down(1, 1, 0, 16, vs[1])
            with pe.Fori(1, PRE // 4 - 1) as i:
                down(2 * i, 0, 0, 16, vs[0])
                down(2 * i + 1, 1, 0, 16, vs[1])
            down(PRE // 2 - 2, 0, 0, 16, vs[0])
            last = PRE // 2 - 1
            down(last, 1, 0, 6)
            turn_u(PRE, 0)
            down(last, 1, 6, 10)
            for u in range(2):
                up(PRE + u)
                turn_u(PRE + u + 1, 1 - u)
                down(last, 1, 10 + 3 * u, 13 + 3 * u)
            expert_group(PRE // 2 + 1, 1)
            with pe.Fori(PRE // 4 + 1, NK // 4 - 1) as i:
                expert_group(2 * i, 0)
                expert_group(2 * i + 1, 1)
            expert_group(NK // 2 - 2, 0)
            expert_group(NK // 2 - 1, 1, last=True)
            down(NK // 2 - 1, 1, 0, 16)


_INS = ['x', 'c', 'ctx', 'c_ctx', 'w_mod', 'b_mod', 'w_in', 'b_in', 'q_norm_g', 'w_uq', 'kv_norm_g', 'w_ukv',
        'w_o_mla', 'w_fourier', 'w_out', 'ln1_g', 'ln1_b', 'peer_wq', 'peer_keys', 'peer_u', 'peer_v',
        'ln2_g', 'ln2_b']


def kernel(**inputs):
    import numpy as _np
    import concourse.bacc as _bacc
    from concourse import mybir as _mybir
    from concourse.bass_utils import run_bass_kernel_spmd as _run

    nc = _bacc.Bacc("TRN2", target_bir_lowering=False, num_devices=1)
    arrays, aps = {}, {}
    tables = constants()
    for name in _INS + list(tables):
        x = _np.ascontiguousarray(inputs[name] if name in inputs else tables[name])
        arrays[f"in_{name}_dram"] = x
        aps[name] = nc.dram_tensor(f"in_{name}_dram", x.shape, _mybir.dt.from_np(x.dtype),
                                   kind="ExternalInput").ap()
    out = nc.dram_tensor("out_0_dram", (1, T, D), _mybir.dt.float32, kind="ExternalOutput").ap()
    layer_kernel(nc, aps, out)
    r = _run(nc, [arrays], core_ids=[0])
    return r.results[0]["out_0_dram"]
```
